# Optimizing a Trainium2 kernel written in Bass

```python
import math
import jax, jax.numpy as jnp
from jax import lax
import numpy as np

D_MODEL = 1024
BATCH = 1
SEQ = 512
DEPTH = 1
DEC_BATCH = 1
DEC_SEQ = 64
PAST_LEN = 512

CHUNK = 64
N_META = 16
HEAD_DIM = 64
A_HEADS = 4
B_HEADS = 8
A_WIDTH = A_HEADS * 2 * HEAD_DIM
B_WIDTH = B_HEADS * HEAD_DIM
MIX_WIDTH = A_WIDTH + B_WIDTH
QKV_WIDTH = 3 * MIX_WIDTH
ROT_DIM = HEAD_DIM // 4
ROPE_THETA = 500000.0
Q_BLOCK = 128
N_KEYS = 128
N_EXPERTS = N_KEYS * N_KEYS
PEER_HEADS = 8
PEER_TOPK = 16
D_KEY = 256
TOKEN_BLOCK = 256
EPS = 1e-6
NEG_BIG = -1e30

kernel_name = 'hybrid_diffattn_stickbreak_peer_stream'

def rms_norm(x, g):
    x32 = x.astype(jnp.float32)
    y = x32 * lax.rsqrt(jnp.mean(x32 * x32, axis=-1, keepdims=True) + EPS)
    return (y * g.astype(jnp.float32)).astype(x.dtype)

def partial_rope(x, pos):
    half = ROT_DIM // 2
    inv_freq = ROPE_THETA ** (-jnp.arange(half, dtype=jnp.float32) * 2.0 / ROT_DIM)
    ang = pos.astype(jnp.float32)[:, None] * inv_freq[None, :]
    cos = jnp.cos(ang)[None, :, None, :]
    sin = jnp.sin(ang)[None, :, None, :]
    x32 = x.astype(jnp.float32)
    x1 = x32[..., :half]
    x2 = x32[..., half:ROT_DIM]
    out = jnp.concatenate([x1 * cos - x2 * sin, x2 * cos + x1 * sin, x32[..., ROT_DIM:]], axis=-1)
    return out.astype(x.dtype)

def chunk_index(pos):
    return jnp.where(pos < N_META, 0, (pos - N_META) // CHUNK + 1)

def project_mixers(hn, w_qkv, pos):
    b, t, _ = hn.shape
    qkv = hn @ w_qkv
    aq, ak, av, bq, bk, bv = jnp.split(
        qkv, [A_WIDTH, 2 * A_WIDTH, 3 * A_WIDTH, 3 * A_WIDTH + B_WIDTH, 3 * A_WIDTH + 2 * B_WIDTH], axis=-1)
    aq = partial_rope(aq.reshape(b, t, 2 * A_HEADS, HEAD_DIM), pos).reshape(b, t, A_HEADS, 2, HEAD_DIM)
    ak = partial_rope(ak.reshape(b, t, 2 * A_HEADS, HEAD_DIM), pos).reshape(b, t, A_HEADS, 2 * HEAD_DIM)
    av = av.reshape(b, t, A_HEADS, 2 * HEAD_DIM)
    bq = bq.reshape(b, t, B_HEADS, HEAD_DIM)
    bk = bk.reshape(b, t, B_HEADS, HEAD_DIM)
    bv = bv.reshape(b, t, B_HEADS, HEAD_DIM)
    return aq, ak, av, bq, bk, bv

def diff_lambda_value(lp, lam_init):
    lp = lp.astype(jnp.float32)
    return jnp.exp(jnp.sum(lp[0] * lp[1])) - jnp.exp(jnp.sum(lp[2] * lp[3])) + lam_init

def diff_attn_block(q, k, v, q_pos, k_pos, k_valid, lam):
    kk = k.reshape(k.shape[:3] + (2, HEAD_DIM))
    s = jnp.einsum('bqhmd,bkhmd->bhmqk', q, kk).astype(jnp.float32) * (HEAD_DIM ** -0.5)
    mask = (chunk_index(k_pos)[None, :] <= chunk_index(q_pos)[:, None]) & k_valid[None, :]
    p = jax.nn.softmax(jnp.where(mask, s, NEG_BIG), axis=-1)
    w = p[:, :, 0] - lam * p[:, :, 1]
    return jnp.einsum('bhqk,bkhe->bqhe', w.astype(v.dtype), v)

def stick_block(q, k, v, q_pos, k_pos, k_valid):
    z = jnp.einsum('bqhd,bkhd->bhqk', q, k).astype(jnp.float32) * (HEAD_DIM ** -0.5)
    mask = (k_pos[None, :] < q_pos[:, None]) & k_valid[None, :]
    log_1m = jnp.where(mask, jax.nn.log_sigmoid(-z), 0.0)
    after = lax.cumsum(log_1m, axis=3, reverse=True) - log_1m
    a = jnp.where(mask, jnp.exp(jax.nn.log_sigmoid(z) + after), 0.0)
    return jnp.einsum('bhqk,bkhd->bqhd', a.astype(v.dtype), v)

def sweep_query_blocks(block_fn, q, q_pos):
    b, t = q.shape[:2]
    nb = t // Q_BLOCK
    qb = jnp.moveaxis(q.reshape((b, nb, Q_BLOCK) + q.shape[2:]), 1, 0)
    out = lax.map(lambda args: block_fn(args[0], args[1]), (qb, q_pos.reshape(nb, Q_BLOCK)))
    return jnp.moveaxis(out, 0, 1).reshape((b, t) + out.shape[3:])

def peer_block(xb, w_q, sub_keys, u, v):
    tb = xb.shape[0]
    q = (xb @ w_q).reshape(tb, PEER_HEADS, 2, D_KEY // 2)
    s = jnp.einsum('thpc,pnc->thpn', q, sub_keys).astype(jnp.float32)
    s_top, i_top = lax.top_k(s, PEER_TOPK)
    cand_s = (s_top[:, :, 0, :, None] + s_top[:, :, 1, None, :]).reshape(tb, PEER_HEADS, PEER_TOPK * PEER_TOPK)
    cand_i = (i_top[:, :, 0, :, None] * N_KEYS + i_top[:, :, 1, None, :]).reshape(tb, PEER_HEADS, PEER_TOPK * PEER_TOPK)
    best_s, best_j = lax.top_k(cand_s, PEER_TOPK)
    expert = jnp.take_along_axis(cand_i, best_j, axis=-1)
    gate = jax.nn.softmax(best_s, axis=-1)
    pre = jnp.einsum('thkd,td->thk', u[expert], xb).astype(jnp.float32)
    act = jax.nn.gelu(pre, approximate=False) * gate
    return jnp.einsum('thk,thkd->td', act.astype(v.dtype), v[expert])

def peer(h, w_q, sub_keys, u, v):
    b, t, d = h.shape
    n = b * t
    nb = -(-n // TOKEN_BLOCK)
    flat = jnp.pad(h.reshape(n, d), ((0, nb * TOKEN_BLOCK - n), (0, 0))).reshape(nb, TOKEN_BLOCK, d)
    out = lax.map(lambda xb: peer_block(xb, w_q, sub_keys, u, v), flat)
    return out.reshape(nb * TOKEN_BLOCK, d)[:n].reshape(b, t, d)

def finish_layer(h, a_out, b_out, a_g, b_g, w_o, g_ffn, w_pq, sub_keys, u, v, lam_init):
    b, t, _ = h.shape
    a = rms_norm(a_out, a_g) * (1.0 - lam_init)
    bo = rms_norm(b_out, b_g)
    merged = jnp.concatenate([a.reshape(b, t, A_WIDTH), bo.reshape(b, t, B_WIDTH)], axis=-1)
    h = h + merged @ w_o
    return h + peer(rms_norm(h, g_ffn), w_pq, sub_keys, u, v)

def prompt_layer(h, w_qkv, lam_p, a_g, b_g, w_o, g_attn, g_ffn, w_pq, sub_keys, u, v, lam_init):
    b, t, _ = h.shape
    t_pad = -(-t // Q_BLOCK) * Q_BLOCK
    pos = jnp.arange(t, dtype=jnp.int32)
    pos_pad = jnp.arange(t_pad, dtype=jnp.int32)
    valid = pos_pad < t
    aq, ak, av, bq, bk, bv = project_mixers(rms_norm(h, g_attn), w_qkv, pos)
    pad = lambda a: jnp.pad(a, [(0, 0), (0, t_pad - t)] + [(0, 0)] * (a.ndim - 2))
    aqp, akp, avp, bqp, bkp, bvp = [pad(a) for a in (aq, ak, av, bq, bk, bv)]
    lam = diff_lambda_value(lam_p, lam_init)
    a_out = sweep_query_blocks(lambda qb, qp: diff_attn_block(qb, akp, avp, qp, pos_pad, valid, lam), aqp, pos_pad)[:, :t]
    b_out = sweep_query_blocks(lambda qb, qp: stick_block(qb, bkp, bvp, qp, pos_pad, valid), bqp, pos_pad)[:, :t]
    h = finish_layer(h, a_out, b_out, a_g, b_g, w_o, g_ffn, w_pq, sub_keys, u, v, lam_init)
    return h, (ak, av, bk, bv)

def sample_layer(h, c_ak, c_av, c_bk, c_bv, w_qkv, lam_p, a_g, b_g, w_o, g_attn, g_ffn, w_pq, sub_keys, u, v, lam_init):
    b, s, _ = h.shape
    n_past = c_ak.shape[1]
    q_pos = n_past + jnp.arange(s, dtype=jnp.int32)
    k_pos = jnp.arange(n_past + s, dtype=jnp.int32)
    valid = jnp.ones((n_past + s,), dtype=bool)
    aq, ak, av, bq, bk, bv = project_mixers(rms_norm(h, g_attn), w_qkv, q_pos)
    lam = diff_lambda_value(lam_p, lam_init)
    a_out = diff_attn_block(aq, jnp.concatenate([c_ak, ak], axis=1), jnp.concatenate([c_av, av], axis=1),
                            q_pos, k_pos, valid, lam)
    b_out = stick_block(bq, jnp.concatenate([c_bk, bk], axis=1), jnp.concatenate([c_bv, bv], axis=1),
                        q_pos, k_pos, valid)
    h = finish_layer(h, a_out, b_out, a_g, b_g, w_o, g_ffn, w_pq, sub_keys, u, v, lam_init)
    return h, (ak, av, bk, bv)

def setup_inputs(seed: int = 0) -> dict:
    key = jax.random.key(seed)
    ks = jax.random.split(key, 19)
    nrm = lambda k, shape, scale=1.0: jax.random.normal(k, shape, jnp.float32) * scale
    t_cache = N_META + PAST_LEN
    return {
        'x_prompt': nrm(ks[0], (BATCH, SEQ, D_MODEL)),
        'x_sample': nrm(ks[1], (DEC_BATCH, DEC_SEQ, D_MODEL)),
        'cache_a_k': nrm(ks[2], (DEPTH, DEC_BATCH, t_cache, A_HEADS, 2 * HEAD_DIM)),
        'cache_a_v': nrm(ks[3], (DEPTH, DEC_BATCH, t_cache, A_HEADS, 2 * HEAD_DIM)),
        'cache_b_k': nrm(ks[4], (DEPTH, DEC_BATCH, t_cache, B_HEADS, HEAD_DIM)),
        'cache_b_v': nrm(ks[5], (DEPTH, DEC_BATCH, t_cache, B_HEADS, HEAD_DIM)),
        'meta_tokens': nrm(ks[6], (N_META, D_MODEL)),
        'g_attn': 1.0 + nrm(ks[7], (DEPTH, D_MODEL), 0.02),
        'w_qkv': nrm(ks[8], (DEPTH, D_MODEL, QKV_WIDTH), D_MODEL ** -0.5),
        'diff_lambda': nrm(ks[9], (DEPTH, 4, HEAD_DIM), 0.1),
        'a_norm_g': 1.0 + nrm(ks[10], (DEPTH, 2 * HEAD_DIM), 0.02),
        'b_norm_g': 1.0 + nrm(ks[11], (DEPTH, HEAD_DIM), 0.02),
        'w_o': nrm(ks[12], (DEPTH, MIX_WIDTH, D_MODEL), MIX_WIDTH ** -0.5),
        'g_ffn': 1.0 + nrm(ks[13], (DEPTH, D_MODEL), 0.02),
        'w_peer_q': nrm(ks[14], (DEPTH, D_MODEL, PEER_HEADS * D_KEY), D_MODEL ** -0.5),
        'peer_sub_keys': nrm(ks[15], (DEPTH, 2, N_KEYS, D_KEY // 2), (D_KEY // 2) ** -0.5),
        'peer_u': nrm(ks[16], (DEPTH, N_EXPERTS, D_MODEL), D_MODEL ** -0.5),
        'peer_v': nrm(ks[17], (DEPTH, N_EXPERTS, D_MODEL), PEER_HEADS ** -0.5),
        'g_final': 1.0 + nrm(ks[18], (D_MODEL,), 0.02),
    }

def reference(x_prompt, x_sample, cache_a_k, cache_a_v, cache_b_k, cache_b_v, meta_tokens, g_attn, w_qkv,
              diff_lambda, a_norm_g, b_norm_g, w_o, g_ffn, w_peer_q, peer_sub_keys, peer_u, peer_v, g_final):
    meta = jnp.broadcast_to(meta_tokens[None].astype(x_prompt.dtype), (x_prompt.shape[0], N_META, D_MODEL))
    hp = jnp.concatenate([meta, x_prompt], axis=1)
    hs = x_sample
    pak, pav, pbk, pbv = [], [], [], []
    sak, sav, sbk, sbv = [], [], [], []
    for l in range(DEPTH):
        lam_init = 0.8 - 0.6 * math.exp(-0.3 * l)
        lw = (w_qkv[l], diff_lambda[l], a_norm_g[l], b_norm_g[l], w_o[l], g_attn[l], g_ffn[l],
              w_peer_q[l], peer_sub_keys[l], peer_u[l], peer_v[l])
        hp, (ak, av, bk, bv) = prompt_layer(hp, *lw, lam_init)
        pak.append(ak); pav.append(av); pbk.append(bk); pbv.append(bv)
        hs, (ak, av, bk, bv) = sample_layer(hs, cache_a_k[l], cache_a_v[l], cache_b_k[l], cache_b_v[l], *lw, lam_init)
        sak.append(ak); sav.append(av); sbk.append(bk); sbv.append(bv)
    y_prompt = rms_norm(hp, g_final)[:, N_META:]
    y_sample = rms_norm(hs, g_final)
    return (y_prompt, y_sample, jnp.stack(pak), jnp.stack(pav), jnp.stack(pbk), jnp.stack(pbv),
            jnp.stack(sak), jnp.stack(sav), jnp.stack(sbk), jnp.stack(sbv))


_drawn_inputs = setup_inputs


def setup_inputs(seed=0):
    import zlib

    import numpy as np

    out = dict(_drawn_inputs(seed))
    spreads = {}
    factors = {'diff_lambda': 3.393,
     'a_norm_g': 3.286,
     'b_norm_g': 3.03,
     'g_ffn': 8.462,
     'g_final': 8.307}
    for name, (base, spread) in spreads.items():
        noise = np.random.default_rng([zlib.crc32(name.encode()), seed]).standard_normal(out[name].shape)
        drawn = base * np.exp(spread * noise) if base else spread * noise
        out[name] = __import__('jax').numpy.asarray(drawn.astype(out[name].dtype))
    for name, factor in factors.items():
        out[name] = (out[name] * factor).astype(out[name].dtype)
    return out
```

```python
from contextlib import ExitStack

import numpy as np

import concourse.bass as bass
from concourse import mybir

F32 = mybir.dt.float32
F32R = mybir.dt.float32r
U32 = mybir.dt.uint32
ALU = mybir.AluOpType
ACT = mybir.ActivationFunctionType
AX_X = mybir.AxisListType.X

P = 128
D = 1024
KC = D // P
N_META, SEQ, DEC, PAST = 16, 512, 64, 512
HD = 64
AH, BH = 4, 8
KP = N_META + SEQ
T = KP + DEC
TQ = SEQ + DEC
HQ = TQ // 2
HT = T // 2
CHUNK = 64
EPS = 1e-6
LAM_INIT = 0.2
SCALE = HD ** -0.5
NEG = -1e30
LOWEST = -3.0e38

N_QKV, N_WO, N_PQ = 24, 8, 16
B_WO = N_QKV
B_PQ = B_WO + N_WO
B_U = B_PQ + N_PQ
N_EXP_J = 128
B_V = B_U + N_EXP_J
N_GROUP = 16
NT_ALL = B_V + N_GROUP * KC

RT_TILES, RT_TOK, U1_PER = 6, 96, 12
U1_TILES = RT_TILES * U1_PER
G_BATCH, G_TOK = 16, 36
MID_TILES = 2
B_U2 = U1_TILES + MID_TILES
U2_ITERS, U2_PER = 4, 10
B_U3 = B_U2 + U2_ITERS * U2_PER
U3_TILES = N_EXP_J - B_U3
BATCH_PER = G_BATCH // U2_ITERS
Q_PER = BATCH_PER * (G_TOK // 4)
GR = 4
HR = 6
HEADS, TOPK = 8, 16
PAIRS = HEADS * TOPK
assert U3_TILES == 14 and Q_PER % GR == 0 and Q_PER % HR == 0 and RT_TILES * RT_TOK == TQ == G_BATCH * G_TOK

C_ID, C_TRI, C_ONE, C_BD, C_ROT, C_MASK, C_NEG, C_IOTA = (P * n for n in range(8))
C_IOTA16 = 8 * P
C_EPS = C_IOTA16 + TOPK
C_W = C_EPS + 1
G_ATTN, G_FFN, G_FINAL, G_A, G_B = 0, 8, 16, 24, 25
G_W = 26

PK = [0, 1, 2, 3, 4]
K_ROWS = [128, 128, 128, 128, 80]
Q_FROM = [0, 112, 240, 368, 496]
P_OFF = [0, 512, 912, 1184, 1584]
S_OFF = [1328, 1392, 1456, 1520, 1600]
B_COLS = 1664
UNITS = [
    (1328, [(128, 0, 256), (80, 256, 80)]),
    (912, [(128, 0, 416)]),
    (512, [(128, 0, 400)]),
    (0, [(128, 0, 512)]),
]
GROUPS = [
    [("s", kt, S_OFF[kt] - 1328, 64) for kt in range(4)] + [("p", 4, 256, 16), ("s", 4, 272, 64)],
    [("p", 3, 272, 144), ("p", 2, 0, 272)],
    [("p", 1, 0, 400)],
    [("p", 0, 0, 512)],
]


def bass_hybrid_step(nc, x_t, consts, tables, gains, lam_p, cache_k, cache_v, cache_vt, w_tiles, sub_keys,
                     y_out, kv_out):
    g_dram = nc.dram_tensor("gates_scattered", (G_BATCH * P, P * G_TOK), F32).ap()
    act_dram = nc.dram_tensor("activated", (N_EXP_J * P, TQ), F32).ap()

    with ExitStack() as ctx:
        base = [16512]

        def at(name, shape, dt, off):
            return nc.alloc_sbuf_tensor_at(name, shape, dt, offset=off)

        def fixed(name, shape, dt=F32):
            n = 4 * int(np.prod(shape[1:]))
            n = (n + 31) // 32 * 32
            off = base[0]
            base[0] += n
            return at(name, shape, dt, off)

        def sem(name):
            return ctx.enter_context(nc.semaphore(name))

        xh = fixed("xh", [P, KC, T])
        cst = fixed("cst", [P, C_W])
        gn = fixed("gn", [P, G_W])
        lam = fixed("lam", [P, 8])
        stat = fixed("stat", [P, 16])
        raw = fixed("raw", [P, 2, KC, P])
        w_hi = fixed("w_hi", [P, 2, KC, P], F32R)
        w_lo = fixed("w_lo", [P, 2, KC, P], F32R)
        m0_off = base[0]
        m0_hi = fixed("m0_hi", [P, KC, T], F32R)
        m0_lo = fixed("m0_lo", [P, KC, T], F32R)
        region = base[0]
        assert region <= 229344 - 121472

        off = region
        qkv = at("qkv", [P, 24, T], F32, off)
        off += 24 * T * 4
        v_nat = at("v_nat", [P, 5, 1024], F32, off)
        off += 5 * 4096
        vs4 = at("vs4", [P, 1024], F32, off)
        off += 4096
        v_cache = at("v_cache", [P, 4, 1024], F32, off)
        norm_off = off
        off += 4 * 4096
        k_cache = at("k_cache", [P, 8, T], F32, off)
        off += 8 * T * 4
        tab = at("tab", [P, 2, T], F32, off)
        off += 2 * T * 4
        assert off <= 229344
        nsq = at("nsq", [P, 2, T], F32, norm_off)
        nrs = at("nrs", [P, 2, T], F32, norm_off + 2 * T * 4)
        ntmp = at("ntmp", [P, 2, T], F32, norm_off + 4 * T * 4)
        off = m0_off
        logk = at("logk", [P, 2, B_COLS], F32, off)
        off += 2 * B_COLS * 4
        prob = at("prob", [P, 2, B_COLS], F32, off)
        off += 2 * B_COLS * 4
        t_abs = at("t_abs", [P, 2, 512], F32, off)
        off += 4096
        t_pos = at("t_pos", [P, 2, 512], F32, off)
        off += 4096
        assert off <= region
        rtmp = at("rtmp", [P, 2, T], F32, m0_off)
        lam_in = at("lam_in", [P, 256], F32, m0_off + 8 * T)
        vs_t = at("vs_t", [P, 8, 80], F32, m0_off + 8 * T + 2048)
        p_a = at("p_a", [P, 2, T], F32, m0_off)
        w_a = at("w_a", [P, 2, T], F32, m0_off + 8 * T)
        wt_a = at("wt_a", [P, 2, 5, P], F32, m0_off + 16 * T)

        off = region
        q_t = at("q_t", [P, 16, TQ], F32, off)
        cand = at("cand", [P, HEADS, TOPK, TOPK], F32, off)
        cand2 = at("cand2", [P, HEADS, TOPK, TOPK], F32, off + 8192)
        eqs = at("eqs", [P, PAIRS, TOPK], F32, off + 16384)
        cur2 = at("cur2", [P, 16, P], F32, off + 24576)
        small = off + 32768
        s16 = at("s16", [P, 16, TOPK], F32, small)
        c16 = at("c16", [P, HEADS, TOPK], F32, small + 1024)
        i16f = at("i16f", [P, 16, TOPK], F32, small + 1536)
        jf = at("jf", [P, 2, PAIRS], F32, small + 2560)
        g_st = at("g_st", [P, 2, P, G_TOK], F32, off)
        off += 16 * TQ * 4
        score = at("score", [P, RT_TILES, 16, P], F32, off)
        off += RT_TILES * 8192
        cur = at("cur", [P, 16, P], F32, off)
        off += 8192
        i16 = at("i16", [P, 16, TOPK], U32, off)
        off += 1024
        j16 = at("j16", [P, HEADS, TOPK], U32, off)
        off += 512
        jab = at("jab", [P, 2, PAIRS], U32, off)
        off += 1024
        act_st = at("act_st", [P, 2, TQ], F32, off)
        off += 2 * TQ * 4
        subk = at("subk", [P, 2, P], F32, off)
        off += 1024
        routed = at("routed", [P, RT_TILES, 3, PAIRS], F32, off)
        off += RT_TILES * 3 * PAIRS * 4
        rt_t = at("rt_t", [P, 4, TQ], F32, region + 16 * TQ * 4)
        g_hi = at("g_hi", [P, RT_TILES, PAIRS], F32R, region + 16 * TQ * 4 + 9216)
        g_lo = at("g_lo", [P, RT_TILES, PAIRS], F32R, region + 16 * TQ * 4 + 9216 + 3072)
        gexp = at("gexp", [P, RT_TILES, PAIRS], F32, region + 16 * TQ * 4 + 9216 + 6144)
        gsum = at("gsum", [P, 2, RT_TILES * HEADS], F32, region + 16 * TQ * 4 + 9216 + 9216)
        hot_off = region + 16 * TQ * 4 + 9216
        hot_i = at("hot_i", [P, HR, 4, P], F32R, hot_off)
        hot_jh = at("hot_jh", [P, HR, 4, P], F32R, hot_off + HR * 2048)
        hot_jl = at("hot_jl", [P, HR, 4, P], F32R, hot_off + 2 * HR * 2048)
        rt_b = at("rt_b", [P, 2, 4, G_TOK], F32, hot_off + 3 * HR * 2048)
        assert off <= 229344

        off = region
        m1_hi = at("m1_hi", [P, KC, TQ], F32R, off)
        off += KC * TQ * 4
        m1_lo = at("m1_lo", [P, KC, TQ], F32R, off)
        off += KC * TQ * 4
        g_in = at("g_in", [P, 2, G_BATCH, KC, G_TOK], F32, off)
        off += 2 * KC * TQ * 4
        act_in = at("act_in", [P, 2, 4, TQ], F32, off)
        off += 2 * 4 * TQ * 4
        gated = at("gated", [P, 2, TQ], F32, off)
        off += 2 * TQ * 4
        assert off <= 229344
        y_st = at("y_st", [P, KC, TQ], F32, region)

        ps = ctx.enter_context(nc.psum_tensor("ps", [P, 8, 512], F32))
        psf = ps[:].rearrange("p b n -> p (b n)")

        ident, tri = cst[:, C_ID:C_ID + P], cst[:, C_TRI:C_TRI + P]
        ones, blocks = cst[:, C_ONE:C_ONE + P], cst[:, C_BD:C_BD + P]
        rot, mask = cst[:, C_ROT:C_ROT + P], cst[:, C_MASK:C_MASK + P]
        negm, iota = cst[:, C_NEG:C_NEG + P], cst[:, C_IOTA:C_IOTA + P]
        iota16, eps = cst[:, C_IOTA16:C_IOTA16 + TOPK], cst[:, C_EPS:C_EPS + 1]

        consts_in, x_in = sem("consts_in"), sem("x_in")
        tables_in, caches_in = sem("tables_in"), sem("caches_in")
        raw_in = [sem("raw_in0"), sem("raw_in1")]
        hi_ready = sem("hi_ready")
        w_split = sem("w_split")
        half_done = sem("half_done")
        free_qkv, free_wo, free_pq = sem("free_qkv"), sem("free_wo"), sem("free_pq")
        free_u, free_v = sem("free_u"), sem("free_v")
        norm_sems = {n: {k: sem(f"{n}_{k}") for k in ("sq", "sum", "std", "rs", "x", "hi", "lo")}
                     for n in ("n1", "nm", "n2", "nf")}
        vt_done, vt_taken = sem("vt_done"), sem("vt_taken")
        rot_done, rope_step, rope_done = sem("rot_done"), sem("rope_step"), sem("rope_done")
        prep_done, lam_step, lam_exp = sem("prep_done"), sem("lam_step"), sem("lam_exp")
        ks_ready = sem("ks_ready")
        b_z, b_abs, b_exp, b_ln, b_log = sem("b_z"), sem("b_abs"), sem("b_exp"), sem("b_ln"), sem("b_log")
        b_raw, b_pos = sem("b_raw"), sem("b_pos")
        b_cum, b_prob, b_av, b_out = sem("b_cum"), sem("b_prob"), sem("b_av"), sem("b_out")
        a_s, a_max, a_neg, a_prob = sem("a_s"), sem("a_max"), sem("a_neg"), sem("a_prob")
        a_step, a_w, a_t, a_wt, a_o, a_out = (sem("a_step"), sem("a_w"), sem("a_t"), sem("a_wt"), sem("a_o"),
                                              sem("a_out"))
        kv_stored, ak_stored = sem("kv_stored"), sem("ak_stored")
        subk_in, sc_done, sc_taken = sem("subk_in"), sem("sc_done"), sem("sc_taken")
        cur_ready, top_read, r_step, routed_s = sem("cur_ready"), sem("top_read"), sem("r_step"), sem("routed_s")
        route_held = sem("route_held")
        g_step, g_exped, g_split = sem("g_step"), sem("g_exped"), sem("g_split")
        rt_done, rt_taken = sem("rt_done"), sem("rt_taken")
        act_stored = [sem("act_stored0"), sem("act_stored1")]
        rtb_ready = sem("rtb_ready")
        hot_ready, hot_used, gm_taken = sem("hot_ready"), sem("hot_used"), sem("gm_taken")
        hot_i_ready, hot_held = sem("hot_i_ready"), sem("hot_held")
        g_stored = [sem("g_stored0"), sem("g_stored1")]
        g_in_s = [sem("g_in0"), sem("g_in1")]
        act_in_s = [sem("act_in0"), sem("act_in1")]
        v_prod, v_hi, v_lo = sem("v_prod"), sem("v_hi"), sem("v_lo")
        y_stored = sem("y_stored")

        block = ctx.enter_context(nc.Block())

        MULT, ADD, SUB = ALU.mult, ALU.add, ALU.subtract

        def merged(c):
            return qkv[:, 8 + c if c < 4 else 16 + c, N_META:T]

        def groups_at(u, m):
            at_m = 48 * u + m + 1
            return [q for q in range(Q_PER) if (q + 1) * 48 * U2_PER // Q_PER == at_m]

        def before_half(u, h):
            late = groups_at(u, 23) if h else groups_at(u - 1, 47) if u else []
            return late + [q for m in range(24 * h, 24 * h + 23) for q in groups_at(u, m)]

        def groups_of(u, half=None):
            return [q for m in range(48) if half is None or m // 24 == half for q in groups_at(u, m)]

        @block.sync
        def _(sp):
            sp.sem_inc(w_split, 2)
            for s in (free_qkv, free_wo, free_pq, free_u, free_v):
                sp.sem_inc(s, 4)
            sp.dma_start(cst[:], consts).then_inc(consts_in, 16)
            sp.dma_start(gn[:], gains).then_inc(consts_in, 16)
            sp.dma_start(xh[:], x_t).then_inc(x_in, 16)

            def load_tile(n, slot):
                sp.wait_ge(w_split, n + 1)
                sp.dma_start(raw[:, slot], w_tiles[bass.ds(n * P, P), :]).then_inc(raw_in[slot], 16)

            with sp.Fori(0, (B_U + B_U3) // 8) as it:
                for u in range(8):
                    load_tile(it * 8 + u, u % 2)

            def load_group(g, gg):
                for s in act_stored:
                    sp.wait_ge(s, g * 64 + 80)
                sp.wait_ge(v_lo, g * 8 + 8)
                sp.dma_start(g_in[:, gg].rearrange("p b j t -> p b (j t)"),
                             g_dram[:, bass.ds(g * (KC * G_TOK), KC * G_TOK)].rearrange(
                                 "(b p) n -> p b n", p=P)).then_inc(g_in_s[gg], 16)
                for hh in range(2):
                    sp.wait_ge(v_lo, g * 8 + 4 * hh + 12)
                    sp.dma_start(act_in[:, hh],
                                 act_dram[bass.ds(g * (8 * P) + hh * 4 * P, 4 * P), :].rearrange(
                                     "(j p) t -> p j t", p=P)).then_inc(act_in_s[hh], 16)

            def load_vs(g, tiles):
                for c in range(tiles):
                    load_tile(g * KC + (B_V + c + 2), c % 2)

            for n in range((B_U + B_U3) // 8 * 8, B_V + 2):
                load_tile(n, n % 2)
                if n == B_U + B_U3 + 4:
                    for s in g_stored:
                        sp.wait_ge(s, 16 * (G_BATCH // 2) + 16)
                    load_group(0, 0)
            with sp.Fori(0, N_GROUP // 2 - 1) as it:
                for gg in range(2):
                    load_group(it * 2 + (gg + 1), 1 - gg)
                    load_vs(it * 2 + gg, KC)
            load_group(N_GROUP - 1, 1)
            load_vs(N_GROUP - 2, KC)
            load_vs(N_GROUP - 1, KC - 2)
            for c in range(KC):
                sp.wait_ge(norm_sems["nf"]["x"], c + 1)
                sp.dma_start(y_out[c], y_st[:, c]).then_inc(y_stored, 16)
            sp.wait_ge(y_stored, 16 * KC)

        @block.gpsimd
        def _(pool):
            pool.dma_start(tab[:], tables).then_inc(tables_in, 16)
            pool.dma_start(k_cache[:, :, 0:KP], cache_k).then_inc(caches_in, 16)
            pool.wait_ge(norm_sems["n1"]["lo"], KC)
            pool.dma_start(v_cache[:], cache_v).then_inc(caches_in, 16)
            pool.wait_ge(free_qkv, 4 + 2 * N_QKV)
            pool.dma_start(lam_in[:], lam_p.partition_broadcast(P)).then_inc(caches_in, 16)
            pool.dma_start(vs_t[:, :, 0:N_META], cache_vt).then_inc(caches_in, 16)
            bq = qkv[:, 12:16, :].rearrange("p c t -> p (c t)")
            nc.gpsimd.tensor_scalar(bq, bq, SCALE, 1.0, MULT, MULT).then_inc(prep_done, 1)
            nc.gpsimd.tensor_copy(k_cache[:, 4:8, KP:T], qkv[:, 16:20, KP:T]).then_inc(prep_done, 1)
            nc.gpsimd.tensor_copy(vs_t[:, 0:4, N_META:80], qkv[:, 8:12, KP:T]).then_inc(prep_done, 1)
            nc.gpsimd.tensor_copy(vs_t[:, 4:8, N_META:80], qkv[:, 20:24, KP:T]).then_inc(prep_done, 1)
            for k, c0 in ((1, 8), (2, 16), (3, 20)):
                pool.dma_start(kv_out[k], qkv[:, c0:c0 + 4, :]).then_inc(kv_stored, 16)
            pool.wait_ge(rope_done, 8)
            nc.gpsimd.tensor_copy(k_cache[:, 0:4, KP:T], qkv[:, 4:8, KP:T]).then_inc(ks_ready, 1)
            pool.dma_start(kv_out[0], qkv[:, 4:8, :]).then_inc(ak_stored, 16)
            pool.wait_ge(kv_stored, 48)
            pool.wait_ge(ak_stored, 16)
            pool.wait_ge(a_out, 5 * AH)
            pool.dma_start(subk[:], sub_keys).then_inc(subk_in, 16)
            pool.wait_ge(rt_taken, RT_TILES)
            pool.sem_inc(hot_i_ready, 18)
            with pool.Fori(0, U2_ITERS) as it:
                for q in range(Q_PER):
                    nb, qq = q // 9, q % 9
                    if qq == 0:
                        pool.wait_ge(rtb_ready, it * BATCH_PER + (nb + 1))
                        pool.sem_inc(hot_held, 1)
                    pool.wait_ge(hot_used, it * Q_PER + (q + 1))
                    pool.sem_inc(hot_held, 1)
                    for t in range(4):
                        last = nc.gpsimd.tensor_scalar(hot_i[:, q % HR, t, :], iota,
                                                       rt_b[:, nb % 2, 0, 4 * qq + t:4 * qq + t + 1], None,
                                                       ALU.is_equal)
                    last.then_inc(hot_i_ready, 1)

        @block.tensor
        def _(pe):
            pe.sem_inc(half_done, 4)

            def tile(n, slot, k, free, hi, lo, col, width, after=None):
                pe.wait_ge(w_split, n + 3)
                for h in range(2):
                    pe.wait_ge(free, k * 2 + h + 1)
                    c0 = col + h * width
                    m = 0
                    for kc in range(KC):
                        for w, x in ((w_hi, hi), (w_hi, lo), (w_lo, hi)):
                            mm = nc.tensor.matmul(ps[:, 2 * slot + h, 0:width], w[:, slot, kc, :],
                                                  x[:, kc, c0:c0 + width], start=(m == 0), stop=(m == 23))
                            m += 1
                            if m == 24:
                                mm.then_inc(half_done, 1)
                            if after is not None:
                                after(24 * h + m - 1)

            def norm_sum(name, weights, halves, step):
                s = norm_sems[name]
                for c in range(KC):
                    pe.wait_ge(s["sq"], c + 1)
                    if step and c >= 2:
                        pe.wait_ge(s["std"], 2 * (c - 1))
                    for h in range(2):
                        mm = nc.tensor.matmul(ps[:, (2 * (c % 2) if step else 0) + h, 0:halves],
                                              weights(c), nsq[:, c % 2, h * halves:(h + 1) * halves],
                                              start=(step or c == 0), stop=(step or c == KC - 1),
                                              skip_group_check=not step)
                    mm.then_inc(s["sum"], 1)

            pe.wait_ge(consts_in, 32)
            norm_sum("n1", lambda c: ones, HT, False)
            pe.wait_ge(norm_sems["n1"]["lo"], KC)
            with pe.Fori(0, N_QKV // 4) as it:
                for u in range(4):
                    n = it * 4 + u
                    tile(n, u % 2, n, free_qkv, m0_hi, m0_lo, 0, HT)
            pe.wait_ge(free_qkv, 4 + 2 * N_QKV)
            pe.wait_ge(prep_done, 4)
            pe.wait_ge(caches_in, 64)
            for i in range(12):
                kt, s = i // 2, i % 2
                if i >= 4:
                    pe.wait_ge(vt_taken, i - 3)
                for c in range(4):
                    if kt < 5:
                        src = qkv[:, (8, 20)[s] + c, kt * P:min(T, kt * P + P)]
                    else:
                        src = vs_t[:, 4 * s + c, :]
                    rows = 128 if kt < 4 else 80
                    mm = nc.tensor.transpose(ps[0:rows, i % 4, c * P:(c + 1) * P], src, ident)
                mm.then_inc(vt_done, 1)
            for c in range(8):
                if c >= 2:
                    pe.wait_ge(rope_done, c - 1)
                b = 4 + 2 * (c % 2)
                nc.tensor.matmul(ps[:, b, 0:512], rot, qkv[:, c, 0:512], start=True, stop=True)
                nc.tensor.matmul(ps[:, b + 1, 0:T - 512], rot, qkv[:, c, 512:T],
                                 start=True, stop=True).then_inc(rot_done, 1)

            pe.wait_ge(vt_taken, 12)
            pe.wait_ge(rope_done, 8)

            def qk(h, kind, kt, dst, start, stop):
                r, c = 64 * (h % 2), h // 2
                rows = K_ROWS[kt]
                if kind == "p":
                    k = qkv[r:r + 64, 16 + c, kt * P:kt * P + rows]
                    q = qkv[r:r + 64, 12 + c, N_META + Q_FROM[kt]:KP]
                else:
                    k = k_cache[r:r + 64, 4 + c, kt * P:kt * P + rows]
                    q = qkv[r:r + 64, 12 + c, KP:T]
                return nc.tensor.matmul(dst, k, q, start=start, stop=stop)

            for h in range(BH + 1):
                for u in range(4):
                    if h < BH:
                        idx = 4 * h + u
                        if idx >= 3:
                            pe.wait_ge(b_abs, idx - 2)
                        for kind, kt, o, n in GROUPS[u]:
                            mm = qk(h, kind, kt, ps[0:K_ROWS[kt], idx % 3, o:o + n], True, True)
                        mm.then_inc(b_z, 1)
                    if h >= 1:
                        idx, hp = 4 * (h - 1) + u, h - 1
                        pe.wait_ge(b_log, idx + 1)
                        if idx >= 3:
                            pe.wait_ge(b_prob, idx - 2)
                        for kind, kt, o, n in GROUPS[u]:
                            rows = K_ROWS[kt]
                            dst = ps[0:rows, 3 + idx % 3, o:o + n]
                            qk(hp, kind, kt, dst, True, False)
                            offs = P_OFF if kind == "p" else S_OFF
                            lg = logk[:, hp % 2]
                            last = kind == "s" and kt < 4
                            for k2 in range(4, kt, -1):
                                c2 = Q_FROM[k2] - Q_FROM[kt] if kind == "p" else 0
                                n2 = n - c2
                                r2 = K_ROWS[k2]
                                nc.tensor.matmul(ps[0:rows, 3 + idx % 3, o + c2:o + n], ones[0:r2, 0:rows],
                                                 lg[0:r2, offs[k2]:offs[k2] + n2], start=False, stop=False)
                            mm = nc.tensor.matmul(dst, tri[0:rows, 0:rows], lg[0:rows, offs[kt]:offs[kt] + n],
                                                  start=False, stop=last)
                            if not last:
                                if kind == "p":
                                    nm = P - 16 if kt == 0 else min(n, P)
                                    m0 = 16 if kt == 0 else 0
                                else:
                                    nm, m0 = 64, 16
                                mm = nc.tensor.matmul(ps[0:rows, 3 + idx % 3, o:o + nm], ident[0:rows, 0:rows],
                                                      negm[0:rows, m0:m0 + nm], start=False, stop=True)
                        mm.then_inc(b_cum, 1)
                if h >= 1:
                    hp = h - 1
                    r, c = 64 * (hp % 2), hp // 2
                    pe.wait_ge(b_prob, 4 * h)
                    if hp >= 1:
                        pe.wait_ge(b_out, hp)
                    pr = prob[:, hp % 2]
                    vc = 512 + 64 * hp
                    for kt in range(5):
                        rows = K_ROWS[kt]
                        nc.tensor.matmul(ps[r:r + 64, 6, Q_FROM[kt]:512], v_nat[0:rows, kt, vc:vc + 64],
                                         pr[0:rows, P_OFF[kt]:P_OFF[kt] + 512 - Q_FROM[kt]],
                                         start=(kt == 0), stop=(kt == 4))
                    for kt in range(5):
                        rows = K_ROWS[kt]
                        v = v_cache[:, kt, vc:vc + 64] if kt < 4 else vs4[0:80, vc:vc + 64]
                        mm = nc.tensor.matmul(ps[r:r + 64, 7, 0:64], v, pr[0:rows, S_OFF[kt]:S_OFF[kt] + 64],
                                              start=(kt == 0), stop=(kt == 4))
                    mm.then_inc(b_av, 1)

            pe.wait_ge(b_out, BH)
            pe.wait_ge(ks_ready, 1)

            def a_scores(idx):
                h, i = idx // 5, idx % 5
                for m in range(2):
                    if idx >= 1:
                        pe.wait_ge(a_prob, 2 * idx - 1 + m)
                    r = slice(64 * m, 64 * m + 64)
                    if i < 4:
                        q = qkv[r, h, N_META + P * i:N_META + P * (i + 1)]
                        w, keys, rows = 144 + P * i, qkv[r, 4 + h, :], P
                    else:
                        q, w, keys, rows = qkv[r, h, KP:T], T, k_cache[r, h, :], 64
                    for b0 in range(0, w, 512):
                        n = min(512, w - b0)
                        mm = nc.tensor.matmul(ps[0:rows, 2 * m + b0 // 512, 0:n], q, keys[:, b0:b0 + n],
                                              start=True, stop=True)
                    mm.then_inc(a_s, 1)

            NA = 5 * AH
            a_scores(0)
            for idx in range(NA):
                h, i = idx // 5, idx % 5
                if idx + 1 < NA:
                    a_scores(idx + 1)
                rows = P if i < 4 else 64
                full = i + 1 if i < 4 else 4
                part = 16 if i < 4 else 80
                pe.wait_ge(a_w, idx + 1)
                if idx >= 1:
                    pe.wait_ge(a_wt, idx)
                for kt in range(full):
                    nc.tensor.transpose(ps[:, 4, kt * rows:(kt + 1) * rows], w_a[0:rows, idx % 2, kt * P:(kt + 1) * P],
                                        ident[0:rows, 0:rows])
                nc.tensor.transpose(ps[0:part, 5, 0:rows], w_a[0:rows, idx % 2, full * P:full * P + part],
                                    ident[0:rows, 0:rows]).then_inc(a_t, 1)
                pe.wait_ge(a_wt, idx + 1)
                if idx >= 2:
                    pe.wait_ge(a_out, idx - 1)
                for kt in range(full + 1):
                    r = P if kt < full else part
                    if i < 4:
                        v = v_nat[0:r, kt, h * P:(h + 1) * P]
                    else:
                        v = v_cache[:, kt, h * P:(h + 1) * P] if kt < 4 else vs4[0:80, h * P:(h + 1) * P]
                    wt = wt_a[0:r, idx % 2, kt, 0:rows]
                    mm = nc.tensor.matmul(ps[:, 6 + idx % 2, 0:rows], v, wt, start=(kt == 0), stop=(kt == full))
                mm.then_inc(a_o, 1)

            norm_sum("nm", lambda c: ones if c < 4 else blocks, HQ, True)
            pe.wait_ge(norm_sems["nm"]["lo"], KC)
            for u in range(N_WO):
                tile(B_WO + u, u % 2, u, free_wo, m0_hi, m0_lo, 0, HQ)

            pe.wait_ge(free_wo, 4 + 2 * N_WO)
            norm_sum("n2", lambda c: ones, HQ, False)
            pe.wait_ge(norm_sems["n2"]["lo"], KC)
            with pe.Fori(0, N_PQ // 4) as it:
                for u in range(4):
                    tile(it * 4 + (B_PQ + u), u % 2, it * 4 + u, free_pq, m0_hi, m0_lo, 0, HQ)
            pe.wait_ge(free_pq, 4 + 2 * N_PQ)
            pe.wait_ge(subk_in, 16)
            for i in range(RT_TILES * 4):
                t, b = i // 4, i % 4
                if i >= 4:
                    pe.wait_ge(sc_taken, i - 3)
                for j in range(4):
                    hp = 4 * b + j
                    mm = nc.tensor.matmul(ps[0:RT_TOK, 4 + i % 4, j * P:(j + 1) * P],
                                          q_t[:, hp, t * RT_TOK:(t + 1) * RT_TOK], subk[:, hp % 2, :],
                                          start=True, stop=True)
                mm.then_inc(sc_done, 1)

            with pe.Fori(0, RT_TILES) as it:
                for u in range(U1_PER):
                    n = it * U1_PER + u
                    tile(n + B_U, u % 2, n, free_u, m0_hi, m0_lo, 0, HQ)
            for u in range(MID_TILES):
                n = U1_TILES + u
                tile(n + B_U, u % 2, n, free_u, m0_hi, m0_lo, 0, HQ)
            pe.wait_ge(g_split, 2)
            for t in range(RT_TILES):
                if t >= 2:
                    pe.wait_ge(rt_taken, t - 1)
                for k, src in enumerate((routed[0:RT_TOK, t, 0, :], routed[0:RT_TOK, t, 1, :],
                                         g_hi[0:RT_TOK, t, :].bitcast(F32), g_lo[0:RT_TOK, t, :].bitcast(F32))):
                    mm = nc.tensor.transpose(ps[:, 4 + t % 2, k * RT_TOK:(k + 1) * RT_TOK], src,
                                             ident[0:RT_TOK, 0:RT_TOK])
                mm.then_inc(rt_done, 1)
            pe.sem_inc(hot_used, HR)
            with pe.Fori(0, U2_ITERS) as it:

                def scatter(q):
                    k = it * Q_PER + q
                    pe.wait_ge(hot_ready, k + 19)
                    pe.wait_ge(hot_i_ready, k + 19)
                    pe.wait_ge(gm_taken, k + 1)
                    for t in range(4):
                        dst = ps[:, 4 + q % GR, t * P:(t + 1) * P]
                        nc.tensor.matmul(dst, hot_i[:, q % HR, t, :], hot_jh[:, q % HR, t, :],
                                         start=True, stop=False)
                        mm = nc.tensor.matmul(dst, hot_i[:, q % HR, t, :], hot_jl[:, q % HR, t, :],
                                              start=False, stop=True)
                    mm.then_inc(hot_used, 1)

                for u in range(U2_PER):
                    n = it * U2_PER + (B_U2 + u)
                    tile(n + B_U, u % 2, n, free_u, m0_hi, m0_lo, 0, HQ,
                         lambda m: [scatter(q) for q in groups_at(u, m)])
            with pe.Fori(0, U3_TILES // 2) as it:
                for u in range(2):
                    n = it * 2 + (B_U3 + u)
                    tile(n + B_U, u, n, free_u, m0_hi, m0_lo, 0, HQ)
            pe.wait_ge(free_u, 4 + 2 * N_EXP_J)
            with pe.Fori(0, N_GROUP // 2) as it:
                for gg in range(2):
                    g = it * 2 + gg
                    hi, lo = ((m1_hi, m1_lo), (m0_hi, m0_lo))[gg]
                    pe.wait_ge(v_lo, g * 8 + 24)
                    for c in range(KC):
                        tile(g * KC + (B_V + c), c % 2, g * KC + c, free_v, hi, lo, 0, HQ)
            pe.wait_ge(free_v, 4 + 2 * N_GROUP * KC)
            norm_sum("nf", lambda c: ones, HQ, False)

        @block.scalar
        def _(act):
            def hi_part(n, slot, k):
                act.wait_ge(raw_in[slot], k * 16)
                act.wait_ge(half_done, n * 2 + 2)
                nc.scalar.copy(w_hi[:, slot], raw[:, slot]).then_inc(hi_ready, 1)

            def norm(name, src, cols, halves, stepwise, hi=None):
                s = norm_sems[name]
                w = 2 * halves

                def std(c):
                    for h in range(2):
                        n = HD if (stepwise and c >= 4) else P if stepwise else D
                        b = (2 * (c % 2) if stepwise else 0) + h
                        act.wait_ge(s["sum"], c + 1)
                        if stepwise and c >= 2:
                            act.wait_ge(s["x"], c - 1)
                        nc.scalar.activation(nrs[:, c % 2 if stepwise else 0, h * halves:(h + 1) * halves],
                                             ps[:, b, 0:halves], ACT.Sqrt, bias=eps,
                                             scale=1.0 / n).then_inc(s["std"], 1)

                def high(c):
                    act.wait_ge(s["x"], c + 1)
                    nc.scalar.copy(hi[:, c, 0:w], ntmp[:, c % 2, 0:w]).then_inc(s["hi"], 1)

                for c in range(KC):
                    if c >= 2:
                        act.wait_ge(s["sum"], c - 1)
                    nc.scalar.square(nsq[:, c % 2, 0:w], src(c)).then_inc(s["sq"], 1)
                    if stepwise and c >= 1:
                        std(c - 1)
                    if stepwise and c >= 2:
                        high(c - 2)
                std(KC - 1)
                if hi is not None:
                    for c in range(KC - 2 if stepwise else 0, KC):
                        high(c)

            act.wait_ge(consts_in, 32)
            act.wait_ge(x_in, 16)
            norm("n1", lambda c: xh[:, c, :], T, HT, False, m0_hi)
            hi_part(0, 0, 1)
            with act.Fori(0, N_QKV // 4) as it:
                for u in range(4):
                    hi_part(it * 4 + (u + 1), (u + 1) % 2, it * 2 + ((u + 1) // 2 + 1))
                    for h in range(2):
                        act.wait_ge(half_done, it * 8 + (2 * u + h + 5))
                        nc.scalar.copy(qkv[:, bass.ds(it * 4 + u, 1), h * HT:(h + 1) * HT],
                                       ps[:, 2 * (u % 2) + h:2 * (u % 2) + h + 1, 0:HT]).then_inc(free_qkv, 1)
            for i in range(12):
                kt, s = i // 2, i % 2
                act.wait_ge(vt_done, i + 1)
                rows = 128 if kt < 4 else 80
                dst = v_nat[0:rows, kt, 512 * s:512 * s + 512] if kt < 5 else vs4[0:80, 512 * s:512 * s + 512]
                nc.scalar.copy(dst, ps[0:rows, i % 4, :]).then_inc(vt_taken, 1)
            act.wait_ge(lam_step, 2)
            nc.scalar.activation(lam[:, 2:4], lam[:, 0:2], ACT.Exp).then_inc(lam_exp, 1)

            act.wait_ge(kv_stored, 48)
            for h in range(BH + 1):
                for u in range(4):
                    if h < BH:
                        idx = 4 * h + u
                        act.wait_ge(b_abs, idx + 1)
                        for rows, o, n in UNITS[u][1]:
                            t = t_abs[0:rows, idx % 2, o:o + n]
                            e1 = nc.scalar.activation(t, t, ACT.Exp)
                        e1.then_inc(b_exp, 1)
                        act.wait_ge(b_exp, idx + 1)
                        for rows, o, n in UNITS[u][1]:
                            t = t_abs[0:rows, idx % 2, o:o + n]
                            e2 = nc.scalar.activation(t, t, ACT.Ln, bias=1.0)
                        e2.then_inc(b_ln, 1)
                    if h >= 1:
                        idx = 4 * (h - 1) + u
                        act.wait_ge(b_cum, idx + 1)
                        if h >= 3:
                            act.wait_ge(b_av, h - 2)
                        for rows, o, n in UNITS[u][1]:
                            off = UNITS[u][0] + o
                            e3 = nc.scalar.activation(prob[0:rows, (h - 1) % 2, off:off + n],
                                                      ps[0:rows, 3 + idx % 3, o:o + n], ACT.Exp)
                        e3.then_inc(b_prob, 1)
                if h >= 1:
                    hp = h - 1
                    r, c = 64 * (hp % 2), 20 + hp // 2
                    act.wait_ge(b_av, h)
                    nc.scalar.copy(qkv[r:r + 64, c, N_META:KP], ps[r:r + 64, 6, :])
                    nc.scalar.copy(qkv[r:r + 64, c, KP:T], ps[r:r + 64, 7, 0:64]).then_inc(b_out, 1)

            for idx in range(5 * AH):
                h, i = idx // 5, idx % 5
                rows, w = (P, 144 + P * i) if i < 4 else (64, T)
                for m in range(2):
                    act.wait_ge(a_neg, 2 * idx + m + 1)
                    if idx >= 1:
                        act.wait_ge(a_w, idx)
                    nc.scalar.activation(p_a[0:rows, m, 0:w], psf[0:rows, 1024 * m:1024 * m + w], ACT.Exp,
                                         bias=stat[0:rows, 2 + m:3 + m], scale=SCALE,
                                         accum_out=stat[0:rows, 4 + m:5 + m]).then_inc(a_prob, 1)
                full = i + 1 if i < 4 else 4
                part = 16 if i < 4 else 80
                act.wait_ge(a_t, idx + 1)
                if idx >= 2:
                    act.wait_ge(a_o, idx - 1)
                nc.scalar.copy(wt_a[:, idx % 2, 0:full, 0:rows],
                               ps[:, 4, 0:full * rows].rearrange("p (k q) -> p k q", q=rows))
                nc.scalar.copy(wt_a[0:part, idx % 2, full, 0:rows], ps[0:part, 5, 0:rows]).then_inc(a_wt, 1)
                act.wait_ge(a_o, idx + 1)
                q0 = N_META + P * i if i < 4 else KP
                nc.scalar.copy(qkv[:, 8 + h, q0:q0 + rows], ps[:, 6 + idx % 2, 0:rows]).then_inc(a_out, 1)

            act.wait_ge(a_out, 5 * AH)
            norm("nm", merged, None, HQ, True, m0_hi)
            for u in range(N_WO):
                hi_part(B_WO + u + 1, (u + 1) % 2, (B_WO + u + 1) // 2 + 1)
            act.wait_ge(free_wo, 4 + 2 * N_WO)
            norm("n2", lambda c: xh[:, c, N_META:T], None, HQ, False, m0_hi)
            act.wait_ge(ak_stored, 16)
            with act.Fori(0, N_PQ // 4) as it:
                for u in range(4):
                    n0 = B_PQ + u
                    hi_part(it * 4 + (n0 + 1), (u + 1) % 2, it * 2 + ((n0 + 1) // 2 + 1))
                    for h in range(2):
                        act.wait_ge(half_done, it * 8 + (2 * n0 + h + 5))
                        nc.scalar.copy(q_t[:, bass.ds(it * 4 + u, 1), h * HQ:(h + 1) * HQ],
                                       ps[:, 2 * (u % 2) + h:2 * (u % 2) + h + 1, 0:HQ]).then_inc(free_pq, 1)
            for i in range(RT_TILES * 4):
                t, b = i // 4, i % 4
                act.wait_ge(sc_done, i + 1)
                nc.scalar.copy(score[0:RT_TOK, t, 4 * b:4 * b + 4, :],
                               ps[0:RT_TOK, 4 + i % 4, :].rearrange("p (j n) -> p j n", j=4)).then_inc(sc_taken, 1)
            act.wait_ge(sc_taken, RT_TILES * 4)

            def v_high(g8, j, buf):
                act.wait_ge(v_prod, g8 + (j + 1))
                nc.scalar.copy((m1_hi, m0_hi)[buf][:, j, 0:TQ], gated[:, j % 2, :]).then_inc(v_hi, 1)

            for s in act_stored + g_stored:
                act.sem_inc(s, 16)

            def u_step(n, n0, u, it, per, between=None):
                hi_part(n + (B_U + 1), (u + 1) % 2, it * (per // 2) + ((B_U + n0 + 1) // 2 + 1))
                act.wait_ge(act_stored[u % 2], it * (8 * per) + (16 * (n0 // 2) + 16))
                for h in range(2):
                    if between is not None:
                        between(h)
                    act.wait_ge(half_done, n * 2 + (2 * B_U + h + 5))
                    nc.scalar.activation(act_st[:, u % 2, h * HQ:(h + 1) * HQ], ps[:, 2 * (u % 2) + h, 0:HQ],
                                         ACT.Gelu).then_inc(free_u, 1)
                act.wait_ge(free_u, n * 2 + 6)
                act.dma_start(act_dram[bass.ds(n * P, P), :],
                              act_st[:, u % 2]).then_inc(act_stored[u % 2], 16)

            with act.Fori(0, RT_TILES) as it:
                act.wait_ge(top_read, it + 1)
                nc.scalar.copy(cur[0:RT_TOK].unsqueeze(1),
                               score[0:RT_TOK, bass.ds(it, 1), :, :]).then_inc(cur_ready, 1)
                for u in range(U1_PER):
                    u_step(it * U1_PER + u, u, u, it, U1_PER)

            def gates_exp(h):
                if h == 0:
                    act.wait_ge(g_step, 1)
                    nc.scalar.activation(gexp[0:RT_TOK], gexp[0:RT_TOK], ACT.Exp).then_inc(g_exped, 1)

            for u in range(MID_TILES):
                u_step(U1_TILES + u, U1_TILES + u, u, 0, 0, gates_exp if u == 0 else None)
            for t in range(RT_TILES):
                act.wait_ge(rt_done, t + 1)
                nc.scalar.copy(rt_t[:, :, t * RT_TOK:(t + 1) * RT_TOK],
                               ps[:, 4 + t % 2, 0:4 * RT_TOK].rearrange("p (k t) -> p k t", k=4)).then_inc(rt_taken, 1)
            act.wait_ge(rt_taken, RT_TILES)
            act.sem_inc(gm_taken, GR)

            with act.Fori(0, U2_ITERS) as it:

                def rows_of(nb):
                    b = it * BATCH_PER + nb
                    act.wait_ge(hot_ready, b * 9 + 9)
                    act.wait_ge(hot_i_ready, b * 9 + 9)
                    nc.scalar.copy(rt_b[:, nb % 2], rt_t[:, :, bass.ds(b * G_TOK, G_TOK)]).then_inc(rtb_ready, 1)

                def take_gates(q):
                    nb, qq = q // 9, q % 9
                    if qq == 1 and nb + 1 < BATCH_PER:
                        rows_of(nb + 1)
                    act.wait_ge(hot_used, it * Q_PER + (q + 1 + HR))
                    if qq == 0:
                        act.wait_ge(g_stored[nb % 2], it * (8 * BATCH_PER) + (16 * (nb // 2) + 16))
                    nc.scalar.copy(g_st[:, nb % 2, :, 4 * qq:4 * qq + 4],
                                   ps[:, 4 + q % GR, :].rearrange("p (t j) -> p j t", t=4)).then_inc(gm_taken, 1)
                    if qq == 8:
                        act.wait_ge(gm_taken, it * Q_PER + (q + 1 + GR))
                        act.dma_start(g_dram[bass.ds((it * BATCH_PER + nb) * P, P), :],
                                      g_st[:, nb % 2].rearrange("p j t -> p (j t)")).then_inc(g_stored[nb % 2], 16)

                rows_of(0)
                for u in range(U2_PER):
                    u_step(it * U2_PER + (B_U2 + u), B_U2 + u, u, it, U2_PER,
                           lambda h: [take_gates(q) for q in before_half(u, h)])
                for q in groups_at(U2_PER - 1, 47):
                    take_gates(q)
            for u in range(U3_TILES):
                n = B_U3 + u
                u_step(n, n, u, 0, 0, (lambda h: v_high(0, u - 6, 0) if h == 0 else None) if u >= 6 else None)

            def v_steps(g, gg, last):
                for c in range(KC):
                    n0 = B_V + gg * KC + c
                    if not (last and c == KC - 1):
                        hi_part(g * KC + (B_V + c + 1), (c + 1) % 2, g * 4 + ((B_V + c + 1) // 2 + 1))
                    if not last:
                        v_high(g * 8 + 8, c, (gg + 1) % 2)

            with act.Fori(0, N_GROUP // 2 - 1) as it:
                for gg in range(2):
                    v_steps(it * 2 + gg, gg, False)
            v_steps(N_GROUP - 2, 0, False)
            v_steps(N_GROUP - 1, 1, True)
            act.wait_ge(free_v, 4 + 2 * N_GROUP * KC)
            norm("nf", lambda c: xh[:, c, N_META:T], None, HQ, False)

        @block.vector
        def _(dve):
            TT, TS = nc.vector.tensor_tensor, nc.vector.tensor_scalar

            def lo_part(n, slot):
                dve.wait_ge(hi_ready, n + 1)
                TT(w_lo[:, slot], raw[:, slot], w_hi[:, slot].bitcast(F32), SUB).then_inc(w_split, 1)

            def norm(name, src, gain, w, stepwise, hi, lo, out=None):
                s = norm_sems[name]

                def rs(c):
                    dve.wait_ge(s["std"], 2 * c + 2)
                    r = nrs[:, c % 2 if stepwise else 0, 0:w]
                    nc.vector.reciprocal(r, r).then_inc(s["rs"], 1)
                    dve.wait_ge(s["rs"], c + 1)

                def low(c):
                    dve.wait_ge(s["hi"], c + 1)
                    TT(lo[:, c, 0:w], ntmp[:, c % 2, 0:w], hi[:, c, 0:w].bitcast(F32), SUB).then_inc(s["lo"], 1)

                if not stepwise:
                    rs(0)
                for c in range(KC):
                    if stepwise:
                        rs(c)
                    if hi is not None and c >= 2:
                        dve.wait_ge(s["lo"], c - 1)
                    dst = ntmp[:, c % 2, 0:w] if out is None else out[:, c]
                    nc.vector.scalar_tensor_tensor(dst, src(c), gain(c), nrs[:, c % 2 if stepwise else 0, 0:w],
                                                   MULT, MULT).then_inc(s["x"], 1)
                    if hi is not None and c >= 1:
                        low(c - 1)
                if hi is not None:
                    low(KC - 1)

            dve.wait_ge(consts_in, 32)
            dve.wait_ge(x_in, 16)
            norm("n1", lambda c: xh[:, c, :], lambda c: gn[:, G_ATTN + c:G_ATTN + c + 1], T, False, m0_hi, m0_lo)
            lo_part(0, 0)
            with dve.Fori(0, N_QKV // 4) as it:
                for u in range(4):
                    lo_part(it * 4 + (u + 1), (u + 1) % 2)

            dve.wait_ge(free_qkv, 4 + 2 * N_QKV)
            dve.wait_ge(tables_in, 16)
            for c in range(8):
                b = 4 + 2 * (c % 2)
                dve.wait_ge(rot_done, c + 1)
                if c >= 2:
                    dve.wait_ge(rope_done, c - 1)
                TT(rtmp[:, c % 2, :], psf[:, 512 * b:512 * b + T], tab[:, 1, :], MULT).then_inc(rope_step, 1)
                TT(qkv[:, c, :], qkv[:, c, :], tab[:, 0, :], MULT).then_inc(rope_step, 1)
                dve.wait_ge(rope_step, 2 * c + 2)
                TT(qkv[:, c, :], qkv[:, c, :], rtmp[:, c % 2, :], ADD).then_inc(rope_done, 1)
            dve.wait_ge(caches_in, 64)
            lp = lam_in[:].rearrange("p (a b d) -> p a b d", a=2, b=2)
            TT(lp[:, :, 0, :], lp[:, :, 0, :], lp[:, :, 1, :], MULT).then_inc(lam_step, 1)
            dve.wait_ge(lam_step, 1)
            nc.vector.tensor_reduce(lam[:, 0:2], lp[:, :, 0, :], AX_X, ADD).then_inc(lam_step, 1)
            dve.wait_ge(lam_exp, 1)
            TT(lam[:, 4:5], lam[:, 3:4], lam[:, 2:3], SUB).then_inc(lam_step, 1)
            dve.wait_ge(lam_step, 3)
            TS(lam[:, 5:6], lam[:, 4:5], -LAM_INIT, None, ADD).then_inc(lam_step, 1)
            TS(gn[:, G_A:G_A + 1], gn[:, G_A:G_A + 1], 1.0 - LAM_INIT, None, MULT).then_inc(lam_step, 1)
            dve.wait_ge(lam_step, 5)

            def b_first(idx):
                u = idx % 4
                dve.wait_ge(b_z, idx + 1)
                if idx >= 2:
                    dve.wait_ge(b_log, idx - 1)
                for rows, o, n in UNITS[u][1]:
                    z = ps[0:rows, idx % 3, o:o + n]
                    last = TS(t_pos[0:rows, idx % 2, o:o + n], z, 0.0, None, ALU.max)
                last.then_inc(b_pos, 1)
                dve.wait_ge(b_pos, idx + 1)
                for rows, o, n in UNITS[u][1]:
                    last = nc.vector.scalar_tensor_tensor(t_abs[0:rows, idx % 2, o:o + n],
                                                          t_pos[0:rows, idx % 2, o:o + n], -2.0,
                                                          ps[0:rows, idx % 3, o:o + n], MULT, ADD)
                last.then_inc(b_abs, 1)

            def b_second(idx):
                h, u = idx // 4, idx % 4
                dve.wait_ge(b_ln, idx + 1)
                if h >= 2:
                    dve.wait_ge(b_cum, 4 * (h - 1))
                dve.wait_ge(b_abs, idx + 1)
                for rows, o, n in UNITS[u][1]:
                    off = UNITS[u][0] + o
                    last = nc.vector.scalar_tensor_tensor(logk[0:rows, h % 2, off:off + n],
                                                          t_abs[0:rows, idx % 2, o:o + n], -1.0,
                                                          t_pos[0:rows, idx % 2, o:o + n], MULT, SUB)
                last.then_inc(b_raw, 1)
                dve.wait_ge(b_raw, idx + 1)
                masks = {0: [(80, 1584, 80, 0)], 1: [(128, 912, 128, 0), (128, 1184, 128, 0)],
                         2: [(128, 512, 128, 0)], 3: [(128, 0, 112, 16)]}[u]
                for rows, off, n, m0 in masks:
                    lg = logk[0:rows, h % 2, off:off + n]
                    last = TT(lg, lg, mask[0:rows, m0:m0 + n], MULT)
                last.then_inc(b_log, 1)

            b_first(0)
            for idx in range(4 * BH):
                if idx + 1 < 4 * BH:
                    b_first(idx + 1)
                b_second(idx)

            k_step = 0
            dve.wait_ge(b_out, BH)
            for idx in range(5 * AH):
                h, i = idx // 5, idx % 5
                rows, w = (P, 144 + P * i) if i < 4 else (64, T)
                for m in range(2):
                    dve.wait_ge(a_s, 2 * idx + m + 1)
                    s = psf[0:rows, 1024 * m:1024 * m + w]
                    if i < 4:
                        e0 = 1024 * m + w
                        if w > 512 and w - CHUNK < 512:
                            nc.vector.memset(psf[0:CHUNK, e0 - CHUNK:1024 * m + 512], NEG)
                            last = nc.vector.memset(psf[0:CHUNK, 1024 * m + 512:e0], NEG)
                        else:
                            last = nc.vector.memset(psf[0:CHUNK, e0 - CHUNK:e0], NEG)
                        last.then_inc(a_step, 1)
                        k_step += 1
                        dve.wait_ge(a_step, k_step)
                    nc.vector.tensor_reduce(stat[0:rows, m:m + 1], s, AX_X, ALU.max).then_inc(a_max, 1)
                    dve.wait_ge(a_max, 2 * idx + m + 1)
                    if idx >= 1:
                        dve.wait_ge(a_prob, 2 * idx)
                    TS(stat[0:rows, 2 + m:3 + m], stat[0:rows, m:m + 1], -SCALE, None, MULT).then_inc(a_neg, 1)
                dve.wait_ge(a_prob, 2 * idx + 2)
                nc.vector.reciprocal(stat[0:rows, 6:8], stat[0:rows, 4:6]).then_inc(a_step, 1)
                k_step += 1
                dve.wait_ge(a_step, k_step)
                TT(stat[0:rows, 8:9], stat[0:rows, 7:8], lam[0:rows, 5:6], MULT).then_inc(a_step, 1)
                if idx >= 2:
                    dve.wait_ge(a_t, idx - 1)
                TS(w_a[0:rows, idx % 2, 0:w], p_a[0:rows, 0, 0:w], stat[0:rows, 6:7], None,
                   MULT).then_inc(a_step, 1)
                k_step += 2
                dve.wait_ge(a_step, k_step)
                nc.vector.scalar_tensor_tensor(w_a[0:rows, idx % 2, 0:w], p_a[0:rows, 1, 0:w], stat[0:rows, 8:9],
                                               w_a[0:rows, idx % 2, 0:w], MULT, ADD).then_inc(a_w, 1)

            dve.wait_ge(a_t, 5 * AH)
            dve.wait_ge(a_o, 5 * AH)
            norm("nm", merged, lambda c: gn[:, G_A:G_A + 1] if c < 4 else gn[:, G_B:G_B + 1], TQ, True, m0_hi,
                 m0_lo)
            for u in range(N_WO):
                lo_part(B_WO + u + 1, (u + 1) % 2)
                for h in range(2):
                    dve.wait_ge(half_done, 2 * (B_WO + u) + h + 5)
                    dst = xh[:, u, N_META + h * HQ:N_META + (h + 1) * HQ]
                    TT(dst, ps[:, 2 * (u % 2) + h, 0:HQ], dst, ADD).then_inc(free_wo, 1)
            norm("n2", lambda c: xh[:, c, N_META:T], lambda c: gn[:, G_FFN + c:G_FFN + c + 1], TQ, False, m0_hi,
                 m0_lo)
            with dve.Fori(0, N_PQ // 4) as it:
                for u in range(4):
                    lo_part(it * 4 + (B_PQ + u + 1), (u + 1) % 2)

            R = RT_TOK
            dve.sem_inc(top_read, 1)
            dve.wait_ge(sc_taken, RT_TILES * 4)
            n_links = [0]

            def route(it):
                k = 0

                def link(ins):
                    nonlocal k
                    k += 1
                    ins.then_inc(r_step, 1)
                    dve.wait_ge(r_step, it * R_LINKS + k)
                    dve.sem_inc(route_held, 1)

                dve.wait_ge(cur_ready, it + 1)
                dve.sem_inc(route_held, 1)
                for first in range(0, 16, 8):
                    for hp in range(first, first + 8):
                        last = nc.vector.max(s16[0:R, hp, 0:8], cur[0:R, hp, :])
                    yield
                link(last)
                for hp in range(16):
                    nc.vector.max_index(i16[0:R, hp, 0:8], s16[0:R, hp, 0:8], cur[0:R, hp, :])
                    last = nc.vector.match_replace(cur2[0:R, hp, :], s16[0:R, hp, 0:8], cur[0:R, hp, :], LOWEST)
                    if hp % 4 == 3 and hp < 15:
                        yield
                last.then_inc(top_read, 1)
                dve.wait_ge(top_read, it + 2)
                dve.sem_inc(route_held, 1)
                yield
                for hp in range(16):
                    last = nc.vector.max(s16[0:R, hp, 8:16], cur2[0:R, hp, :])
                    if hp == 7:
                        yield
                link(last)
                yield
                for hp in range(16):
                    nc.vector.max_index(i16[0:R, hp, 8:16], s16[0:R, hp, 8:16], cur2[0:R, hp, :])
                    if hp % 8 == 7:
                        yield
                s4 = s16[0:R].rearrange("p (h s) a -> p h s a", s=2)
                link(TT(cand[0:R], s4[:, :, 0, :].unsqueeze(3).broadcast_to((R, HEADS, TOPK, TOPK)),
                        s4[:, :, 1, :].unsqueeze(2).broadcast_to((R, HEADS, TOPK, TOPK)), ADD))
                link(nc.vector.tensor_copy(i16f[0:R], i16[0:R]))
                cf = cand[0:R].rearrange("p h a b -> p h (a b)")
                cf2 = cand2[0:R].rearrange("p h a b -> p h (a b)")
                for h in range(HEADS):
                    last = nc.vector.max(c16[0:R, h, 0:8], cf[:, h, :])
                link(last)
                yield
                for h in range(HEADS):
                    nc.vector.max_index(j16[0:R, h, 0:8], c16[0:R, h, 0:8], cf[:, h, :])
                    last = nc.vector.match_replace(cf2[:, h, :], c16[0:R, h, 0:8], cf[:, h, :], LOWEST)
                    if h == 3:
                        yield
                link(last)
                yield
                for h in range(HEADS):
                    last = nc.vector.max(c16[0:R, h, 8:16], cf2[:, h, :])
                link(last)
                yield
                for h in range(HEADS):
                    last = nc.vector.max_index(j16[0:R, h, 8:16], c16[0:R, h, 8:16], cf2[:, h, :])
                link(last)
                jj = j16[0:R].rearrange("p h k -> p (h k)")
                TS(jab[0:R, 0], jj, 4, None, ALU.logical_shift_right)
                link(TS(jab[0:R, 1], jj, TOPK - 1, None, ALU.bitwise_and))
                link(nc.vector.tensor_copy(jf[0:R], jab[0:R]))
                yield
                i4 = i16f[0:R].rearrange("p (h s) a -> p h s a", s=2)
                for s in range(2):
                    link(TT(eqs[0:R], jf[0:R, s].unsqueeze(2).broadcast_to((R, PAIRS, TOPK)),
                            iota16[0:R].unsqueeze(1).broadcast_to((R, PAIRS, TOPK)), ALU.is_equal))
                    yield
                    e4 = eqs[0:R].rearrange("p (h k) a -> p h k a", h=HEADS)
                    link(TT(e4, e4, i4[:, :, s, :].unsqueeze(2).broadcast_to((R, HEADS, TOPK, TOPK)), MULT))
                    yield
                    link(nc.vector.tensor_reduce(routed[0:R, bass.ds(it, 1), s, :].rearrange("p o k -> p (o k)"),
                                                 eqs[0:R], AX_X, ADD))
                    yield
                link(nc.vector.tensor_copy(routed[0:R, bass.ds(it, 1), 2, :].rearrange("p o k -> p (o k)"),
                                           c16[0:R].rearrange("p h k -> p (h k)")))
                n_links[0] = k
                yield "ended"

            with dve.Fori(0, RT_TILES) as it:
                steps = route(it)
                for u in range(U1_PER):
                    lo_part(it * U1_PER + (B_U + u + 1), (u + 1) % 2)
                    for _ in range(R_STEPS * u // U1_PER, R_STEPS * (u + 1) // U1_PER):
                        got = next(steps, "too many")
                assert got == "ended", got
                assert not list(steps)
                assert n_links[0] == R_LINKS, n_links

            G6 = (R, RT_TILES, HEADS, TOPK)
            sc = routed[0:R, :, 2, :].rearrange("p t (h k) -> p t h k", h=HEADS)
            ge = gexp[0:R].rearrange("p t (h k) -> p t h k", h=HEADS)
            gs = gsum[0:R, 0].rearrange("p (t h) -> p t h", h=HEADS)
            gr = gsum[0:R, 1].rearrange("p (t h) -> p t h", h=HEADS)

            def glink(ins, n):
                ins.then_inc(g_step, 1)
                dve.wait_ge(g_step, n)

            lo_part(B_U + U1_TILES + 1, 1)
            for t in range(RT_TILES):
                last = TT(ge[:, t], sc[:, t], sc[:, t, :, 0:1].broadcast_to((R, HEADS, TOPK)), SUB)
            glink(last, 1)
            dve.wait_ge(g_exped, 1)
            glink(nc.vector.tensor_reduce(gsum[0:R, 0], gexp[0:R].rearrange("p t (h k) -> p (t h) k", k=TOPK),
                                          AX_X, ADD), 2)
            glink(nc.vector.reciprocal(gsum[0:R, 1], gsum[0:R, 0]), 3)
            lo_part(B_U + U1_TILES + 2, 0)
            gk = gexp[0:R].rearrange("p t (h k) -> p (t h) k", k=TOPK)
            glink(TT(gk, gk, gsum[0:R, 1].unsqueeze(2).broadcast_to((R, RT_TILES * HEADS, TOPK)), MULT), 4)
            nc.vector.tensor_copy(g_hi[0:R], gexp[0:R]).then_inc(g_split, 1)
            dve.wait_ge(g_split, 1)
            TT(g_lo[0:R], gexp[0:R], g_hi[0:R].bitcast(F32), SUB).then_inc(g_split, 1)

            dve.sem_inc(hot_ready, 18)
            with dve.Fori(0, U2_ITERS) as it:
                for u in range(U2_PER):
                    for i, q in enumerate(groups_of(u)):
                        if i == 2:
                            lo_part(it * U2_PER + (B_U + B_U2 + u + 1), (u + 1) % 2)
                        nb, qq = q // 9, q % 9
                        if qq == 0:
                            dve.wait_ge(rtb_ready, it * BATCH_PER + (nb + 1))
                        dve.wait_ge(hot_used, it * Q_PER + (q + 1))
                        for t in range(4):
                            r = rt_b[:, nb % 2, :, 4 * qq + t:4 * qq + t + 1]
                            TS(hot_jh[:, q % HR, t, :], iota, r[:, 1], r[:, 2], ALU.is_equal, MULT)
                            last = TS(hot_jl[:, q % HR, t, :], iota, r[:, 1], r[:, 3], ALU.is_equal, MULT)
                        last.then_inc(hot_ready, 1)

            dve.sem_inc(v_lo, 16)

            def product(g8, gg, j, kg, ka):
                if j == 0:
                    dve.wait_ge(g_in_s[gg], kg)
                if j % 4 == 0:
                    dve.wait_ge(act_in_s[j // 4], ka)
                TT(gated[:, j % 2, :].rearrange("p (b t) -> p b t", b=G_BATCH),
                   act_in[:, j // 4, j % 4, :].rearrange("p (b t) -> p b t", b=G_BATCH),
                   g_in[:, gg, :, j, :], MULT).then_inc(v_prod, 1)
                dve.wait_ge(v_hi, g8 + (j + 1))
                TT((m1_lo, m0_lo)[gg][:, j, 0:TQ], gated[:, j % 2, :],
                   (m1_hi, m0_hi)[gg][:, j, 0:TQ].bitcast(F32), SUB).then_inc(v_lo, 1)

            for u in range(U3_TILES):
                lo_part(B_U + B_U3 + u + 1, (u + 1) % 2)
                if u == 6:
                    for s in g_stored:
                        dve.wait_ge(s, 16 * (G_BATCH // 2) + 16)
                if u >= 6:
                    product(0, 0, u - 6, 16, 16)

            def v_steps(g, gg, it, last):
                for c in range(KC):
                    if not (last and c == KC - 1):
                        lo_part(g * KC + (B_V + c + 1), (c + 1) % 2)
                    if not last:
                        nxt = (gg + 1) % 2
                        if c == 0:
                            dve.wait_ge(half_done, g * (2 * KC) + (2 * B_V + 4))
                        product(g * 8 + 8, nxt, c, it * 16 + (16 if nxt else 32), g * 16 + 32)
                    for h in range(2):
                        dve.wait_ge(half_done, g * (2 * KC) + (2 * (B_V + c) + h + 5))
                        dst = xh[:, c, N_META + h * HQ:N_META + (h + 1) * HQ]
                        TT(dst, ps[:, 2 * (c % 2) + h, 0:HQ], dst, ADD).then_inc(free_v, 1)

            with dve.Fori(0, N_GROUP // 2 - 1) as it:
                for gg in range(2):
                    v_steps(it * 2 + gg, gg, it, False)
            v_steps(N_GROUP - 2, 0, N_GROUP // 2 - 1, False)
            v_steps(N_GROUP - 1, 1, N_GROUP // 2 - 1, True)
            norm("nf", lambda c: xh[:, c, N_META:T], lambda c: gn[:, G_FINAL + c:G_FINAL + c + 1], TQ, False, None,
                 None, out=y_st)


R_LINKS = 17
R_STEPS = 22


def constants():
    k, m = np.arange(P)[:, None], np.arange(P)[None, :]
    c = np.zeros((P, C_W), np.float32)
    c[:, C_ID:C_ID + P] = k == m
    c[:, C_TRI:C_TRI + P] = k >= m
    c[:, C_ONE:C_ONE + P] = 1
    c[:, C_BD:C_BD + P] = k // HD == m // HD
    half = HD // 8
    d = np.arange(P)
    for j in range(P):
        if d[j] % HD < half:
            c[j + half, C_ROT + j] = -1
        elif d[j] % HD < 2 * half:
            c[j - half, C_ROT + j] = 1
    c[:, C_MASK:C_MASK + P] = k < m
    c[:, C_NEG:C_NEG + P] = np.where(k < m, 0, NEG)
    c[:, C_IOTA:C_IOTA + P] = m
    c[:, C_IOTA16:C_IOTA16 + TOPK] = np.arange(TOPK)
    c[:, C_EPS] = EPS
    inv = (np.float32(500000.0) ** (-np.arange(half, dtype=np.float32) * np.float32(2.0) / np.float32(2 * half)))
    ang = np.arange(T, dtype=np.float32)[None, :] * inv.astype(np.float32)[:, None]
    tab = np.zeros((P, 2, T), np.float32)
    tab[:, 0] = 1
    for j in range(P):
        if d[j] % HD < 2 * half:
            tab[j, 0] = np.cos(ang[d[j] % half])
            tab[j, 1] = np.sin(ang[d[j] % half])
    return c, tab


def kernel(x_prompt, x_sample, cache_a_k, cache_a_v, cache_b_k, cache_b_v, meta_tokens, g_attn, w_qkv,
           diff_lambda, a_norm_g, b_norm_g, w_o, g_ffn, w_peer_q, peer_sub_keys, peer_u, peer_v, g_final):
    import concourse.bacc as bacc
    from concourse.bass_utils import run_bass_kernel_spmd

    consts, tab = constants()
    x = np.concatenate([meta_tokens, x_prompt[0], x_sample[0]], axis=0)
    x_t = x.T.reshape(KC, P, T).transpose(1, 0, 2)
    col = lambda g: np.asarray(g).reshape(-1, P).T
    gains = np.concatenate([col(g_attn[0]), col(g_ffn[0]), col(g_final), col(a_norm_g[0]),
                            np.concatenate([b_norm_g[0], b_norm_g[0]]).reshape(P, 1)], axis=1)

    def k_t(c):
        return np.asarray(c).reshape(KP, 4, P).transpose(2, 1, 0)

    cache_k = np.concatenate([k_t(cache_a_k[0, 0]), k_t(cache_b_k[0, 0])], axis=1)
    va, vb = np.asarray(cache_a_v)[0, 0].reshape(KP, 512), np.asarray(cache_b_v)[0, 0].reshape(KP, 512)
    v = np.concatenate([va, vb], axis=1)
    cache_v = v[:512].reshape(4, P, 1024).transpose(1, 0, 2)
    cache_vt = v[512:].T.reshape(8, P, N_META).transpose(1, 0, 2)

    def w_t(w):
        w = np.asarray(w)
        return w.reshape(KC, P, w.shape[1] // P, P).transpose(2, 1, 0, 3).reshape(-1, KC * P)

    u_t = np.asarray(peer_u)[0].reshape(P, P, KC, P).transpose(1, 3, 2, 0).reshape(-1, KC * P)
    v_t = np.asarray(peer_v)[0].reshape(P, N_GROUP, 8, KC, P).transpose(1, 3, 0, 2, 4).reshape(-1, KC * P)
    w_tiles = np.concatenate([w_t(w_qkv[0]), w_t(w_o[0]), w_t(w_peer_q[0]), u_t, v_t], axis=0)
    sub_keys = np.asarray(peer_sub_keys)[0].transpose(2, 0, 1)

    nc = bacc.Bacc("TRN2", target_bir_lowering=False, num_devices=1)
    arrays, args = {}, []
    for name, a in (("x_t", x_t), ("consts", consts), ("tables", tab), ("gains", gains),
                    ("lam_p", np.asarray(diff_lambda)[0].reshape(256)), ("cache_k", cache_k), ("cache_v", cache_v),
                    ("cache_vt", cache_vt), ("w_tiles", w_tiles), ("sub_keys", sub_keys)):
        arrays[name] = np.ascontiguousarray(a)
        args.append(nc.dram_tensor(name, a.shape, F32, kind="ExternalInput").ap())
    args.append(nc.dram_tensor("y_t", (KC, P, TQ), F32, kind="ExternalOutput").ap())
    args.append(nc.dram_tensor("kv_t", (4, P, 4, T), F32, kind="ExternalOutput").ap())
    bass_hybrid_step(nc, *args)
    out = run_bass_kernel_spmd(nc, [arrays], core_ids=[0]).results[0]

    y = out["y_t"].reshape(D, TQ).T
    a_k, a_v, b_k, b_v = out["kv_t"].transpose(0, 3, 2, 1).reshape(4, T, 512)
    a_shape, b_shape = (1, 1, -1, AH, 2 * HD), (1, 1, -1, BH, HD)
    parts = [(a_k, a_shape), (a_v, a_shape), (b_k, b_shape), (b_v, b_shape)]
    return ((np.ascontiguousarray(y[None, :SEQ]), np.ascontiguousarray(y[None, SEQ:]))
            + tuple(np.ascontiguousarray(a[:KP].reshape(s)) for a, s in parts)
            + tuple(np.ascontiguousarray(a[KP:].reshape(s)) for a, s in parts))
```

```python
from contextlib import ExitStack

import numpy as np

import concourse.bass as bass
from concourse import mybir

F32 = mybir.dt.float32
F32R = mybir.dt.float32r
U32 = mybir.dt.uint32
ALU = mybir.AluOpType
ACT = mybir.ActivationFunctionType
AX_X = mybir.AxisListType.X

P = 128
D = 1024
KC = D // P
N_META, SEQ, DEC, PAST = 16, 512, 64, 512
HD = 64
AH, BH = 4, 8
KP = N_META + SEQ
T = KP + DEC
TQ = SEQ + DEC
HQ = TQ // 2
HT = T // 2
CHUNK = 64
EPS = 1e-6
LAM_INIT = 0.2
SCALE = HD ** -0.5
NEG = -1e30
LOWEST = -3.0e38

N_QKV, N_WO, N_PQ = 24, 8, 16
B_WO = N_QKV
B_PQ = B_WO + N_WO
B_U = B_PQ + N_PQ
N_EXP_J = 128
B_V = B_U + N_EXP_J
N_GROUP = 16
NT_ALL = B_V + N_GROUP * KC

RT_TILES, RT_TOK, U1_PER = 6, 96, 12
U1_TILES = RT_TILES * U1_PER
G_BATCH, G_TOK = 16, 36
MID_TILES = 2
B_U2 = U1_TILES + MID_TILES
U2_ITERS, U2_PER = 4, 10
B_U3 = B_U2 + U2_ITERS * U2_PER
U3_TILES = N_EXP_J - B_U3
BATCH_PER = G_BATCH // U2_ITERS
Q_PER = BATCH_PER * (G_TOK // 4)
GR = 4
HR = 6
HOT_AHEAD = 4
HEADS, TOPK = 8, 16
PAIRS = HEADS * TOPK
assert U3_TILES == 14 and Q_PER % GR == 0 and BATCH_PER % 2 == 0 and Q_PER % HR == 0 and RT_TILES * RT_TOK == TQ == G_BATCH * G_TOK

C_ID, C_TRI, C_ONE, C_BD, C_ROT, C_MASK, C_NEG, C_IOTA = (P * n for n in range(8))
C_IOTA16 = 8 * P
C_EPS = C_IOTA16 + TOPK
C_W = C_EPS + 1
G_ATTN, G_FFN, G_FINAL, G_A, G_B = 0, 8, 16, 24, 25
G_W = 26

PK = [0, 1, 2, 3, 4]
K_ROWS = [128, 128, 128, 128, 80]
Q_FROM = [0, 112, 240, 368, 496]
P_OFF = [0, 512, 912, 1184, 1584]
S_OFF = [1328, 1392, 1456, 1520, 1600]
B_COLS = 1664
UNITS = [
    (1328, [(128, 0, 256), (80, 256, 80)]),
    (912, [(128, 0, 416)]),
    (512, [(128, 0, 400)]),
    (0, [(128, 0, 512)]),
]
B_LAG = 4
NA = 5 * AH
A_SHAPE = [(P, i + 1, 16) for i in range(4)] + [(64, 4, 80)]
GROUPS = [
    [("s", kt, S_OFF[kt] - 1328, 64) for kt in range(4)] + [("p", 4, 256, 16), ("s", 4, 272, 64)],
    [("p", 3, 272, 144), ("p", 2, 0, 272)],
    [("p", 1, 0, 400)],
    [("p", 0, 0, 512)],
]


def bass_hybrid_step(nc, x_t, consts, tables, gains, lam_p, cache_k, cache_v, cache_vt, w_tiles, sub_keys,
                     y_out, kv_out):
    g_dram = nc.dram_tensor("gates_scattered", (G_BATCH * P, P * G_TOK), F32).ap()
    act_dram = nc.dram_tensor("activated", (N_EXP_J * P, TQ), F32).ap()

    with ExitStack() as ctx:
        base = [16512]

        def at(name, shape, dt, off):
            return nc.alloc_sbuf_tensor_at(name, shape, dt, offset=off)

        def fixed(name, shape, dt=F32):
            n = 4 * int(np.prod(shape[1:]))
            n = (n + 31) // 32 * 32
            off = base[0]
            base[0] += n
            return at(name, shape, dt, off)

        def sem(name):
            return ctx.enter_context(nc.semaphore(name))

        xh = fixed("xh", [P, KC, T])
        cst = fixed("cst", [P, C_W])
        gn = fixed("gn", [P, G_W])
        lam = fixed("lam", [P, 8])
        stat = fixed("stat", [P, 16])
        raw = fixed("raw", [P, 2, KC, P])
        w_hi = fixed("w_hi", [P, 2, KC, P], F32R)
        w_lo = fixed("w_lo", [P, 2, KC, P], F32R)
        m0_off = base[0]
        m0_hi = fixed("m0_hi", [P, KC, T], F32R)
        m0_lo = fixed("m0_lo", [P, KC, T], F32R)
        region = base[0]
        assert region <= 229344 - 121472

        off = region
        qkv = at("qkv", [P, 24, T], F32, off)
        off += 24 * T * 4
        v_nat = at("v_nat", [P, 5, 1024], F32, off)
        off += 5 * 4096
        vs4 = at("vs4", [P, 1024], F32, off)
        off += 4096
        v_cache = at("v_cache", [P, 4, 1024], F32, off)
        norm_off = off
        off += 4 * 4096
        k_cache = at("k_cache", [P, 8, T], F32, off)
        off += 8 * T * 4
        tab = at("tab", [P, 2, T], F32, off)
        off += 2 * T * 4
        assert off <= 229344
        nsq = at("nsq", [P, 2, T], F32, norm_off)
        nrs = at("nrs", [P, 2, T], F32, norm_off + 2 * T * 4)
        ntmp = at("ntmp", [P, 2, T], F32, norm_off + 4 * T * 4)
        off = m0_off
        log_hi = at("log_hi", [P, 2, B_COLS], F32R, off)
        off += 2 * B_COLS * 4
        log_lo = at("log_lo", [P, 2, B_COLS], F32R, off)
        off += 2 * B_COLS * 4
        t_abs = at("t_abs", [P, 3, 512], F32, off)
        off += 6144
        t_pos = at("t_pos", [P, 2, 512], F32, off)
        off += 4096
        assert off <= region
        prob = at("prob", [P, 3, 512], F32, region + 8 * T * 4)
        cst_r = [at(f"cst_r{k}", [P, P], F32R, region + 8 * T * 4 + 6144 + 512 * k) for k in range(4)]
        ones_r, tri_r, ident_r, negm_r = cst_r
        rtmp = at("rtmp", [P, 2, T], F32, m0_off)
        lam_in = at("lam_in", [P, 256], F32, m0_off + 8 * T)
        vs_t = at("vs_t", [P, 8, 80], F32, m0_off + 8 * T + 2048)
        p_a = at("p_a", [P, 4, T], F32, m0_off)
        w_a = at("w_a", [P, 2, T], F32, m0_off + 16 * T)
        wt_a = at("wt_a", [P, 2, 5, P], F32, m0_off + 24 * T)

        off = region
        q_t = at("q_t", [P, 16, TQ], F32, off)
        cand = at("cand", [P, HEADS, TOPK, TOPK], F32, off)
        cand2 = at("cand2", [P, HEADS, TOPK, TOPK], F32, off + 8192)
        eqs = at("eqs", [P, PAIRS, TOPK], F32, off + 16384)
        cur2 = at("cur2", [P, 16, P], F32, off + 24576)
        small = off + 32768
        s16 = at("s16", [P, 16, TOPK], F32, small)
        c16 = at("c16", [P, HEADS, TOPK], F32, small + 1024)
        i16f = at("i16f", [P, 16, TOPK], F32, small + 1536)
        jf = at("jf", [P, 2, PAIRS], F32, small + 2560)
        g_st = at("g_st", [P, 2, P, G_TOK], F32, off)
        off += 16 * TQ * 4
        score = at("score", [P, RT_TILES, 16, P], F32, off)
        off += RT_TILES * 8192
        cur = at("cur", [P, 16, P], F32, off)
        off += 8192
        i16 = at("i16", [P, 16, TOPK], U32, off)
        off += 1024
        j16 = at("j16", [P, HEADS, TOPK], U32, off)
        off += 512
        jab = at("jab", [P, 2, PAIRS], U32, off)
        off += 1024
        act_st = at("act_st", [P, 2, TQ], F32, off)
        off += 2 * TQ * 4
        subk = at("subk", [P, 2, P], F32, off)
        off += 1024
        eq_j = at("eq_j", [P, 3, 4, P], F32, off)
        routed = at("routed", [P, RT_TILES, 3, PAIRS], F32, off)
        off += RT_TILES * 3 * PAIRS * 4
        rt_t = at("rt_t", [P, 4, TQ], F32, region + 16 * TQ * 4)
        g_hi = at("g_hi", [P, RT_TILES, PAIRS], F32R, region + 16 * TQ * 4 + 9216)
        g_lo = at("g_lo", [P, RT_TILES, PAIRS], F32R, region + 16 * TQ * 4 + 9216 + 3072)
        gexp = at("gexp", [P, RT_TILES, PAIRS], F32, region + 16 * TQ * 4 + 9216 + 6144)
        gsum = at("gsum", [P, 2, RT_TILES * HEADS], F32, region + 16 * TQ * 4 + 9216 + 9216)
        hot_off = region + 16 * TQ * 4 + 9216
        hot_i = at("hot_i", [P, HR, 4, P], F32R, hot_off)
        hot_j = at("hot_j", [P, HR, 2, 4, P], F32R, hot_off + HR * 2048)
        rt_b = at("rt_b", [P, 2, 4, G_TOK], F32, hot_off + 3 * HR * 2048)
        assert off <= 229344

        off = region
        m1_hi = at("m1_hi", [P, KC, TQ], F32R, off)
        off += KC * TQ * 4
        m1_lo = at("m1_lo", [P, KC, TQ], F32R, off)
        off += KC * TQ * 4
        g_in = at("g_in", [P, 2, G_BATCH, KC, G_TOK], F32, off)
        off += 2 * KC * TQ * 4
        act_in = at("act_in", [P, 2, 4, TQ], F32, off)
        off += 2 * 4 * TQ * 4
        gated = at("gated", [P, 2, TQ], F32, off)
        off += 2 * TQ * 4
        assert off <= 229344
        y_st = at("y_st", [P, KC, TQ], F32, region)

        ps = ctx.enter_context(nc.psum_tensor("ps", [P, 8, 512], F32))
        psf = ps[:].rearrange("p b n -> p (b n)")

        ident, tri = cst[:, C_ID:C_ID + P], cst[:, C_TRI:C_TRI + P]
        ones, blocks = cst[:, C_ONE:C_ONE + P], cst[:, C_BD:C_BD + P]
        rot, mask = cst[:, C_ROT:C_ROT + P], cst[:, C_MASK:C_MASK + P]
        negm, iota = cst[:, C_NEG:C_NEG + P], cst[:, C_IOTA:C_IOTA + P]
        iota16, eps = cst[:, C_IOTA16:C_IOTA16 + TOPK], cst[:, C_EPS:C_EPS + 1]

        consts_in, x_in = sem("consts_in"), sem("x_in")
        tables_in, caches_in = sem("tables_in"), sem("caches_in")
        raw_in = [sem("raw_in0"), sem("raw_in1")]
        hi_ready = sem("hi_ready")
        w_split = sem("w_split")
        half_done = sem("half_done")
        free_qkv, free_wo, free_pq = sem("free_qkv"), sem("free_wo"), sem("free_pq")
        free_u, free_v = sem("free_u"), sem("free_v")
        norm_sems = {n: {k: sem(f"{n}_{k}") for k in ("sq", "sum", "std", "rs", "x", "hi", "lo")}
                     for n in ("n1", "nm", "n2", "nf")}
        vt_done, vt_taken = sem("vt_done"), sem("vt_taken")
        rot_done, rope_step, rope_done = sem("rot_done"), sem("rope_step"), sem("rope_done")
        prep_done, lam_step, lam_exp = sem("prep_done"), sem("lam_step"), sem("lam_exp")
        ks_ready = sem("ks_ready")
        b_z, b_abs, b_exp, b_ln, b_log = sem("b_z"), sem("b_abs"), sem("b_exp"), sem("b_ln"), sem("b_log")
        b_raw, b_pos, b_hi, b_lo, b_consts = sem("b_raw"), sem("b_pos"), sem("b_hi"), sem("b_lo"), sem("b_consts")
        b_cum, b_prob, b_av, b_out = sem("b_cum"), sem("b_prob"), sem("b_av"), sem("b_out")
        a_s, a_max, a_neg, a_prob = sem("a_s"), sem("a_max"), sem("a_neg"), sem("a_prob")
        a_step, a_w, a_t, a_wt, a_o, a_out = (sem("a_step"), sem("a_w"), sem("a_t"), sem("a_wt"), sem("a_o"),
                                              sem("a_out"))
        kv_stored, ak_stored = sem("kv_stored"), sem("ak_stored")
        subk_in, sc_done, sc_taken = sem("subk_in"), sem("sc_done"), sem("sc_taken")
        cur_ready, top_read, r_step, routed_s = sem("cur_ready"), sem("top_read"), sem("r_step"), sem("routed_s")
        route_held = sem("route_held")
        g_step, g_exped, g_split = sem("g_step"), sem("g_exped"), sem("g_split")
        rt_done, rt_taken = sem("rt_done"), sem("rt_taken")
        act_stored = [sem("act_stored0"), sem("act_stored1")]
        rtb_ready = sem("rtb_ready")
        hot_ready, hot_used, gm_taken = sem("hot_ready"), sem("hot_used"), sem("gm_taken")
        hot_j_ready, hot_held = sem("hot_j_ready"), sem("hot_held")
        g_stored = [sem("g_stored0"), sem("g_stored1")]
        g_in_s = [sem("g_in0"), sem("g_in1")]
        act_in_s = [sem("act_in0"), sem("act_in1")]
        v_prod, v_hi, v_lo = sem("v_prod"), sem("v_hi"), sem("v_lo")
        y_stored = sem("y_stored")

        block = ctx.enter_context(nc.Block())

        MULT, ADD, SUB = ALU.mult, ALU.add, ALU.subtract

        def merged(c):
            return qkv[:, 8 + c if c < 4 else 16 + c, N_META:T]

        def groups_at(u, m):
            at_m = 48 * u + m + 1
            return [q for q in range(Q_PER) if (q + 1) * 48 * U2_PER // Q_PER == at_m]

        def before_half(u, h):
            late = groups_at(u, 23) if h else groups_at(u - 1, 47) if u else []
            return late + [q for m in range(24 * h, 24 * h + 23) for q in groups_at(u, m)]

        def groups_of(u, half=None):
            return [q for m in range(48) if half is None or m // 24 == half for q in groups_at(u, m)]

        @block.sync
        def _(sp):
            sp.sem_inc(w_split, 2)
            for s in (free_qkv, free_wo, free_pq, free_u, free_v):
                sp.sem_inc(s, 4)
            sp.dma_start(cst[:], consts).then_inc(consts_in, 16)
            sp.dma_start(gn[:], gains).then_inc(consts_in, 16)
            sp.dma_start(xh[:], x_t).then_inc(x_in, 16)

            def load_tile(n, slot):
                sp.wait_ge(w_split, n + 1)
                sp.dma_start(raw[:, slot], w_tiles[bass.ds(n * P, P), :]).then_inc(raw_in[slot], 16)

            with sp.Fori(0, B_U // 8) as it:
                for u in range(8):
                    load_tile(it * 8 + u, u % 2)
            for n in range(B_U, B_U + 3):
                load_tile(n, n % 2)

            def load_group(g, gg):
                for s in act_stored:
                    sp.wait_ge(s, g * 64 + 80)
                sp.wait_ge(v_lo, g * 8 + 8)
                sp.dma_start(g_in[:, gg].rearrange("p b j t -> p b (j t)"),
                             g_dram[:, bass.ds(g * (KC * G_TOK), KC * G_TOK)].rearrange(
                                 "(b p) n -> p b n", p=P)).then_inc(g_in_s[gg], 16)
                for hh in range(2):
                    sp.wait_ge(v_lo, g * 8 + 4 * hh + 12)
                    sp.dma_start(act_in[:, hh],
                                 act_dram[bass.ds(g * (8 * P) + hh * 4 * P, 4 * P), :].rearrange(
                                     "(j p) t -> p j t", p=P)).then_inc(act_in_s[hh], 16)

            def load_vs(g, tiles):
                for c in range(tiles):
                    load_tile(g * KC + (B_V + c + 2), c % 2)

            for s in act_stored + g_stored:
                sp.sem_inc(s, 16)

            def store_act(n, slot):
                sp.wait_ge(free_u, n * 2 + 6)
                sp.dma_start(act_dram[bass.ds(n * P, P), :], act_st[:, slot]).then_inc(act_stored[slot], 16)

            with sp.Fori(0, B_U2 // 2) as it:
                for u in range(2):
                    load_tile(it * 2 + (B_U + 3 + u), (u + 1) % 2)
                    store_act(it * 2 + u, u)
            with sp.Fori(0, U2_ITERS) as it:
                for u in range(U2_PER):
                    load_tile(it * U2_PER + (B_U + B_U2 + 3 + u), (u + 1) % 2)
                    store_act(it * U2_PER + (B_U2 + u), u % 2)
                    for nb in range(BATCH_PER):
                        if 9 * nb + 8 in groups_of(u):
                            sp.wait_ge(gm_taken, it * Q_PER + (9 * (nb + 1) + GR))
                            sp.dma_start(g_dram[bass.ds((it * BATCH_PER + nb) * P, P), :],
                                         g_st[:, nb % 2].rearrange("p j t -> p (j t)")).then_inc(g_stored[nb % 2], 16)
            for m in range(B_U3, N_EXP_J):
                n = B_U + 3 + m
                if n < B_V + 2:
                    load_tile(n, n % 2)
                store_act(m, m % 2)
                if n == B_U + B_U3 + 4:
                    for s in g_stored:
                        sp.wait_ge(s, 16 * (G_BATCH // 2) + 16)
                    load_group(0, 0)
            with sp.Fori(0, N_GROUP // 2 - 1) as it:
                for gg in range(2):
                    load_group(it * 2 + (gg + 1), 1 - gg)
                    load_vs(it * 2 + gg, KC)
            load_group(N_GROUP - 1, 1)
            load_vs(N_GROUP - 2, KC)
            load_vs(N_GROUP - 1, KC - 2)
            for c in range(KC):
                sp.wait_ge(norm_sems["nf"]["x"], c + 1)
                sp.dma_start(y_out[c], y_st[:, c]).then_inc(y_stored, 16)
            sp.wait_ge(y_stored, 16 * KC)

        @block.gpsimd
        def _(pool):
            pool.dma_start(tab[:], tables).then_inc(tables_in, 16)
            pool.dma_start(k_cache[:, :, 0:KP], cache_k).then_inc(caches_in, 16)
            pool.wait_ge(norm_sems["n1"]["lo"], KC)
            pool.dma_start(v_cache[:], cache_v).then_inc(caches_in, 16)
            pool.wait_ge(free_qkv, 4 + 2 * N_QKV)
            pool.dma_start(lam_in[:], lam_p.partition_broadcast(P)).then_inc(caches_in, 16)
            pool.dma_start(vs_t[:, :, 0:N_META], cache_vt).then_inc(caches_in, 16)
            bq = qkv[:, 12:16, :].rearrange("p c t -> p (c t)")
            nc.gpsimd.tensor_scalar(bq, bq, SCALE, 1.0, MULT, MULT).then_inc(prep_done, 1)
            nc.gpsimd.tensor_copy(k_cache[:, 4:8, KP:T], qkv[:, 16:20, KP:T]).then_inc(prep_done, 1)
            nc.gpsimd.tensor_copy(vs_t[:, 0:4, N_META:80], qkv[:, 8:12, KP:T]).then_inc(prep_done, 1)
            nc.gpsimd.tensor_copy(vs_t[:, 4:8, N_META:80], qkv[:, 20:24, KP:T]).then_inc(prep_done, 1)
            for k, c0 in ((1, 8), (2, 16), (3, 20)):
                pool.dma_start(kv_out[k], qkv[:, c0:c0 + 4, :]).then_inc(kv_stored, 16)
            pool.wait_ge(rope_done, 8)
            nc.gpsimd.tensor_copy(k_cache[:, 0:4, KP:T], qkv[:, 4:8, KP:T]).then_inc(ks_ready, 1)
            pool.dma_start(kv_out[0], qkv[:, 4:8, :]).then_inc(ak_stored, 16)
            pool.wait_ge(kv_stored, 48)
            pool.wait_ge(ak_stored, 16)
            pool.wait_ge(a_out, 5 * AH)
            pool.dma_start(subk[:], sub_keys).then_inc(subk_in, 16)
            pool.wait_ge(rt_taken, RT_TILES)
            pool.sem_inc(hot_j_ready, 18)
            with pool.Fori(0, U2_ITERS) as it:
                for q in range(Q_PER):
                    nb, qq = q // 9, q % 9
                    pool.wait_ge(hot_ready, it * Q_PER + (q + 19))
                    pool.sem_inc(hot_held, 1)
                    pool.wait_ge(hot_used, it * Q_PER + (q + 1))
                    nc.gpsimd.tensor_tensor(
                        hot_j[:, q % HR], eq_j[:, q % 3].unsqueeze(1).broadcast_to((P, 2, 4, P)),
                        rt_b[:, nb % 2, 2:4, 4 * qq:4 * qq + 4].unsqueeze(3).broadcast_to((P, 2, 4, P)),
                        MULT).then_inc(hot_j_ready, 1)

        @block.tensor
        def _(pe):
            pe.sem_inc(half_done, 4)

            def tile(n, slot, k, free, hi, lo, col, width, after=None):
                pe.wait_ge(w_split, n + 3)
                for h in range(2):
                    pe.wait_ge(free, k * 2 + h + 1)
                    c0 = col + h * width
                    m = 0
                    for kc in range(KC):
                        for w, x in ((w_hi, hi), (w_hi, lo), (w_lo, hi)):
                            mm = nc.tensor.matmul(ps[:, 2 * slot + h, 0:width], w[:, slot, kc, :],
                                                  x[:, kc, c0:c0 + width], start=(m == 0), stop=(m == 23))
                            m += 1
                            if m == 24:
                                mm.then_inc(half_done, 1)
                            if after is not None:
                                after(24 * h + m - 1)

            def norm_sum(name, weights, halves, step):
                s = norm_sems[name]
                for c in range(KC):
                    pe.wait_ge(s["sq"], c + 1)
                    if step and c >= 2:
                        pe.wait_ge(s["std"], 2 * (c - 1))
                    for h in range(2):
                        mm = nc.tensor.matmul(ps[:, (2 * (c % 2) if step else 0) + h, 0:halves],
                                              weights(c), nsq[:, c % 2, h * halves:(h + 1) * halves],
                                              start=(step or c == 0), stop=(step or c == KC - 1),
                                              skip_group_check=not step)
                    mm.then_inc(s["sum"], 1)

            pe.wait_ge(consts_in, 32)
            norm_sum("n1", lambda c: ones, HT, False)
            pe.wait_ge(norm_sems["n1"]["lo"], KC)
            with pe.Fori(0, N_QKV // 4) as it:
                for u in range(4):
                    n = it * 4 + u
                    tile(n, u % 2, n, free_qkv, m0_hi, m0_lo, 0, HT)
            pe.wait_ge(free_qkv, 4 + 2 * N_QKV)
            pe.wait_ge(prep_done, 4)
            pe.wait_ge(caches_in, 64)
            for i in range(12):
                kt, s = i // 2, i % 2
                if i >= 4:
                    pe.wait_ge(vt_taken, i - 3)
                for c in range(4):
                    if kt < 5:
                        src = qkv[:, (8, 20)[s] + c, kt * P:min(T, kt * P + P)]
                    else:
                        src = vs_t[:, 4 * s + c, :]
                    rows = 128 if kt < 4 else 80
                    mm = nc.tensor.transpose(ps[0:rows, i % 4, c * P:(c + 1) * P], src, ident)
                mm.then_inc(vt_done, 1)
            for c in range(8):
                if c >= 2:
                    pe.wait_ge(rope_done, c - 1)
                b = 4 + 2 * (c % 2)
                nc.tensor.matmul(ps[:, b, 0:512], rot, qkv[:, c, 0:512], start=True, stop=True)
                nc.tensor.matmul(ps[:, b + 1, 0:T - 512], rot, qkv[:, c, 512:T],
                                 start=True, stop=True).then_inc(rot_done, 1)

            pe.wait_ge(vt_taken, 12)
            pe.wait_ge(rope_done, 8)

            def qk(h, kind, kt, dst, start):
                r, c = 64 * (h % 2), h // 2
                rows = K_ROWS[kt]
                if kind == "p":
                    k = qkv[r:r + 64, 16 + c, kt * P:kt * P + rows]
                    q = qkv[r:r + 64, 12 + c, N_META + Q_FROM[kt]:KP]
                else:
                    k = k_cache[r:r + 64, 4 + c, kt * P:kt * P + rows]
                    q = qkv[r:r + 64, 12 + c, KP:T]
                return nc.tensor.matmul(dst, k, q, start=start, stop=True, skip_group_check=True)

            def b_sums(idx):
                h, u = idx // 4, idx % 4
                pe.wait_ge(b_lo, idx + 1)
                hp = h % 2

                def add(lhs, rhs, rows, o, n):
                    return nc.tensor.matmul(ps[0:rows, idx % 6, o:o + n], lhs, rhs, start=False, stop=True,
                                            skip_group_check=True)

                if u == 0:
                    for lg in (log_hi, log_lo):
                        for k2 in range(4, 0, -1):
                            r2 = K_ROWS[k2]
                            rhs = lg[0:r2, hp, S_OFF[k2]:S_OFF[k2] + 64].unsqueeze(1).broadcast_to((r2, k2, 64))
                            add(ones_r[0:r2, :], rhs, P, 0, 64 * k2)
                        add(tri_r[:], lg[:, hp, S_OFF[0]:S_OFF[0] + 256], P, 0, 256)
                        add(tri_r[0:80, 0:80], lg[0:80, hp, P_OFF[4]:P_OFF[4] + 80], 80, 256, 80)
                    mm = add(ident_r[0:80, 0:80], negm_r[0:80, 0:80], 80, 256, 80)
                else:
                    for _, kt, o, n in GROUPS[u]:
                        for lg in (log_hi, log_lo):
                            for k2 in range(4, kt, -1):
                                c, r2 = Q_FROM[k2] - Q_FROM[kt], K_ROWS[k2]
                                add(ones_r[0:r2, :], lg[0:r2, hp, P_OFF[k2]:P_OFF[k2] + n - c], P, o + c, n - c)
                            add(tri_r[:], lg[:, hp, P_OFF[kt]:P_OFF[kt] + n], P, o, n)
                        nm, m0 = (P - 16, 16) if kt == 0 else (P, 0)
                        mm = add(ident_r[:], negm_r[:, m0:m0 + nm], P, o, nm)
                mm.then_inc(b_cum, 1)

            def b_values(idx):
                h, u = idx // 4, idx % 4
                r = 64 * (h % 2)
                pe.wait_ge(b_prob, idx + 1)
                if u == 0 and h >= 1:
                    pe.wait_ge(b_out, h)
                vc = 512 + 64 * h
                for kind, kt, o, n in GROUPS[u]:
                    rows = K_ROWS[kt]
                    if kind == "s":
                        v = v_cache[:, kt, vc:vc + 64] if kt < 4 else vs4[0:80, vc:vc + 64]
                        dst, start = ps[r:r + 64, 7, 0:64], kt == 0
                    else:
                        v = v_nat[0:rows, kt, vc:vc + 64]
                        dst, start = ps[r:r + 64, 6, Q_FROM[kt]:512], kt == 4
                    mm = nc.tensor.matmul(dst, v, prob[0:rows, idx % 3, o:o + n], start=start, stop=True,
                                          skip_group_check=True)
                mm.then_inc(b_av, 1)

            pe.wait_ge(b_consts, 1)
            for s in range(4 * BH + B_LAG + 2):
                if s < 4 * BH:
                    if s >= 6:
                        pe.wait_ge(b_prob, s - 5)
                    for k, (kind, kt, o, n) in enumerate(GROUPS[s % 4]):
                        mm = qk(s // 4, kind, kt, ps[0:K_ROWS[kt], s % 6, o:o + n], k == 0)
                    mm.then_inc(b_z, 1)
                if 0 <= s - B_LAG < 4 * BH:
                    b_sums(s - B_LAG)
                if s > B_LAG + 1:
                    b_values(s - B_LAG - 2)

            pe.wait_ge(b_out, BH)
            pe.wait_ge(ks_ready, 1)

            def a_scores(idx):
                h, i = idx // 5, idx % 5
                for m in range(2):
                    if idx >= 1:
                        pe.wait_ge(a_prob, 2 * idx - 1 + m)
                    r = slice(64 * m, 64 * m + 64)
                    if i < 4:
                        q = qkv[r, h, N_META + P * i:N_META + P * (i + 1)]
                        w, keys, rows = 144 + P * i, qkv[r, 4 + h, :], P
                    else:
                        q, w, keys, rows = qkv[r, h, KP:T], T, k_cache[r, h, :], 64
                    for b0 in range(0, w, 512):
                        n = min(512, w - b0)
                        mm = nc.tensor.matmul(ps[0:rows, 2 * m + b0 // 512, 0:n], q, keys[:, b0:b0 + n],
                                              start=True, stop=True)
                    mm.then_inc(a_s, 1)

            def a_transpose(idx):
                i = idx % 5
                rows, full, part = A_SHAPE[i]
                pe.wait_ge(a_w, idx + 1)
                if idx >= 1:
                    pe.wait_ge(a_wt, idx)
                for kt in range(full):
                    nc.tensor.transpose(ps[:, 4, kt * rows:(kt + 1) * rows], w_a[0:rows, idx % 2, kt * P:(kt + 1) * P],
                                        ident[0:rows, 0:rows])
                nc.tensor.transpose(ps[0:part, 5, 0:rows], w_a[0:rows, idx % 2, full * P:full * P + part],
                                    ident[0:rows, 0:rows]).then_inc(a_t, 1)

            def a_values(idx):
                h, i = idx // 5, idx % 5
                rows, full, part = A_SHAPE[i]
                pe.wait_ge(a_wt, idx + 1)
                if idx >= 2:
                    pe.wait_ge(a_out, idx - 1)
                for kt in range(full + 1):
                    r = P if kt < full else part
                    if i < 4:
                        v = v_nat[0:r, kt, h * P:(h + 1) * P]
                    else:
                        v = v_cache[:, kt, h * P:(h + 1) * P] if kt < 4 else vs4[0:80, h * P:(h + 1) * P]
                    wt = wt_a[0:r, idx % 2, kt, 0:rows]
                    mm = nc.tensor.matmul(ps[:, 6 + idx % 2, 0:rows], v, wt, start=(kt == 0), stop=(kt == full))
                mm.then_inc(a_o, 1)

            a_scores(0)
            for idx in range(NA + 1):
                if idx + 1 < NA:
                    a_scores(idx + 1)
                if idx >= 1:
                    a_values(idx - 1)
                if idx < NA:
                    a_transpose(idx)

            norm_sum("nm", lambda c: ones if c < 4 else blocks, HQ, True)
            pe.wait_ge(norm_sems["nm"]["lo"], KC)
            for u in range(N_WO):
                tile(B_WO + u, u % 2, u, free_wo, m0_hi, m0_lo, 0, HQ)

            pe.wait_ge(free_wo, 4 + 2 * N_WO)
            norm_sum("n2", lambda c: ones, HQ, False)
            pe.wait_ge(norm_sems["n2"]["lo"], KC)
            with pe.Fori(0, N_PQ // 4) as it:
                for u in range(4):
                    tile(it * 4 + (B_PQ + u), u % 2, it * 4 + u, free_pq, m0_hi, m0_lo, 0, HQ)
            pe.wait_ge(free_pq, 4 + 2 * N_PQ)
            pe.wait_ge(subk_in, 16)
            for i in range(RT_TILES * 4):
                t, b = i // 4, i % 4
                if i >= 4:
                    pe.wait_ge(sc_taken, i - 3)
                for j in range(4):
                    hp = 4 * b + j
                    mm = nc.tensor.matmul(ps[0:RT_TOK, 4 + i % 4, j * P:(j + 1) * P],
                                          q_t[:, hp, t * RT_TOK:(t + 1) * RT_TOK], subk[:, hp % 2, :],
                                          start=True, stop=True)
                mm.then_inc(sc_done, 1)

            with pe.Fori(0, RT_TILES) as it:
                for u in range(U1_PER):
                    n = it * U1_PER + u
                    tile(n + B_U, u % 2, n, free_u, m0_hi, m0_lo, 0, HQ)
            for u in range(MID_TILES):
                n = U1_TILES + u
                tile(n + B_U, u % 2, n, free_u, m0_hi, m0_lo, 0, HQ)
            pe.wait_ge(g_split, 2)
            for t in range(RT_TILES):
                if t >= 2:
                    pe.wait_ge(rt_taken, t - 1)
                for k, src in enumerate((routed[0:RT_TOK, t, 0, :], routed[0:RT_TOK, t, 1, :],
                                         g_hi[0:RT_TOK, t, :].bitcast(F32), g_lo[0:RT_TOK, t, :].bitcast(F32))):
                    mm = nc.tensor.transpose(ps[:, 4 + t % 2, k * RT_TOK:(k + 1) * RT_TOK], src,
                                             ident[0:RT_TOK, 0:RT_TOK])
                mm.then_inc(rt_done, 1)
            pe.sem_inc(hot_used, HR)
            with pe.Fori(0, U2_ITERS) as it:

                def scatter(q):
                    k = it * Q_PER + q
                    pe.wait_ge(hot_ready, k + 19)
                    pe.wait_ge(hot_j_ready, k + 19)
                    pe.wait_ge(gm_taken, k + 1)
                    for t in range(4):
                        dst = ps[:, 4 + q % GR, t * P:(t + 1) * P]
                        nc.tensor.matmul(dst, hot_i[:, q % HR, t, :], hot_j[:, q % HR, 0, t, :],
                                         start=True, stop=False)
                        mm = nc.tensor.matmul(dst, hot_i[:, q % HR, t, :], hot_j[:, q % HR, 1, t, :],
                                              start=False, stop=True)
                    mm.then_inc(hot_used, 1)

                for u in range(U2_PER):
                    n = it * U2_PER + (B_U2 + u)
                    tile(n + B_U, u % 2, n, free_u, m0_hi, m0_lo, 0, HQ,
                         lambda m: [scatter(q) for q in groups_at(u, m)])
            with pe.Fori(0, U3_TILES // 2) as it:
                for u in range(2):
                    n = it * 2 + (B_U3 + u)
                    tile(n + B_U, u, n, free_u, m0_hi, m0_lo, 0, HQ)
            pe.wait_ge(free_u, 4 + 2 * N_EXP_J)
            with pe.Fori(0, N_GROUP // 2) as it:
                for gg in range(2):
                    g = it * 2 + gg
                    hi, lo = ((m1_hi, m1_lo), (m0_hi, m0_lo))[gg]
                    pe.wait_ge(v_lo, g * 8 + 24)
                    for c in range(KC):
                        tile(g * KC + (B_V + c), c % 2, g * KC + c, free_v, hi, lo, 0, HQ)
            pe.wait_ge(free_v, 4 + 2 * N_GROUP * KC)
            norm_sum("nf", lambda c: ones, HQ, False)

        @block.scalar
        def _(act):
            def hi_part(n, slot, k):
                act.wait_ge(raw_in[slot], k * 16)
                act.wait_ge(half_done, n * 2 + 2)
                nc.scalar.copy(w_hi[:, slot], raw[:, slot]).then_inc(hi_ready, 1)

            def norm(name, src, cols, halves, stepwise, hi=None):
                s = norm_sems[name]
                w = 2 * halves

                def std(c):
                    for h in range(2):
                        n = HD if (stepwise and c >= 4) else P if stepwise else D
                        b = (2 * (c % 2) if stepwise else 0) + h
                        act.wait_ge(s["sum"], c + 1)
                        if stepwise and c >= 2:
                            act.wait_ge(s["x"], c - 1)
                        nc.scalar.activation(nrs[:, c % 2 if stepwise else 0, h * halves:(h + 1) * halves],
                                             ps[:, b, 0:halves], ACT.Sqrt, bias=eps,
                                             scale=1.0 / n).then_inc(s["std"], 1)

                def high(c):
                    act.wait_ge(s["x"], c + 1)
                    nc.scalar.copy(hi[:, c, 0:w], ntmp[:, c % 2, 0:w]).then_inc(s["hi"], 1)

                for c in range(KC):
                    if c >= 2:
                        act.wait_ge(s["sum"], c - 1)
                    nc.scalar.square(nsq[:, c % 2, 0:w], src(c)).then_inc(s["sq"], 1)
                    if stepwise and c >= 1:
                        std(c - 1)
                    if stepwise and c >= 2:
                        high(c - 2)
                std(KC - 1)
                if hi is not None:
                    for c in range(KC - 2 if stepwise else 0, KC):
                        high(c)

            act.wait_ge(consts_in, 32)
            act.wait_ge(x_in, 16)
            norm("n1", lambda c: xh[:, c, :], T, HT, False, m0_hi)
            hi_part(0, 0, 1)
            with act.Fori(0, N_QKV // 4) as it:
                for u in range(4):
                    hi_part(it * 4 + (u + 1), (u + 1) % 2, it * 2 + ((u + 1) // 2 + 1))
                    for h in range(2):
                        act.wait_ge(half_done, it * 8 + (2 * u + h + 5))
                        nc.scalar.copy(qkv[:, bass.ds(it * 4 + u, 1), h * HT:(h + 1) * HT],
                                       ps[:, 2 * (u % 2) + h:2 * (u % 2) + h + 1, 0:HT]).then_inc(free_qkv, 1)
            for i in range(12):
                kt, s = i // 2, i % 2
                act.wait_ge(vt_done, i + 1)
                rows = 128 if kt < 4 else 80
                dst = v_nat[0:rows, kt, 512 * s:512 * s + 512] if kt < 5 else vs4[0:80, 512 * s:512 * s + 512]
                nc.scalar.copy(dst, ps[0:rows, i % 4, :]).then_inc(vt_taken, 1)
            nc.scalar.preload_act_table_set("natural_log_exp_and_others")
            act.wait_ge(lam_step, 2)
            nc.scalar.activation(lam[:, 2:4], lam[:, 0:2], ACT.Exp).then_inc(lam_exp, 1)

            act.wait_ge(kv_stored, 48)
            nc.scalar.copy(ones_r[:], ones)
            nc.scalar.copy(tri_r[:], tri)
            nc.scalar.copy(ident_r[:], ident)
            nc.scalar.copy(negm_r[:], negm).then_inc(b_consts, 1)
            for s in range(4 * BH + B_LAG + 3):
                done = s - B_LAG - 1
                if done >= 5 and done % 4 == 1:
                    h = done // 4 - 1
                    r, c = 64 * (h % 2), 20 + h // 2
                    act.wait_ge(b_av, 4 * h + 4)
                    nc.scalar.copy(qkv[r:r + 64, c, N_META:KP], ps[r:r + 64, 6, :])
                    nc.scalar.copy(qkv[r:r + 64, c, KP:T], ps[r:r + 64, 7, 0:64]).then_inc(b_out, 1)
                if 0 <= done < 4 * BH:
                    act.wait_ge(b_cum, done + 1)
                    if done >= 3:
                        act.wait_ge(b_av, done - 2)
                    for rows, o, n in UNITS[done % 4][1]:
                        e = nc.scalar.activation(prob[0:rows, done % 3, o:o + n], ps[0:rows, done % 6, o:o + n],
                                                 ACT.Exp)
                    e.then_inc(b_prob, 1)
                if s < 4 * BH:
                    act.wait_ge(b_abs, s + 1)
                    for rows, o, n in UNITS[s % 4][1]:
                        t = t_abs[0:rows, s % 3, o:o + n]
                        e = nc.scalar.activation(t, t, ACT.Exp)
                    e.then_inc(b_exp, 1)
                    act.wait_ge(b_exp, s + 1)
                    for rows, o, n in UNITS[s % 4][1]:
                        t = t_abs[0:rows, s % 3, o:o + n]
                        e = nc.scalar.activation(t, t, ACT.Ln, bias=1.0)
                    e.then_inc(b_ln, 1)
                if 1 <= s <= 4 * BH:
                    h, u = (s - 1) // 4, (s - 1) % 4
                    act.wait_ge(b_log, s)
                    if h >= 2:
                        act.wait_ge(b_cum, 4 * (h - 1))
                    for rows, o, n in UNITS[u][1]:
                        off = UNITS[u][0] + o
                        e = nc.scalar.copy(log_hi[0:rows, h % 2, off:off + n], t_abs[0:rows, (s - 1) % 3, o:o + n])
                    e.then_inc(b_hi, 1)

            for s in range(NA + 2):
                if s < NA:
                    i = s % 5
                    rows, w = (P, 144 + P * i) if i < 4 else (64, T)
                    for m in range(2):
                        act.wait_ge(a_neg, 2 * s + m + 1)
                        if s >= 2:
                            act.wait_ge(a_w, s - 1)
                        nc.scalar.activation(p_a[0:rows, 2 * (s % 2) + m, 0:w], psf[0:rows, 1024 * m:1024 * m + w],
                                             ACT.Exp, bias=stat[0:rows, 2 + m:3 + m], scale=SCALE,
                                             accum_out=stat[0:rows, 4 + m:5 + m]).then_inc(a_prob, 1)
                if s >= 2:
                    h, i = (s - 2) // 5, (s - 2) % 5
                    rows = A_SHAPE[i][0]
                    q0 = N_META + P * i if i < 4 else KP
                    act.wait_ge(a_o, s - 1)
                    nc.scalar.copy(qkv[:, 8 + h, q0:q0 + rows], ps[:, 6 + s % 2, 0:rows]).then_inc(a_out, 1)
                if 1 <= s <= NA:
                    rows, full, part = A_SHAPE[(s - 1) % 5]
                    act.wait_ge(a_t, s)
                    if s >= 3:
                        act.wait_ge(a_o, s - 2)
                    nc.scalar.copy(wt_a[:, (s - 1) % 2, 0:full, 0:rows],
                                   ps[:, 4, 0:full * rows].rearrange("p (k q) -> p k q", q=rows))
                    nc.scalar.copy(wt_a[0:part, (s - 1) % 2, full, 0:rows], ps[0:part, 5, 0:rows]).then_inc(a_wt, 1)

            act.wait_ge(a_out, 5 * AH)
            norm("nm", merged, None, HQ, True, m0_hi)
            for u in range(N_WO):
                hi_part(B_WO + u + 1, (u + 1) % 2, (B_WO + u + 1) // 2 + 1)
            act.wait_ge(free_wo, 4 + 2 * N_WO)
            norm("n2", lambda c: xh[:, c, N_META:T], None, HQ, False, m0_hi)
            act.wait_ge(ak_stored, 16)
            with act.Fori(0, N_PQ // 4) as it:
                for u in range(4):
                    n0 = B_PQ + u
                    hi_part(it * 4 + (n0 + 1), (u + 1) % 2, it * 2 + ((n0 + 1) // 2 + 1))
                    for h in range(2):
                        act.wait_ge(half_done, it * 8 + (2 * n0 + h + 5))
                        nc.scalar.copy(q_t[:, bass.ds(it * 4 + u, 1), h * HQ:(h + 1) * HQ],
                                       ps[:, 2 * (u % 2) + h:2 * (u % 2) + h + 1, 0:HQ]).then_inc(free_pq, 1)
            for i in range(RT_TILES * 4):
                t, b = i // 4, i % 4
                act.wait_ge(sc_done, i + 1)
                nc.scalar.copy(score[0:RT_TOK, t, 4 * b:4 * b + 4, :],
                               ps[0:RT_TOK, 4 + i % 4, :].rearrange("p (j n) -> p j n", j=4)).then_inc(sc_taken, 1)
            act.wait_ge(sc_taken, RT_TILES * 4)

            def v_high(g8, j, buf):
                act.wait_ge(v_prod, g8 + (j + 1))
                nc.scalar.copy((m1_hi, m0_hi)[buf][:, j, 0:TQ], gated[:, j % 2, :]).then_inc(v_hi, 1)

            def u_step(n, n0, u, it, per, between=None):
                hi_part(n + (B_U + 1), (u + 1) % 2, it * (per // 2) + ((B_U + n0 + 1) // 2 + 1))
                act.wait_ge(act_stored[u % 2], it * (8 * per) + (16 * (n0 // 2) + 16))
                for h in range(2):
                    if between is not None:
                        between(h)
                    act.wait_ge(half_done, n * 2 + (2 * B_U + h + 5))
                    nc.scalar.activation(act_st[:, u % 2, h * HQ:(h + 1) * HQ], ps[:, 2 * (u % 2) + h, 0:HQ],
                                         ACT.Gelu).then_inc(free_u, 1)

            with act.Fori(0, RT_TILES) as it:
                act.wait_ge(top_read, it + 1)
                nc.scalar.copy(cur[0:RT_TOK].unsqueeze(1),
                               score[0:RT_TOK, bass.ds(it, 1), :, :]).then_inc(cur_ready, 1)
                for u in range(U1_PER):
                    u_step(it * U1_PER + u, u, u, it, U1_PER)

            def gates_exp(h):
                if h == 0:
                    act.wait_ge(g_step, 1)
                    nc.scalar.activation(gexp[0:RT_TOK], gexp[0:RT_TOK], ACT.Exp).then_inc(g_exped, 1)

            for u in range(MID_TILES):
                u_step(U1_TILES + u, U1_TILES + u, u, 0, 0, gates_exp if u == 0 else None)
            for t in range(RT_TILES):
                act.wait_ge(rt_done, t + 1)
                nc.scalar.copy(rt_t[:, :, t * RT_TOK:(t + 1) * RT_TOK],
                               ps[:, 4 + t % 2, 0:4 * RT_TOK].rearrange("p (k t) -> p k t", k=4)).then_inc(rt_taken, 1)
            act.wait_ge(rt_taken, RT_TILES)
            act.sem_inc(gm_taken, GR)

            def rows_of(b, slot):
                act.wait_ge(hot_ready, b * 9 + 9)
                act.wait_ge(hot_j_ready, b * 9 + 9)
                nc.scalar.copy(rt_b[:, slot], rt_t[:, :, bass.ds(b * G_TOK, G_TOK)]).then_inc(rtb_ready, 1)

            def u2_iteration(it, last):

                def take_gates(q):
                    nb, qq = q // 9, q % 9
                    if qq == 1 and not (last and nb == BATCH_PER - 1):
                        rows_of(it * BATCH_PER + (nb + 1), (nb + 1) % 2)
                    act.wait_ge(hot_used, it * Q_PER + (q + 1 + HR))
                    if qq == 0:
                        act.wait_ge(g_stored[nb % 2], it * (8 * BATCH_PER) + (16 * (nb // 2) + 16))
                    nc.scalar.copy(g_st[:, nb % 2, :, 4 * qq:4 * qq + 4],
                                   ps[:, 4 + q % GR, :].rearrange("p (t j) -> p j t", t=4)).then_inc(gm_taken, 1)

                for u in range(U2_PER):
                    u_step(it * U2_PER + (B_U2 + u), B_U2 + u, u, it, U2_PER,
                           lambda h: [take_gates(q) for q in before_half(u, h)])
                for q in groups_at(U2_PER - 1, 47):
                    take_gates(q)

            rows_of(0, 0)
            with act.Fori(0, U2_ITERS - 1) as it:
                u2_iteration(it, False)
            u2_iteration(U2_ITERS - 1, True)
            for u in range(U3_TILES):
                n = B_U3 + u
                u_step(n, n, u, 0, 0, (lambda h: v_high(0, u - 6, 0) if h == 0 else None) if u >= 6 else None)

            def v_steps(g, gg, last):
                for c in range(KC):
                    n0 = B_V + gg * KC + c
                    if not (last and c == KC - 1):
                        hi_part(g * KC + (B_V + c + 1), (c + 1) % 2, g * 4 + ((B_V + c + 1) // 2 + 1))
                    if not last:
                        v_high(g * 8 + 8, c, (gg + 1) % 2)

            with act.Fori(0, N_GROUP // 2 - 1) as it:
                for gg in range(2):
                    v_steps(it * 2 + gg, gg, False)
            v_steps(N_GROUP - 2, 0, False)
            v_steps(N_GROUP - 1, 1, True)
            act.wait_ge(free_v, 4 + 2 * N_GROUP * KC)
            norm("nf", lambda c: xh[:, c, N_META:T], None, HQ, False)

        @block.vector
        def _(dve):
            TT, TS = nc.vector.tensor_tensor, nc.vector.tensor_scalar

            def lo_part(n, slot):
                dve.wait_ge(hi_ready, n + 1)
                TT(w_lo[:, slot], raw[:, slot], w_hi[:, slot].bitcast(F32), SUB).then_inc(w_split, 1)

            def norm(name, src, gain, w, stepwise, hi, lo, out=None):
                s = norm_sems[name]

                def rs(c):
                    dve.wait_ge(s["std"], 2 * c + 2)
                    r = nrs[:, c % 2 if stepwise else 0, 0:w]
                    nc.vector.reciprocal(r, r).then_inc(s["rs"], 1)
                    dve.wait_ge(s["rs"], c + 1)

                def low(c):
                    dve.wait_ge(s["hi"], c + 1)
                    TT(lo[:, c, 0:w], ntmp[:, c % 2, 0:w], hi[:, c, 0:w].bitcast(F32), SUB).then_inc(s["lo"], 1)

                if not stepwise:
                    rs(0)
                for c in range(KC):
                    if stepwise:
                        rs(c)
                    if hi is not None and c >= 2:
                        dve.wait_ge(s["lo"], c - 1)
                    dst = ntmp[:, c % 2, 0:w] if out is None else out[:, c]
                    nc.vector.scalar_tensor_tensor(dst, src(c), gain(c), nrs[:, c % 2 if stepwise else 0, 0:w],
                                                   MULT, MULT).then_inc(s["x"], 1)
                    if hi is not None and c >= 1:
                        low(c - 1)
                if hi is not None:
                    low(KC - 1)

            dve.wait_ge(consts_in, 32)
            dve.wait_ge(x_in, 16)
            norm("n1", lambda c: xh[:, c, :], lambda c: gn[:, G_ATTN + c:G_ATTN + c + 1], T, False, m0_hi, m0_lo)
            lo_part(0, 0)
            with dve.Fori(0, N_QKV // 4) as it:
                for u in range(4):
                    lo_part(it * 4 + (u + 1), (u + 1) % 2)

            dve.wait_ge(free_qkv, 4 + 2 * N_QKV)
            dve.wait_ge(tables_in, 16)
            for c in range(8):
                b = 4 + 2 * (c % 2)
                dve.wait_ge(rot_done, c + 1)
                if c >= 2:
                    dve.wait_ge(rope_done, c - 1)
                TT(rtmp[:, c % 2, :], psf[:, 512 * b:512 * b + T], tab[:, 1, :], MULT).then_inc(rope_step, 1)
                TT(qkv[:, c, :], qkv[:, c, :], tab[:, 0, :], MULT).then_inc(rope_step, 1)
                dve.wait_ge(rope_step, 2 * c + 2)
                TT(qkv[:, c, :], qkv[:, c, :], rtmp[:, c % 2, :], ADD).then_inc(rope_done, 1)
            dve.wait_ge(caches_in, 64)
            lp = lam_in[:].rearrange("p (a b d) -> p a b d", a=2, b=2)
            TT(lp[:, :, 0, :], lp[:, :, 0, :], lp[:, :, 1, :], MULT).then_inc(lam_step, 1)
            dve.wait_ge(lam_step, 1)
            nc.vector.tensor_reduce(lam[:, 0:2], lp[:, :, 0, :], AX_X, ADD).then_inc(lam_step, 1)
            dve.wait_ge(lam_exp, 1)
            TT(lam[:, 4:5], lam[:, 3:4], lam[:, 2:3], SUB).then_inc(lam_step, 1)
            dve.wait_ge(lam_step, 3)
            TS(lam[:, 5:6], lam[:, 4:5], -LAM_INIT, None, ADD).then_inc(lam_step, 1)
            TS(gn[:, G_A:G_A + 1], gn[:, G_A:G_A + 1], 1.0 - LAM_INIT, None, MULT).then_inc(lam_step, 1)
            dve.wait_ge(lam_step, 5)

            def b_first(idx):
                u = idx % 4
                dve.wait_ge(b_z, idx + 1)
                if idx >= 2:
                    dve.wait_ge(b_raw, idx - 1)
                for rows, o, n in UNITS[u][1]:
                    last = TS(t_pos[0:rows, idx % 2, o:o + n], ps[0:rows, idx % 6, o:o + n], 0.0, None, ALU.max)
                last.then_inc(b_pos, 1)
                dve.wait_ge(b_pos, idx + 1)
                if idx >= 3:
                    dve.wait_ge(b_lo, idx - 2)
                for rows, o, n in UNITS[u][1]:
                    last = nc.vector.scalar_tensor_tensor(t_abs[0:rows, idx % 3, o:o + n],
                                                          t_pos[0:rows, idx % 2, o:o + n], -2.0,
                                                          ps[0:rows, idx % 6, o:o + n], MULT, ADD)
                last.then_inc(b_abs, 1)

            def b_second(idx):
                u = idx % 4
                dve.wait_ge(b_ln, idx + 1)
                for rows, o, n in UNITS[u][1]:
                    t = t_abs[0:rows, idx % 3, o:o + n]
                    last = nc.vector.scalar_tensor_tensor(t, t, -1.0, t_pos[0:rows, idx % 2, o:o + n], MULT, SUB)
                last.then_inc(b_raw, 1)
                dve.wait_ge(b_raw, idx + 1)
                masks = {0: [(80, 256, 80, 0)], 1: [(128, 0, 128, 0), (128, 272, 128, 0)],
                         2: [(128, 0, 128, 0)], 3: [(128, 0, 112, 16)]}[u]
                for rows, o, n, m0 in masks:
                    t = t_abs[0:rows, idx % 3, o:o + n]
                    last = TT(t, t, mask[0:rows, m0:m0 + n], MULT)
                last.then_inc(b_log, 1)

            def b_third(idx):
                h, u = idx // 4, idx % 4
                dve.wait_ge(b_hi, idx + 1)
                for rows, o, n in UNITS[u][1]:
                    part = slice(UNITS[u][0] + o, UNITS[u][0] + o + n)
                    last = TT(log_lo[0:rows, h % 2, part], t_abs[0:rows, idx % 3, o:o + n],
                              log_hi[0:rows, h % 2, part].bitcast(F32), SUB)
                last.then_inc(b_lo, 1)

            b_first(0)
            for idx in range(4 * BH):
                if idx + 1 < 4 * BH:
                    b_first(idx + 1)
                if idx >= 1:
                    b_third(idx - 1)
                b_second(idx)
            b_third(4 * BH - 1)

            k_step = 0
            dve.wait_ge(b_out, BH)

            def a_step_done(ins):
                nonlocal k_step
                ins.then_inc(a_step, 1)
                k_step += 1
                dve.wait_ge(a_step, k_step)

            def a_greatest(idx):
                i = idx % 5
                rows, w = (P, 144 + P * i) if i < 4 else (64, T)
                for m in range(2):
                    dve.wait_ge(a_s, 2 * idx + m + 1)
                    if i < 4:
                        e0 = 1024 * m + w
                        if w > 512 and w - CHUNK < 512:
                            nc.vector.memset(psf[0:CHUNK, e0 - CHUNK:1024 * m + 512], NEG)
                            a_step_done(nc.vector.memset(psf[0:CHUNK, 1024 * m + 512:e0], NEG))
                        else:
                            a_step_done(nc.vector.memset(psf[0:CHUNK, e0 - CHUNK:e0], NEG))
                    nc.vector.tensor_reduce(stat[0:rows, m:m + 1], psf[0:rows, 1024 * m:1024 * m + w], AX_X,
                                            ALU.max).then_inc(a_max, 1)
                    dve.wait_ge(a_max, 2 * idx + m + 1)
                    TS(stat[0:rows, 2 + m:3 + m], stat[0:rows, m:m + 1], -SCALE, None, MULT).then_inc(a_neg, 1)

            a_greatest(0)
            for idx in range(NA):
                i = idx % 5
                rows, w = (P, 144 + P * i) if i < 4 else (64, T)
                p0 = 2 * (idx % 2)
                dve.wait_ge(a_prob, 2 * idx + 2)
                a_step_done(nc.vector.reciprocal(stat[0:rows, 6:8], stat[0:rows, 4:6]))
                TT(stat[0:rows, 8:9], stat[0:rows, 7:8], lam[0:rows, 5:6], MULT).then_inc(a_step, 1)
                k_step += 1
                if idx >= 2:
                    dve.wait_ge(a_t, idx - 1)
                a_step_done(TS(w_a[0:rows, idx % 2, 0:w], p_a[0:rows, p0, 0:w], stat[0:rows, 6:7], None, MULT))
                nc.vector.scalar_tensor_tensor(w_a[0:rows, idx % 2, 0:w], p_a[0:rows, p0 + 1, 0:w], stat[0:rows, 8:9],
                                               w_a[0:rows, idx % 2, 0:w], MULT, ADD).then_inc(a_w, 1)
                if idx + 1 < NA:
                    a_greatest(idx + 1)

            dve.wait_ge(a_t, 5 * AH)
            dve.wait_ge(a_o, 5 * AH)
            norm("nm", merged, lambda c: gn[:, G_A:G_A + 1] if c < 4 else gn[:, G_B:G_B + 1], TQ, True, m0_hi,
                 m0_lo)
            for u in range(N_WO):
                lo_part(B_WO + u + 1, (u + 1) % 2)
                for h in range(2):
                    dve.wait_ge(half_done, 2 * (B_WO + u) + h + 5)
                    dst = xh[:, u, N_META + h * HQ:N_META + (h + 1) * HQ]
                    TT(dst, ps[:, 2 * (u % 2) + h, 0:HQ], dst, ADD).then_inc(free_wo, 1)
            norm("n2", lambda c: xh[:, c, N_META:T], lambda c: gn[:, G_FFN + c:G_FFN + c + 1], TQ, False, m0_hi,
                 m0_lo)
            with dve.Fori(0, N_PQ // 4) as it:
                for u in range(4):
                    lo_part(it * 4 + (B_PQ + u + 1), (u + 1) % 2)

            R = RT_TOK
            dve.sem_inc(top_read, 1)
            dve.wait_ge(sc_taken, RT_TILES * 4)
            n_links = [0]

            def route(it):
                k = 0

                def link(ins):
                    nonlocal k
                    k += 1
                    ins.then_inc(r_step, 1)
                    dve.wait_ge(r_step, it * R_LINKS + k)
                    dve.sem_inc(route_held, 1)

                dve.wait_ge(cur_ready, it + 1)
                dve.sem_inc(route_held, 1)
                for first in range(0, 16, 8):
                    for hp in range(first, first + 8):
                        last = nc.vector.max(s16[0:R, hp, 0:8], cur[0:R, hp, :])
                    yield
                link(last)
                for hp in range(16):
                    nc.vector.max_index(i16[0:R, hp, 0:8], s16[0:R, hp, 0:8], cur[0:R, hp, :])
                    last = nc.vector.match_replace(cur2[0:R, hp, :], s16[0:R, hp, 0:8], cur[0:R, hp, :], LOWEST)
                    if hp % 4 == 3 and hp < 15:
                        yield
                last.then_inc(top_read, 1)
                dve.wait_ge(top_read, it + 2)
                dve.sem_inc(route_held, 1)
                yield
                for hp in range(16):
                    last = nc.vector.max(s16[0:R, hp, 8:16], cur2[0:R, hp, :])
                    if hp == 7:
                        yield
                link(last)
                yield
                for hp in range(16):
                    nc.vector.max_index(i16[0:R, hp, 8:16], s16[0:R, hp, 8:16], cur2[0:R, hp, :])
                    if hp % 8 == 7:
                        yield
                s4 = s16[0:R].rearrange("p (h s) a -> p h s a", s=2)
                link(TT(cand[0:R], s4[:, :, 0, :].unsqueeze(3).broadcast_to((R, HEADS, TOPK, TOPK)),
                        s4[:, :, 1, :].unsqueeze(2).broadcast_to((R, HEADS, TOPK, TOPK)), ADD))
                link(nc.vector.tensor_copy(i16f[0:R], i16[0:R]))
                cf = cand[0:R].rearrange("p h a b -> p h (a b)")
                cf2 = cand2[0:R].rearrange("p h a b -> p h (a b)")
                for h in range(HEADS):
                    last = nc.vector.max(c16[0:R, h, 0:8], cf[:, h, :])
                link(last)
                yield
                for h in range(HEADS):
                    nc.vector.max_index(j16[0:R, h, 0:8], c16[0:R, h, 0:8], cf[:, h, :])
                    last = nc.vector.match_replace(cf2[:, h, :], c16[0:R, h, 0:8], cf[:, h, :], LOWEST)
                    if h == 3:
                        yield
                link(last)
                yield
                for h in range(HEADS):
                    last = nc.vector.max(c16[0:R, h, 8:16], cf2[:, h, :])
                link(last)
                yield
                for h in range(HEADS):
                    last = nc.vector.max_index(j16[0:R, h, 8:16], c16[0:R, h, 8:16], cf2[:, h, :])
                link(last)
                jj = j16[0:R].rearrange("p h k -> p (h k)")
                TS(jab[0:R, 0], jj, 4, None, ALU.logical_shift_right)
                link(TS(jab[0:R, 1], jj, TOPK - 1, None, ALU.bitwise_and))
                link(nc.vector.tensor_copy(jf[0:R], jab[0:R]))
                yield
                i4 = i16f[0:R].rearrange("p (h s) a -> p h s a", s=2)
                for s in range(2):
                    link(TT(eqs[0:R], jf[0:R, s].unsqueeze(2).broadcast_to((R, PAIRS, TOPK)),
                            iota16[0:R].unsqueeze(1).broadcast_to((R, PAIRS, TOPK)), ALU.is_equal))
                    yield
                    e4 = eqs[0:R].rearrange("p (h k) a -> p h k a", h=HEADS)
                    link(TT(e4, e4, i4[:, :, s, :].unsqueeze(2).broadcast_to((R, HEADS, TOPK, TOPK)), MULT))
                    yield
                    link(nc.vector.tensor_reduce(routed[0:R, bass.ds(it, 1), s, :].rearrange("p o k -> p (o k)"),
                                                 eqs[0:R], AX_X, ADD))
                    yield
                link(nc.vector.tensor_copy(routed[0:R, bass.ds(it, 1), 2, :].rearrange("p o k -> p (o k)"),
                                           c16[0:R].rearrange("p h k -> p (h k)")))
                n_links[0] = k
                yield "ended"

            with dve.Fori(0, RT_TILES) as it:
                steps = route(it)
                for u in range(U1_PER):
                    lo_part(it * U1_PER + (B_U + u + 1), (u + 1) % 2)
                    for _ in range(R_STEPS * u // U1_PER, R_STEPS * (u + 1) // U1_PER):
                        got = next(steps, "too many")
                assert got == "ended", got
                assert not list(steps)
                assert n_links[0] == R_LINKS, n_links

            G6 = (R, RT_TILES, HEADS, TOPK)
            sc = routed[0:R, :, 2, :].rearrange("p t (h k) -> p t h k", h=HEADS)
            ge = gexp[0:R].rearrange("p t (h k) -> p t h k", h=HEADS)
            gs = gsum[0:R, 0].rearrange("p (t h) -> p t h", h=HEADS)
            gr = gsum[0:R, 1].rearrange("p (t h) -> p t h", h=HEADS)

            def glink(ins, n):
                ins.then_inc(g_step, 1)
                dve.wait_ge(g_step, n)

            lo_part(B_U + U1_TILES + 1, 1)
            for t in range(RT_TILES):
                last = TT(ge[:, t], sc[:, t], sc[:, t, :, 0:1].broadcast_to((R, HEADS, TOPK)), SUB)
            glink(last, 1)
            dve.wait_ge(g_exped, 1)
            glink(nc.vector.tensor_reduce(gsum[0:R, 0], gexp[0:R].rearrange("p t (h k) -> p (t h) k", k=TOPK),
                                          AX_X, ADD), 2)
            glink(nc.vector.reciprocal(gsum[0:R, 1], gsum[0:R, 0]), 3)
            lo_part(B_U + U1_TILES + 2, 0)
            gk = gexp[0:R].rearrange("p t (h k) -> p (t h) k", k=TOPK)
            glink(TT(gk, gk, gsum[0:R, 1].unsqueeze(2).broadcast_to((R, RT_TILES * HEADS, TOPK)), MULT), 4)
            nc.vector.tensor_copy(g_hi[0:R], gexp[0:R]).then_inc(g_split, 1)
            dve.wait_ge(g_split, 1)
            TT(g_lo[0:R], gexp[0:R], g_hi[0:R].bitcast(F32), SUB).then_inc(g_split, 1)

            dve.sem_inc(hot_ready, 18)

            def one_hot(it, q):
                nb, qq = q // 9, q % 9
                if qq == 0:
                    dve.wait_ge(rtb_ready, it * BATCH_PER + (nb + 1))
                dve.wait_ge(hot_used, it * Q_PER + (q + 1))
                dve.wait_ge(hot_j_ready, it * Q_PER + (q + 16))

                def rows(k):
                    return rt_b[:, nb % 2, k, 4 * qq:4 * qq + 4].unsqueeze(2).broadcast_to((P, 4, P))

                TT(eq_j[:, q % 3], iota.unsqueeze(1).broadcast_to((P, 4, P)), rows(1), ALU.is_equal)
                TT(hot_i[:, q % HR], iota.unsqueeze(1).broadcast_to((P, 4, P)), rows(0),
                   ALU.is_equal).then_inc(hot_ready, 1)

            def u2_iteration(it, last):
                for u in range(U2_PER):
                    lo_part(it * U2_PER + (B_U + B_U2 + u + 1), (u + 1) % 2)
                    for q in groups_of(u):
                        if not (last and q + HOT_AHEAD >= Q_PER):
                            one_hot(it, q + HOT_AHEAD)

            for q in range(HOT_AHEAD):
                one_hot(0, q)
            with dve.Fori(0, U2_ITERS - 1) as it:
                u2_iteration(it, False)
            u2_iteration(U2_ITERS - 1, True)

            dve.sem_inc(v_lo, 16)

            def product(g8, gg, j, kg, ka):
                if j == 0:
                    dve.wait_ge(g_in_s[gg], kg)
                if j % 4 == 0:
                    dve.wait_ge(act_in_s[j // 4], ka)
                TT(gated[:, j % 2, :].rearrange("p (b t) -> p b t", b=G_BATCH),
                   act_in[:, j // 4, j % 4, :].rearrange("p (b t) -> p b t", b=G_BATCH),
                   g_in[:, gg, :, j, :], MULT).then_inc(v_prod, 1)
                dve.wait_ge(v_hi, g8 + (j + 1))
                TT((m1_lo, m0_lo)[gg][:, j, 0:TQ], gated[:, j % 2, :],
                   (m1_hi, m0_hi)[gg][:, j, 0:TQ].bitcast(F32), SUB).then_inc(v_lo, 1)

            for u in range(U3_TILES):
                lo_part(B_U + B_U3 + u + 1, (u + 1) % 2)
                if u == 6:
                    for s in g_stored:
                        dve.wait_ge(s, 16 * (G_BATCH // 2) + 16)
                if u >= 6:
                    product(0, 0, u - 6, 16, 16)

            def v_steps(g, gg, it, last):
                for c in range(KC):
                    if not (last and c == KC - 1):
                        lo_part(g * KC + (B_V + c + 1), (c + 1) % 2)
                    if not last:
                        nxt = (gg + 1) % 2
                        if c == 0:
                            dve.wait_ge(half_done, g * (2 * KC) + (2 * B_V + 4))
                        product(g * 8 + 8, nxt, c, it * 16 + (16 if nxt else 32), g * 16 + 32)
                    for h in range(2):
                        dve.wait_ge(half_done, g * (2 * KC) + (2 * (B_V + c) + h + 5))
                        dst = xh[:, c, N_META + h * HQ:N_META + (h + 1) * HQ]
                        TT(dst, ps[:, 2 * (c % 2) + h, 0:HQ], dst, ADD).then_inc(free_v, 1)

            with dve.Fori(0, N_GROUP // 2 - 1) as it:
                for gg in range(2):
                    v_steps(it * 2 + gg, gg, it, False)
            v_steps(N_GROUP - 2, 0, N_GROUP // 2 - 1, False)
            v_steps(N_GROUP - 1, 1, N_GROUP // 2 - 1, True)
            norm("nf", lambda c: xh[:, c, N_META:T], lambda c: gn[:, G_FINAL + c:G_FINAL + c + 1], TQ, False, None,
                 None, out=y_st)


R_LINKS = 17
R_STEPS = 22


def constants():
    k, m = np.arange(P)[:, None], np.arange(P)[None, :]
    c = np.zeros((P, C_W), np.float32)
    c[:, C_ID:C_ID + P] = k == m
    c[:, C_TRI:C_TRI + P] = k >= m
    c[:, C_ONE:C_ONE + P] = 1
    c[:, C_BD:C_BD + P] = k // HD == m // HD
    half = HD // 8
    d = np.arange(P)
    for j in range(P):
        if d[j] % HD < half:
            c[j + half, C_ROT + j] = -1
        elif d[j] % HD < 2 * half:
            c[j - half, C_ROT + j] = 1
    c[:, C_MASK:C_MASK + P] = k < m
    c[:, C_NEG:C_NEG + P] = np.where(k < m, 0, NEG)
    c[:, C_IOTA:C_IOTA + P] = m
    c[:, C_IOTA16:C_IOTA16 + TOPK] = np.arange(TOPK)
    c[:, C_EPS] = EPS
    inv = (np.float32(500000.0) ** (-np.arange(half, dtype=np.float32) * np.float32(2.0) / np.float32(2 * half)))
    ang = np.arange(T, dtype=np.float32)[None, :] * inv.astype(np.float32)[:, None]
    tab = np.zeros((P, 2, T), np.float32)
    tab[:, 0] = 1
    for j in range(P):
        if d[j] % HD < 2 * half:
            tab[j, 0] = np.cos(ang[d[j] % half])
            tab[j, 1] = np.sin(ang[d[j] % half])
    return c, tab


def kernel(x_prompt, x_sample, cache_a_k, cache_a_v, cache_b_k, cache_b_v, meta_tokens, g_attn, w_qkv,
           diff_lambda, a_norm_g, b_norm_g, w_o, g_ffn, w_peer_q, peer_sub_keys, peer_u, peer_v, g_final):
    import concourse.bacc as bacc
    from concourse.bass_utils import run_bass_kernel_spmd

    consts, tab = constants()
    x = np.concatenate([meta_tokens, x_prompt[0], x_sample[0]], axis=0)
    x_t = x.T.reshape(KC, P, T).transpose(1, 0, 2)
    col = lambda g: np.asarray(g).reshape(-1, P).T
    gains = np.concatenate([col(g_attn[0]), col(g_ffn[0]), col(g_final), col(a_norm_g[0]),
                            np.concatenate([b_norm_g[0], b_norm_g[0]]).reshape(P, 1)], axis=1)

    def k_t(c):
        return np.asarray(c).reshape(KP, 4, P).transpose(2, 1, 0)

    cache_k = np.concatenate([k_t(cache_a_k[0, 0]), k_t(cache_b_k[0, 0])], axis=1)
    va, vb = np.asarray(cache_a_v)[0, 0].reshape(KP, 512), np.asarray(cache_b_v)[0, 0].reshape(KP, 512)
    v = np.concatenate([va, vb], axis=1)
    cache_v = v[:512].reshape(4, P, 1024).transpose(1, 0, 2)
    cache_vt = v[512:].T.reshape(8, P, N_META).transpose(1, 0, 2)

    def w_t(w):
        w = np.asarray(w)
        return w.reshape(KC, P, w.shape[1] // P, P).transpose(2, 1, 0, 3).reshape(-1, KC * P)

    u_t = np.asarray(peer_u)[0].reshape(P, P, KC, P).transpose(1, 3, 2, 0).reshape(-1, KC * P)
    v_t = np.asarray(peer_v)[0].reshape(P, N_GROUP, 8, KC, P).transpose(1, 3, 0, 2, 4).reshape(-1, KC * P)
    w_tiles = np.concatenate([w_t(w_qkv[0]), w_t(w_o[0]), w_t(w_peer_q[0]), u_t, v_t], axis=0)
    sub_keys = np.asarray(peer_sub_keys)[0].transpose(2, 0, 1)

    nc = bacc.Bacc("TRN2", target_bir_lowering=False, num_devices=1)
    arrays, args = {}, []
    for name, a in (("x_t", x_t), ("consts", consts), ("tables", tab), ("gains", gains),
                    ("lam_p", np.asarray(diff_lambda)[0].reshape(256)), ("cache_k", cache_k), ("cache_v", cache_v),
                    ("cache_vt", cache_vt), ("w_tiles", w_tiles), ("sub_keys", sub_keys)):
        arrays[name] = np.ascontiguousarray(a)
        args.append(nc.dram_tensor(name, a.shape, F32, kind="ExternalInput").ap())
    args.append(nc.dram_tensor("y_t", (KC, P, TQ), F32, kind="ExternalOutput").ap())
    args.append(nc.dram_tensor("kv_t", (4, P, 4, T), F32, kind="ExternalOutput").ap())
    bass_hybrid_step(nc, *args)
    out = run_bass_kernel_spmd(nc, [arrays], core_ids=[0]).results[0]

    y = out["y_t"].reshape(D, TQ).T
    a_k, a_v, b_k, b_v = out["kv_t"].transpose(0, 3, 2, 1).reshape(4, T, 512)
    a_shape, b_shape = (1, 1, -1, AH, 2 * HD), (1, 1, -1, BH, HD)
    parts = [(a_k, a_shape), (a_v, a_shape), (b_k, b_shape), (b_v, b_shape)]
    return ((np.ascontiguousarray(y[None, :SEQ]), np.ascontiguousarray(y[None, SEQ:]))
            + tuple(np.ascontiguousarray(a[:KP].reshape(s)) for a, s in parts)
            + tuple(np.ascontiguousarray(a[KP:].reshape(s)) for a, s in parts))
```

```python
from contextlib import ExitStack

import numpy as np

import concourse.bass as bass
from concourse import mybir

F32 = mybir.dt.float32
F32R = mybir.dt.float32r
U32 = mybir.dt.uint32
ALU = mybir.AluOpType
ACT = mybir.ActivationFunctionType
AX_X = mybir.AxisListType.X

P = 128
D = 1024
KC = D // P
N_META, SEQ, DEC, PAST = 16, 512, 64, 512
HD = 64
AH, BH = 4, 8
KP = N_META + SEQ
T = KP + DEC
TQ = SEQ + DEC
HQ = TQ // 2
HT = T // 2
CHUNK = 64
EPS = 1e-6
LAM_INIT = 0.2
SCALE = HD ** -0.5
NEG = -1e30
LOWEST = -3.0e38

N_QKV, N_WO, N_PQ = 24, 8, 16
B_WO = N_QKV
B_PQ = B_WO + N_WO
B_U = B_PQ + N_PQ
N_EXP_J = 128
B_V = B_U + N_EXP_J
N_GROUP = 16
NT_ALL = B_V + N_GROUP * KC

RT_TILES, RT_TOK, U1_PER = 6, 96, 12
U1_TILES = RT_TILES * U1_PER
G_BATCH, G_TOK = 16, 36
MID_TILES = 2
B_U2 = U1_TILES + MID_TILES
U2_ITERS, U2_PER = 4, 10
B_U3 = B_U2 + U2_ITERS * U2_PER
U3_TILES = N_EXP_J - B_U3
BATCH_PER = G_BATCH // U2_ITERS
Q_PER = BATCH_PER * (G_TOK // 4)
GR = 4
HR = 6
HOT_AHEAD = 4
HEADS, TOPK = 8, 16
PAIRS = HEADS * TOPK
assert U3_TILES == 14 and Q_PER % GR == 0 and BATCH_PER % 2 == 0 and Q_PER % HR == 0 and RT_TILES * RT_TOK == TQ == G_BATCH * G_TOK

C_ID, C_TRI, C_ONE, C_SEL, C_ROT, C_MASK, C_NEG, C_IOTA = (P * n for n in range(8))
C_IOTA16 = 8 * P
C_EPS = C_IOTA16 + TOPK
C_W = C_EPS + 1
NH_ROWS = 12
NM_BANK = (4, 6, 2)
G_ATTN, G_FFN, G_FINAL, G_A, G_B = 0, 8, 16, 24, 25
G_W = 26

PK = [0, 1, 2, 3, 4]
K_ROWS = [128, 128, 128, 128, 80]
Q_FROM = [0, 112, 240, 368, 496]
P_OFF = [0, 512, 912, 1184, 1584]
S_OFF = [1328, 1392, 1456, 1520, 1600]
B_COLS = 1664
UNITS = [
    (1328, [(128, 0, 256), (80, 256, 80)]),
    (912, [(128, 0, 416)]),
    (512, [(128, 0, 400)]),
    (0, [(128, 0, 512)]),
]
B_LAG = 4
NA = 5 * AH
A_SHAPE = [(P, i + 1, 16) for i in range(4)] + [(64, 4, 80)]
GROUPS = [
    [("s", kt, S_OFF[kt] - 1328, 64) for kt in range(4)] + [("p", 4, 256, 16), ("s", 4, 272, 64)],
    [("p", 3, 272, 144), ("p", 2, 0, 272)],
    [("p", 1, 0, 400)],
    [("p", 0, 0, 512)],
]


def bass_hybrid_step(nc, x_t, consts, tables, spread, gains, lam_p, cache_k, cache_v, cache_vt, w_tiles, sub_keys,
                     y_out, kv_out):
    g_dram = nc.dram_tensor("gates_scattered", (G_BATCH * P, P * G_TOK), F32).ap()
    act_dram = nc.dram_tensor("activated", (N_EXP_J * P, TQ), F32).ap()

    with ExitStack() as ctx:
        base = [16512]

        def at(name, shape, dt, off):
            return nc.alloc_sbuf_tensor_at(name, shape, dt, offset=off)

        def fixed(name, shape, dt=F32):
            n = 4 * int(np.prod(shape[1:]))
            n = (n + 31) // 32 * 32
            off = base[0]
            base[0] += n
            return at(name, shape, dt, off)

        def sem(name):
            return ctx.enter_context(nc.semaphore(name))

        xh = fixed("xh", [P, KC, T])
        cst = fixed("cst", [P, C_W])
        gn = fixed("gn", [P, G_W])
        lam = fixed("lam", [P, 8])
        stat = fixed("stat", [P, 16])
        raw = fixed("raw", [P, 2, KC, P])
        w_hi = fixed("w_hi", [P, 2, KC, P], F32R)
        w_lo = fixed("w_lo", [P, 2, KC, P], F32R)
        m0_off = base[0]
        m0_hi = fixed("m0_hi", [P, KC, T], F32R)
        m0_lo = fixed("m0_lo", [P, KC, T], F32R)
        region = base[0]
        assert region <= 229344 - 121472

        off = region
        qkv = at("qkv", [P, 24, T], F32, off)
        off += 24 * T * 4
        v_nat = at("v_nat", [P, 5, 1024], F32, off)
        off += 5 * 4096
        vs4 = at("vs4", [P, 1024], F32, off)
        off += 4096
        v_cache = at("v_cache", [P, 4, 1024], F32, off)
        norm_off = off
        off += 4 * 4096
        k_cache = at("k_cache", [P, 8, T], F32, off)
        off += 8 * T * 4
        tab = at("tab", [P, 2, T], F32, off)
        spr = at("spr", [P, KC, P], F32, off)
        off += 2 * T * 4
        assert off <= 229344
        nsq = at("nsq", [P, 2, T], F32, norm_off)
        nrs = at("nrs", [P, T], F32, norm_off + 2 * T * 4)
        ntmp = at("ntmp", [P, 2, T], F32, norm_off + 4 * T * 4)
        off = m0_off
        log_hi = at("log_hi", [P, 2, B_COLS], F32R, off)
        off += 2 * B_COLS * 4
        log_lo = at("log_lo", [P, 2, B_COLS], F32R, off)
        off += 2 * B_COLS * 4
        t_abs = at("t_abs", [P, 3, 512], F32, off)
        off += 6144
        t_pos = at("t_pos", [P, 2, 512], F32, off)
        off += 4096
        assert off <= region
        prob = at("prob", [P, 3, 512], F32, region + 8 * T * 4)
        cst_r = [at(f"cst_r{k}", [P, P], F32R, region + 8 * T * 4 + 6144 + 512 * k) for k in range(4)]
        ones_r, tri_r, ident_r, negm_r = cst_r
        rtmp = at("rtmp", [P, 2, T], F32, m0_off)
        lam_in = at("lam_in", [P, 256], F32, m0_off + 8 * T)
        vs_t = at("vs_t", [P, 8, 80], F32, m0_off + 8 * T + 2048)
        p_a = at("p_a", [P, 4, T], F32, m0_off)
        w_a = at("w_a", [P, 2, T], F32, m0_off + 16 * T)
        wt_a = at("wt_a", [P, 2, 5, P], F32, m0_off + 24 * T)

        off = region
        q_t = at("q_t", [P, 16, TQ], F32, off)
        cand = at("cand", [P, HEADS, TOPK, TOPK], F32, off)
        cand2 = at("cand2", [P, HEADS, TOPK, TOPK], F32, off + 8192)
        eqs = at("eqs", [P, PAIRS, TOPK], F32, off + 16384)
        cur2 = at("cur2", [P, 16, P], F32, off + 24576)
        small = off + 32768
        s16 = at("s16", [P, 16, TOPK], F32, small)
        c16 = at("c16", [P, HEADS, TOPK], F32, small + 1024)
        i16f = at("i16f", [P, 16, TOPK], F32, small + 1536)
        jf = at("jf", [P, 2, PAIRS], F32, small + 2560)
        g_st = at("g_st", [P, 2, P, G_TOK], F32, off)
        off += 16 * TQ * 4
        score = at("score", [P, RT_TILES, 16, P], F32, off)
        off += RT_TILES * 8192
        cur = at("cur", [P, 16, P], F32, off)
        off += 8192
        i16 = at("i16", [P, 16, TOPK], U32, off)
        off += 1024
        j16 = at("j16", [P, HEADS, TOPK], U32, off)
        off += 512
        jab = at("jab", [P, 2, PAIRS], U32, off)
        off += 1024
        act_st = at("act_st", [P, 2, TQ], F32, off)
        off += 2 * TQ * 4
        subk = at("subk", [P, 2, P], F32, off)
        off += 1024
        eq_j = at("eq_j", [P, 3, 4, P], F32, off)
        routed = at("routed", [P, RT_TILES, 3, PAIRS], F32, off)
        off += RT_TILES * 3 * PAIRS * 4
        rt_t = at("rt_t", [P, 4, TQ], F32, region + 16 * TQ * 4)
        g_hi = at("g_hi", [P, RT_TILES, PAIRS], F32R, region + 16 * TQ * 4 + 9216)
        g_lo = at("g_lo", [P, RT_TILES, PAIRS], F32R, region + 16 * TQ * 4 + 9216 + 3072)
        gexp = at("gexp", [P, RT_TILES, PAIRS], F32, region + 16 * TQ * 4 + 9216 + 6144)
        gsum = at("gsum", [P, 2, RT_TILES * HEADS], F32, region + 16 * TQ * 4 + 9216 + 9216)
        hot_off = region + 16 * TQ * 4 + 9216
        hot_i = at("hot_i", [P, HR, 4, P], F32R, hot_off)
        hot_j = at("hot_j", [P, HR, 2, 4, P], F32R, hot_off + HR * 2048)
        rt_b = at("rt_b", [P, 2, 4, G_TOK], F32, hot_off + 3 * HR * 2048)
        assert off <= 229344

        off = region
        m1_hi = at("m1_hi", [P, KC, TQ], F32R, off)
        off += KC * TQ * 4
        m1_lo = at("m1_lo", [P, KC, TQ], F32R, off)
        off += KC * TQ * 4
        g_in = at("g_in", [P, 2, G_BATCH, KC, G_TOK], F32, off)
        off += 2 * KC * TQ * 4
        act_in = at("act_in", [P, 2, 4, TQ], F32, off)
        off += 2 * 4 * TQ * 4
        gated = at("gated", [P, 2, TQ], F32, off)
        off += 2 * TQ * 4
        assert off <= 229344
        y_st = at("y_st", [P, KC, TQ], F32, region)

        ps = ctx.enter_context(nc.psum_tensor("ps", [P, 8, 512], F32))
        psf = ps[:].rearrange("p b n -> p (b n)")

        ident, tri = cst[:, C_ID:C_ID + P], cst[:, C_TRI:C_TRI + P]
        ones, sel = cst[:, C_ONE:C_ONE + P], cst[:, C_SEL:C_SEL + NH_ROWS * KC]
        rot, mask = cst[:, C_ROT:C_ROT + P], cst[:, C_MASK:C_MASK + P]
        negm, iota = cst[:, C_NEG:C_NEG + P], cst[:, C_IOTA:C_IOTA + P]
        iota16, eps = cst[:, C_IOTA16:C_IOTA16 + TOPK], cst[:, C_EPS:C_EPS + 1]

        consts_in, x_in = sem("consts_in"), [sem(f"x_in{c}") for c in range(KC)]
        spread_in, nm_factored = sem("spread_in"), sem("nm_factored")
        tables_in, caches_in = sem("tables_in"), sem("caches_in")
        raw_in = [sem("raw_in0"), sem("raw_in1")]
        hi_ready = sem("hi_ready")
        w_split = sem("w_split")
        half_done = sem("half_done")
        free_qkv, free_wo, free_pq = sem("free_qkv"), sem("free_wo"), sem("free_pq")
        free_u, free_v = sem("free_u"), sem("free_v")
        norm_sems = {n: {k: sem(f"{n}_{k}") for k in ("sq", "sum", "std", "rs", "x", "hi", "lo")}
                     for n in ("n1", "nm", "n2", "nf")}
        vt_done, vt_taken = sem("vt_done"), sem("vt_taken")
        q_scaled, cos_done = sem("q_scaled"), sem("cos_done")
        rot_done, rope_step, rope_done = sem("rot_done"), sem("rope_step"), sem("rope_done")
        prep_done, lam_step, lam_exp = sem("prep_done"), sem("lam_step"), sem("lam_exp")
        ks_ready = sem("ks_ready")
        b_z, b_abs, b_exp, b_ln, b_log = sem("b_z"), sem("b_abs"), sem("b_exp"), sem("b_ln"), sem("b_log")
        b_raw, b_pos, b_hi, b_lo, b_consts = sem("b_raw"), sem("b_pos"), sem("b_hi"), sem("b_lo"), sem("b_consts")
        b_cum, b_prob, b_av, b_out = sem("b_cum"), sem("b_prob"), sem("b_av"), sem("b_out")
        a_s, a_max, a_neg, a_prob = sem("a_s"), sem("a_max"), sem("a_neg"), sem("a_prob")
        a_step, a_w, a_t, a_wt, a_o, a_out = (sem("a_step"), sem("a_w"), sem("a_t"), sem("a_wt"), sem("a_o"),
                                              sem("a_out"))
        kv_stored, ak_stored = sem("kv_stored"), sem("ak_stored")
        subk_in, sc_done, sc_taken = sem("subk_in"), sem("sc_done"), sem("sc_taken")
        cur_ready, top_read, r_step, routed_s = sem("cur_ready"), sem("top_read"), sem("r_step"), sem("routed_s")
        route_held = sem("route_held")
        g_step, g_exped, g_split = sem("g_step"), sem("g_exped"), sem("g_split")
        rt_done, rt_taken = sem("rt_done"), sem("rt_taken")
        act_stored = [sem("act_stored0"), sem("act_stored1")]
        rtb_ready = sem("rtb_ready")
        hot_ready, hot_used, gm_taken = sem("hot_ready"), sem("hot_used"), sem("gm_taken")
        hot_j_ready, hot_held = sem("hot_j_ready"), sem("hot_held")
        g_stored = [sem("g_stored0"), sem("g_stored1")]
        g_in_s = [sem("g_in0"), sem("g_in1")]
        act_in_s = [sem("act_in0"), sem("act_in1")]
        v_prod, v_hi, v_lo = sem("v_prod"), sem("v_hi"), sem("v_lo")
        y_stored = sem("y_stored")

        block = ctx.enter_context(nc.Block())

        MULT, ADD, SUB = ALU.mult, ALU.add, ALU.subtract

        def merged(c):
            return qkv[:, 8 + c if c < 4 else 16 + c, N_META:T]

        def groups_at(u, m):
            at_m = 48 * u + m + 1
            return [q for q in range(Q_PER) if (q + 1) * 48 * U2_PER // Q_PER == at_m]

        def before_half(u, h):
            late = groups_at(u, 23) if h else groups_at(u - 1, 47) if u else []
            return late + [q for m in range(24 * h, 24 * h + 23) for q in groups_at(u, m)]

        def groups_of(u, half=None):
            return [q for m in range(48) if half is None or m // 24 == half for q in groups_at(u, m)]

        @block.sync
        def _(sp):
            sp.sem_inc(w_split, 2)
            for s in (free_qkv, free_wo, free_pq, free_u, free_v):
                sp.sem_inc(s, 4)
            sp.dma_start(cst[:], consts).then_inc(consts_in, 16)
            sp.dma_start(gn[:], gains).then_inc(consts_in, 16)
            for c in range(KC):
                sp.dma_start(xh[:, c], x_t[:, c]).then_inc(x_in[c], 16)

            def load_tile(n, slot):
                sp.wait_ge(w_split, n + 1)
                sp.dma_start(raw[:, slot], w_tiles[bass.ds(n * P, P), :]).then_inc(raw_in[slot], 16)

            with sp.Fori(0, B_U // 8) as it:
                for u in range(8):
                    load_tile(it * 8 + u, u % 2)
            for n in range(B_U, B_U + 3):
                load_tile(n, n % 2)

            def load_gates(g, gg):
                sp.wait_ge(v_lo, g * 8 + 8)
                sp.dma_start(g_in[:, gg].rearrange("p b j t -> p b (j t)"),
                             g_dram[:, bass.ds(g * (KC * G_TOK), KC * G_TOK)].rearrange(
                                 "(b p) n -> p b n", p=P)).then_inc(g_in_s[gg], 16)

            def load_acts(g, hh):
                sp.wait_ge(v_lo, g * 8 + 4 * hh + 12)
                for s in act_stored:
                    sp.wait_ge(s, g * 64 + 80)
                sp.dma_start(act_in[:, hh],
                             act_dram[bass.ds(g * (8 * P) + hh * 4 * P, 4 * P), :].rearrange(
                                 "(j p) t -> p j t", p=P)).then_inc(act_in_s[hh], 16)

            def load_vs(g, gg, tiles=KC, inputs=True):
                for c in range(tiles):
                    load_tile(g * KC + (B_V + c + 2), c % 2)
                    if c == 0 and tiles == KC:
                        load_acts(g + 1, 1)
                    if c == 1 and inputs:
                        load_gates(g + 2, gg)
                    if c == 5 and inputs:
                        load_acts(g + 2, 0)

            for s in act_stored + g_stored:
                sp.sem_inc(s, 16)

            def store_act(n, slot):
                sp.wait_ge(free_u, n * 2 + 6)
                sp.dma_start(act_dram[bass.ds(n * P, P), :], act_st[:, slot]).then_inc(act_stored[slot], 16)

            with sp.Fori(0, B_U2 // 2) as it:
                for u in range(2):
                    load_tile(it * 2 + (B_U + 3 + u), (u + 1) % 2)
                    store_act(it * 2 + u, u)
            with sp.Fori(0, U2_ITERS) as it:
                for u in range(U2_PER):
                    load_tile(it * U2_PER + (B_U + B_U2 + 3 + u), (u + 1) % 2)
                    store_act(it * U2_PER + (B_U2 + u), u % 2)
                    for nb in range(BATCH_PER):
                        if 9 * nb + 8 in groups_of(u):
                            sp.wait_ge(gm_taken, it * Q_PER + (9 * (nb + 1) + GR))
                            sp.dma_start(g_dram[bass.ds((it * BATCH_PER + nb) * P, P), :],
                                         g_st[:, nb % 2].rearrange("p j t -> p (j t)")).then_inc(g_stored[nb % 2], 16)
            for m in range(B_U3, N_EXP_J):
                n = B_U + 3 + m
                if n < B_V + 2:
                    load_tile(n, n % 2)
                store_act(m, m % 2)
                if n == B_U + B_U3 + 4:
                    for s in g_stored:
                        sp.wait_ge(s, 16 * (G_BATCH // 2) + 16)
                    load_gates(0, 0)
                    load_acts(0, 0)
                    load_acts(0, 1)
                if n == B_U + B_U3 + 9:
                    load_gates(1, 1)
                if n == B_V + 2:
                    load_acts(1, 0)
            with sp.Fori(0, N_GROUP // 2 - 1) as it:
                for gg in range(2):
                    load_vs(it * 2 + gg, gg)
            load_vs(N_GROUP - 2, 0, inputs=False)
            load_vs(N_GROUP - 1, 1, KC - 2, inputs=False)
            for c in range(KC):
                sp.wait_ge(norm_sems["nf"]["x"], c + 1)
                sp.dma_start(y_out[c], y_st[:, c]).then_inc(y_stored, 16)
            sp.wait_ge(y_stored, 16 * KC)

        @block.gpsimd
        def _(pool):
            pool.dma_start(tab[:], tables).then_inc(tables_in, 16)
            pool.dma_start(k_cache[:, :, 0:KP], cache_k).then_inc(caches_in, 16)
            pool.wait_ge(norm_sems["n1"]["lo"], KC)
            pool.dma_start(v_cache[:], cache_v).then_inc(caches_in, 16)
            pool.wait_ge(free_qkv, 4 + 2 * N_QKV)
            pool.dma_start(lam_in[:], lam_p.partition_broadcast(P)).then_inc(caches_in, 16)
            pool.dma_start(vs_t[:, :, 0:N_META], cache_vt).then_inc(caches_in, 16)
            nc.gpsimd.tensor_copy(vs_t[:, 0:4, N_META:80], qkv[:, 8:12, KP:T]).then_inc(prep_done, 1)
            nc.gpsimd.tensor_copy(vs_t[:, 4:8, N_META:80], qkv[:, 20:24, KP:T]).then_inc(prep_done, 1)
            pool.wait_ge(tables_in, 16)
            for c in range(8):
                pool.wait_ge(rot_done, c + 1)
                nc.gpsimd.tensor_tensor(qkv[:, c, :], qkv[:, c, :], tab[:, 0, :], MULT).then_inc(cos_done, 1)
            nc.gpsimd.tensor_copy(k_cache[:, 4:8, KP:T], qkv[:, 16:20, KP:T]).then_inc(prep_done, 1)
            pool.wait_ge(rope_done, 8)
            nc.gpsimd.tensor_copy(k_cache[:, 0:4, KP:T], qkv[:, 4:8, KP:T]).then_inc(ks_ready, 1)
            pool.dma_start(kv_out[0], qkv[:, 4:8, :]).then_inc(ak_stored, 16)
            pool.dma_start(spr[0:NH_ROWS], spread).then_inc(spread_in, 16)
            pool.wait_ge(kv_stored, 48)
            pool.wait_ge(ak_stored, 16)
            pool.wait_ge(a_out, 5 * AH)
            pool.dma_start(subk[:], sub_keys).then_inc(subk_in, 16)
            pool.wait_ge(rt_taken, RT_TILES)
            pool.sem_inc(hot_j_ready, 18)
            with pool.Fori(0, U2_ITERS) as it:
                for q in range(Q_PER):
                    nb, qq = q // 9, q % 9
                    pool.wait_ge(hot_ready, it * Q_PER + (q + 19))
                    pool.sem_inc(hot_held, 1)
                    pool.wait_ge(hot_used, it * Q_PER + (q + 1))
                    nc.gpsimd.tensor_tensor(
                        hot_j[:, q % HR], eq_j[:, q % 3].unsqueeze(1).broadcast_to((P, 2, 4, P)),
                        rt_b[:, nb % 2, 2:4, 4 * qq:4 * qq + 4].unsqueeze(3).broadcast_to((P, 2, 4, P)),
                        MULT).then_inc(hot_j_ready, 1)

        @block.tensor
        def _(pe):
            pe.sem_inc(half_done, 4)

            def tile(n, slot, k, free, hi, lo, col, width, after=None, chunk=None):
                pe.wait_ge(w_split, n + 3)
                for h in range(2):
                    pe.wait_ge(free, k * 2 + h + 1)
                    c0 = col + h * width
                    m = 0
                    for kc in range(KC):
                        if chunk is not None and h == 0:
                            chunk(kc)
                        for w, x in ((w_hi, hi), (w_hi, lo), (w_lo, hi)):
                            mm = nc.tensor.matmul(ps[:, 2 * slot + h, 0:width], w[:, slot, kc, :],
                                                  x[:, kc, c0:c0 + width], start=(m == 0), stop=(m == 23))
                            m += 1
                            if m == 24:
                                mm.then_inc(half_done, 1)
                            if after is not None:
                                after(24 * h + m - 1)

            def norm_sum(name, c, halves, weights=ones, rows=P):
                s = norm_sems[name]
                pe.wait_ge(s["sq"], c + 1)
                for h in range(2):
                    mm = nc.tensor.matmul(ps[0:rows, 4 + h, 0:halves], weights,
                                          nsq[:, c % 2, h * halves:(h + 1) * halves], start=(c == 0),
                                          stop=(c == KC - 1), skip_group_check=True)
                mm.then_inc(s["sum"], 1)

            def split_of(name):
                return lambda kc: pe.wait_ge(norm_sems[name]["lo"], kc + 1)

            pe.wait_ge(consts_in, 32)
            for c in range(KC):
                norm_sum("n1", c, HT)
            with pe.Fori(0, N_QKV // 4) as it:
                for u in range(4):
                    n = it * 4 + u
                    tile(n, u % 2, n, free_qkv, m0_hi, m0_lo, 0, HT, chunk=split_of("n1"))
            pe.wait_ge(free_qkv, 4 + 2 * N_QKV)
            for k in range(8):
                if k >= 2:
                    pe.wait_ge(rope_step, k - 1)
                b = 4 + 2 * (k % 2)
                nc.tensor.matmul(ps[:, b, 0:512], rot, qkv[:, k, 0:512], start=True, stop=True)
                nc.tensor.matmul(ps[:, b + 1, 0:T - 512], rot, qkv[:, k, 512:T],
                                 start=True, stop=True).then_inc(rot_done, 1)
                for i in range(12 * k // 8, 12 * (k + 1) // 8):
                    kt, s = i // 2, i % 2
                    if i >= 4:
                        pe.wait_ge(vt_taken, i - 3)
                    if i == 10:
                        pe.wait_ge(prep_done, 2)
                        pe.wait_ge(caches_in, 64)
                    for c in range(4):
                        if kt < 5:
                            src = qkv[:, (8, 20)[s] + c, kt * P:min(T, kt * P + P)]
                        else:
                            src = vs_t[:, 4 * s + c, :]
                        rows = 128 if kt < 4 else 80
                        mm = nc.tensor.transpose(ps[0:rows, i % 4, c * P:(c + 1) * P], src, ident)
                    mm.then_inc(vt_done, 1)

            pe.wait_ge(vt_taken, 12)
            pe.wait_ge(rope_done, 8)
            pe.wait_ge(q_scaled, 1)
            pe.wait_ge(prep_done, 3)

            def qk(h, kind, kt, dst, start):
                r, c = 64 * (h % 2), h // 2
                rows = K_ROWS[kt]
                if kind == "p":
                    k = qkv[r:r + 64, 16 + c, kt * P:kt * P + rows]
                    q = qkv[r:r + 64, 12 + c, N_META + Q_FROM[kt]:KP]
                else:
                    k = k_cache[r:r + 64, 4 + c, kt * P:kt * P + rows]
                    q = qkv[r:r + 64, 12 + c, KP:T]
                return nc.tensor.matmul(dst, k, q, start=start, stop=True, skip_group_check=True)

            def b_sums(idx):
                h, u = idx // 4, idx % 4
                pe.wait_ge(b_lo, idx + 1)
                hp = h % 2

                def add(lhs, rhs, rows, o, n):
                    return nc.tensor.matmul(ps[0:rows, idx % 6, o:o + n], lhs, rhs, start=False, stop=True,
                                            skip_group_check=True)

                if u == 0:
                    for lg in (log_hi, log_lo):
                        for k2 in range(4, 0, -1):
                            r2 = K_ROWS[k2]
                            rhs = lg[0:r2, hp, S_OFF[k2]:S_OFF[k2] + 64].unsqueeze(1).broadcast_to((r2, k2, 64))
                            add(ones_r[0:r2, :], rhs, P, 0, 64 * k2)
                        add(tri_r[:], lg[:, hp, S_OFF[0]:S_OFF[0] + 256], P, 0, 256)
                        add(tri_r[0:80, 0:80], lg[0:80, hp, P_OFF[4]:P_OFF[4] + 80], 80, 256, 80)
                    mm = add(ident_r[0:80, 0:80], negm_r[0:80, 0:80], 80, 256, 80)
                else:
                    for _, kt, o, n in GROUPS[u]:
                        for lg in (log_hi, log_lo):
                            for k2 in range(4, kt, -1):
                                c, r2 = Q_FROM[k2] - Q_FROM[kt], K_ROWS[k2]
                                add(ones_r[0:r2, :], lg[0:r2, hp, P_OFF[k2]:P_OFF[k2] + n - c], P, o + c, n - c)
                            add(tri_r[:], lg[:, hp, P_OFF[kt]:P_OFF[kt] + n], P, o, n)
                        nm, m0 = (P - 16, 16) if kt == 0 else (P, 0)
                        mm = add(ident_r[:], negm_r[:, m0:m0 + nm], P, o, nm)
                mm.then_inc(b_cum, 1)

            def b_values(idx):
                h, u = idx // 4, idx % 4
                r = 64 * (h % 2)
                pe.wait_ge(b_prob, idx + 1)
                if u == 0 and h >= 1:
                    pe.wait_ge(b_out, h)
                vc = 512 + 64 * h
                for kind, kt, o, n in GROUPS[u]:
                    rows = K_ROWS[kt]
                    if kind == "s":
                        v = v_cache[:, kt, vc:vc + 64] if kt < 4 else vs4[0:80, vc:vc + 64]
                        dst, start = ps[r:r + 64, 7, 0:64], kt == 0
                    else:
                        v = v_nat[0:rows, kt, vc:vc + 64]
                        dst, start = ps[r:r + 64, 6, Q_FROM[kt]:512], kt == 4
                    mm = nc.tensor.matmul(dst, v, prob[0:rows, idx % 3, o:o + n], start=start, stop=True,
                                          skip_group_check=True)
                mm.then_inc(b_av, 1)

            pe.wait_ge(b_consts, 1)
            for s in range(4 * BH + B_LAG + 2):
                if s < 4 * BH:
                    if s >= 6:
                        pe.wait_ge(b_prob, s - 5)
                    for k, (kind, kt, o, n) in enumerate(GROUPS[s % 4]):
                        mm = qk(s // 4, kind, kt, ps[0:K_ROWS[kt], s % 6, o:o + n], k == 0)
                    mm.then_inc(b_z, 1)
                if 0 <= s - B_LAG < 4 * BH:
                    b_sums(s - B_LAG)
                if s > B_LAG + 1:
                    b_values(s - B_LAG - 2)

            pe.wait_ge(b_out, BH)
            pe.wait_ge(ks_ready, 1)

            def a_scores(idx):
                h, i = idx // 5, idx % 5
                for m in range(2):
                    if idx >= 1:
                        pe.wait_ge(a_prob, 2 * idx - 1 + m)
                    r = slice(64 * m, 64 * m + 64)
                    if i < 4:
                        q = qkv[r, h, N_META + P * i:N_META + P * (i + 1)]
                        w, keys, rows = 144 + P * i, qkv[r, 4 + h, :], P
                    else:
                        q, w, keys, rows = qkv[r, h, KP:T], T, k_cache[r, h, :], 64
                    for b0 in range(0, w, 512):
                        n = min(512, w - b0)
                        mm = nc.tensor.matmul(ps[0:rows, 2 * m + b0 // 512, 0:n], q, keys[:, b0:b0 + n],
                                              start=True, stop=True)
                    mm.then_inc(a_s, 1)

            def a_transpose(idx):
                i = idx % 5
                rows, full, part = A_SHAPE[i]
                pe.wait_ge(a_w, idx + 1)
                if idx >= 1:
                    pe.wait_ge(a_wt, idx)
                for kt in range(full):
                    nc.tensor.transpose(ps[:, 4, kt * rows:(kt + 1) * rows], w_a[0:rows, idx % 2, kt * P:(kt + 1) * P],
                                        ident[0:rows, 0:rows])
                nc.tensor.transpose(ps[0:part, 5, 0:rows], w_a[0:rows, idx % 2, full * P:full * P + part],
                                    ident[0:rows, 0:rows]).then_inc(a_t, 1)

            def a_values(idx):
                h, i = idx // 5, idx % 5
                rows, full, part = A_SHAPE[i]
                pe.wait_ge(a_wt, idx + 1)
                if idx >= 2:
                    pe.wait_ge(a_out, idx - 1)
                for kt in range(full + 1):
                    r = P if kt < full else part
                    if i < 4:
                        v = v_nat[0:r, kt, h * P:(h + 1) * P]
                    else:
                        v = v_cache[:, kt, h * P:(h + 1) * P] if kt < 4 else vs4[0:80, h * P:(h + 1) * P]
                    wt = wt_a[0:r, idx % 2, kt, 0:rows]
                    mm = nc.tensor.matmul(ps[:, 6 + idx % 2, 0:rows], v, wt, start=(kt == 0), stop=(kt == full))
                mm.then_inc(a_o, 1)

            a_scores(0)
            for idx in range(NA + 1):
                if idx + 1 < NA:
                    a_scores(idx + 1)
                if idx >= 1:
                    a_values(idx - 1)
                if idx < NA:
                    a_transpose(idx)

            for c in range(KC):
                norm_sum("nm", c, HQ, sel[:, NH_ROWS * c:NH_ROWS * (c + 1)], NH_ROWS)
            pe.wait_ge(spread_in, 16)
            pe.wait_ge(norm_sems["nm"]["rs"], 1)
            def nm_factors(c):
                if c >= 3:
                    pe.wait_ge(norm_sems["nm"]["x"], c - 2)
                for h in range(2):
                    mm = nc.tensor.matmul(ps[:, NM_BANK[c % 3] + h, 0:HQ], spr[0:NH_ROWS, c, :],
                                          nrs[0:NH_ROWS, h * HQ:(h + 1) * HQ], start=True, stop=True)
                mm.then_inc(nm_factored, 1)

            def merged_chunk(kc):
                if kc < KC - 3:
                    nm_factors(kc + 3)
                pe.wait_ge(norm_sems["nm"]["lo"], kc + 1)

            for c in range(3):
                nm_factors(c)
            for u in range(N_WO):
                tile(B_WO + u, u % 2, u, free_wo, m0_hi, m0_lo, 0, HQ, chunk=merged_chunk if u == 0 else None)
                if u >= 2:
                    norm_sum("n2", u - 2, HQ)

            for c in range(KC - 2, KC):
                norm_sum("n2", c, HQ)
            with pe.Fori(0, N_PQ // 4) as it:
                for u in range(4):
                    tile(it * 4 + (B_PQ + u), u % 2, it * 4 + u, free_pq, m0_hi, m0_lo, 0, HQ,
                         chunk=split_of("n2"))
            pe.wait_ge(free_pq, 4 + 2 * N_PQ)
            pe.wait_ge(subk_in, 16)
            for i in range(RT_TILES * 4):
                t, b = i // 4, i % 4
                if i >= 4:
                    pe.wait_ge(sc_taken, i - 3)
                for j in range(4):
                    hp = 4 * b + j
                    mm = nc.tensor.matmul(ps[0:RT_TOK, 4 + i % 4, j * P:(j + 1) * P],
                                          q_t[:, hp, t * RT_TOK:(t + 1) * RT_TOK], subk[:, hp % 2, :],
                                          start=True, stop=True)
                mm.then_inc(sc_done, 1)

            with pe.Fori(0, RT_TILES) as it:
                for u in range(U1_PER):
                    n = it * U1_PER + u
                    tile(n + B_U, u % 2, n, free_u, m0_hi, m0_lo, 0, HQ)
            for u in range(MID_TILES):
                n = U1_TILES + u
                tile(n + B_U, u % 2, n, free_u, m0_hi, m0_lo, 0, HQ)
            pe.wait_ge(g_split, 2)
            for t in range(RT_TILES):
                if t >= 2:
                    pe.wait_ge(rt_taken, t - 1)
                for k, src in enumerate((routed[0:RT_TOK, t, 0, :], routed[0:RT_TOK, t, 1, :],
                                         g_hi[0:RT_TOK, t, :].bitcast(F32), g_lo[0:RT_TOK, t, :].bitcast(F32))):
                    mm = nc.tensor.transpose(ps[:, 4 + t % 2, k * RT_TOK:(k + 1) * RT_TOK], src,
                                             ident[0:RT_TOK, 0:RT_TOK])
                mm.then_inc(rt_done, 1)
            pe.sem_inc(hot_used, HR)
            with pe.Fori(0, U2_ITERS) as it:

                def scatter(q):
                    k = it * Q_PER + q
                    pe.wait_ge(hot_ready, k + 19)
                    pe.wait_ge(hot_j_ready, k + 19)
                    pe.wait_ge(gm_taken, k + 1)
                    for t in range(4):
                        dst = ps[:, 4 + q % GR, t * P:(t + 1) * P]
                        nc.tensor.matmul(dst, hot_i[:, q % HR, t, :], hot_j[:, q % HR, 0, t, :],
                                         start=True, stop=False)
                        mm = nc.tensor.matmul(dst, hot_i[:, q % HR, t, :], hot_j[:, q % HR, 1, t, :],
                                              start=False, stop=True)
                    mm.then_inc(hot_used, 1)

                for u in range(U2_PER):
                    n = it * U2_PER + (B_U2 + u)
                    tile(n + B_U, u % 2, n, free_u, m0_hi, m0_lo, 0, HQ,
                         lambda m: [scatter(q) for q in groups_at(u, m)])
            with pe.Fori(0, U3_TILES // 2) as it:
                for u in range(2):
                    n = it * 2 + (B_U3 + u)
                    tile(n + B_U, u, n, free_u, m0_hi, m0_lo, 0, HQ)
            pe.wait_ge(free_u, 4 + 2 * N_EXP_J)
            def v_group(g, gg, last):
                hi, lo = ((m1_hi, m1_lo), (m0_hi, m0_lo))[gg]
                pe.wait_ge(v_lo, g * 8 + 24)
                for c in range(KC):
                    tile(g * KC + (B_V + c), c % 2, g * KC + c, free_v, hi, lo, 0, HQ)
                    if last and c >= 2:
                        norm_sum("nf", c - 2, HQ)

            with pe.Fori(0, N_GROUP // 2 - 1) as it:
                for gg in range(2):
                    v_group(it * 2 + gg, gg, False)
            v_group(N_GROUP - 2, 0, False)
            v_group(N_GROUP - 1, 1, True)
            for c in range(KC - 2, KC):
                norm_sum("nf", c, HQ)

        @block.scalar
        def _(act):
            def hi_part(n, slot, k):
                act.wait_ge(raw_in[slot], k * 16)
                act.wait_ge(half_done, n * 2 + 2)
                nc.scalar.copy(w_hi[:, slot], raw[:, slot]).then_inc(hi_ready, 1)

            def squares(name, c, src, w):
                if c >= 2:
                    act.wait_ge(norm_sems[name]["sum"], c - 1)
                nc.scalar.square(nsq[:, c % 2, 0:w], src).then_inc(norm_sems[name]["sq"], 1)

            def deviations(name, halves, scale, rows=P):
                act.wait_ge(norm_sems[name]["sum"], KC)
                for h in range(2):
                    nc.scalar.activation(nrs[0:rows, h * halves:(h + 1) * halves], ps[0:rows, 4 + h, 0:halves],
                                         ACT.Sqrt, bias=eps[0:rows], scale=scale).then_inc(norm_sems[name]["std"], 1)

            def highs(name, w):
                for c in range(KC):
                    act.wait_ge(norm_sems[name]["x"], c + 1)
                    nc.scalar.copy(m0_hi[:, c, 0:w], ntmp[:, c % 2, 0:w]).then_inc(norm_sems[name]["hi"], 1)

            act.wait_ge(consts_in, 32)
            for c in range(KC):
                act.wait_ge(x_in[c], 16)
                squares("n1", c, xh[:, c, :], T)
            hi_part(0, 0, 1)
            deviations("n1", HT, 1.0 / D)
            highs("n1", T)
            with act.Fori(0, N_QKV // 4) as it:
                for u in range(4):
                    hi_part(it * 4 + (u + 1), (u + 1) % 2, it * 2 + ((u + 1) // 2 + 1))
                    for h in range(2):
                        act.wait_ge(half_done, it * 8 + (2 * u + h + 5))
                        nc.scalar.copy(qkv[:, bass.ds(it * 4 + u, 1), h * HT:(h + 1) * HT],
                                       ps[:, 2 * (u % 2) + h:2 * (u % 2) + h + 1, 0:HT]).then_inc(free_qkv, 1)
            act.wait_ge(free_qkv, 4 + 2 * N_QKV)
            nc.scalar.mul(qkv[:, 12:16, :], qkv[:, 12:16, :], SCALE).then_inc(q_scaled, 1)
            for k, c0 in ((1, 8), (2, 16), (3, 20)):
                act.dma_start(kv_out[k], qkv[:, c0:c0 + 4, :]).then_inc(kv_stored, 16)
            for i in range(12):
                kt, s = i // 2, i % 2
                act.wait_ge(vt_done, i + 1)
                rows = 128 if kt < 4 else 80
                dst = v_nat[0:rows, kt, 512 * s:512 * s + 512] if kt < 5 else vs4[0:80, 512 * s:512 * s + 512]
                nc.scalar.copy(dst, ps[0:rows, i % 4, :]).then_inc(vt_taken, 1)
            nc.scalar.preload_act_table_set("natural_log_exp_and_others")
            act.wait_ge(lam_step, 2)
            nc.scalar.activation(lam[:, 2:4], lam[:, 0:2], ACT.Exp).then_inc(lam_exp, 1)

            act.wait_ge(kv_stored, 48)
            nc.scalar.copy(ones_r[:], ones)
            nc.scalar.copy(tri_r[:], tri)
            nc.scalar.copy(ident_r[:], ident)
            nc.scalar.copy(negm_r[:], negm).then_inc(b_consts, 1)
            for s in range(4 * BH + B_LAG + 3):
                done = s - B_LAG - 1
                if done >= 5 and done % 4 == 1:
                    h = done // 4 - 1
                    r, c = 64 * (h % 2), 20 + h // 2
                    act.wait_ge(b_av, 4 * h + 4)
                    nc.scalar.copy(qkv[r:r + 64, c, N_META:KP], ps[r:r + 64, 6, :])
                    nc.scalar.copy(qkv[r:r + 64, c, KP:T], ps[r:r + 64, 7, 0:64]).then_inc(b_out, 1)
                if 0 <= done < 4 * BH:
                    act.wait_ge(b_cum, done + 1)
                    if done >= 3:
                        act.wait_ge(b_av, done - 2)
                    for rows, o, n in UNITS[done % 4][1]:
                        e = nc.scalar.activation(prob[0:rows, done % 3, o:o + n], ps[0:rows, done % 6, o:o + n],
                                                 ACT.Exp)
                    e.then_inc(b_prob, 1)
                if s < 4 * BH:
                    act.wait_ge(b_abs, s + 1)
                    for rows, o, n in UNITS[s % 4][1]:
                        t = t_abs[0:rows, s % 3, o:o + n]
                        e = nc.scalar.activation(t, t, ACT.Exp)
                    e.then_inc(b_exp, 1)
                    act.wait_ge(b_exp, s + 1)
                    for rows, o, n in UNITS[s % 4][1]:
                        t = t_abs[0:rows, s % 3, o:o + n]
                        e = nc.scalar.activation(t, t, ACT.Ln, bias=1.0)
                    e.then_inc(b_ln, 1)
                if 1 <= s <= 4 * BH:
                    h, u = (s - 1) // 4, (s - 1) % 4
                    act.wait_ge(b_log, s)
                    if h >= 2:
                        act.wait_ge(b_cum, 4 * (h - 1))
                    for rows, o, n in UNITS[u][1]:
                        off = UNITS[u][0] + o
                        e = nc.scalar.copy(log_hi[0:rows, h % 2, off:off + n], t_abs[0:rows, (s - 1) % 3, o:o + n])
                    e.then_inc(b_hi, 1)

            for s in range(NA + 2):
                if s < NA:
                    i = s % 5
                    rows, w = (P, 144 + P * i) if i < 4 else (64, T)
                    for m in range(2):
                        act.wait_ge(a_neg, 2 * s + m + 1)
                        if s >= 2:
                            act.wait_ge(a_w, s - 1)
                        nc.scalar.activation(p_a[0:rows, 2 * (s % 2) + m, 0:w], psf[0:rows, 1024 * m:1024 * m + w],
                                             ACT.Exp, bias=stat[0:rows, 2 + m:3 + m], scale=SCALE,
                                             accum_out=stat[0:rows, 4 + m:5 + m]).then_inc(a_prob, 1)
                if s >= 2:
                    h, i = (s - 2) // 5, (s - 2) % 5
                    rows = A_SHAPE[i][0]
                    q0 = N_META + P * i if i < 4 else KP
                    act.wait_ge(a_o, s - 1)
                    nc.scalar.copy(qkv[:, 8 + h, q0:q0 + rows], ps[:, 6 + s % 2, 0:rows]).then_inc(a_out, 1)
                if 1 <= s <= NA:
                    rows, full, part = A_SHAPE[(s - 1) % 5]
                    act.wait_ge(a_t, s)
                    if s >= 3:
                        act.wait_ge(a_o, s - 2)
                    nc.scalar.copy(wt_a[:, (s - 1) % 2, 0:full, 0:rows],
                                   ps[:, 4, 0:full * rows].rearrange("p (k q) -> p k q", q=rows))
                    nc.scalar.copy(wt_a[0:part, (s - 1) % 2, full, 0:rows], ps[0:part, 5, 0:rows]).then_inc(a_wt, 1)

            act.wait_ge(a_out, 5 * AH)
            for c in range(KC):
                squares("nm", c, merged(c), TQ)
            deviations("nm", HQ, 1.0, NH_ROWS)
            highs("nm", TQ)

            def residual_squares(name, c):
                squares(name, c, xh[:, c, N_META:T], TQ)

            for u in range(N_WO):
                hi_part(B_WO + u + 1, (u + 1) % 2, (B_WO + u + 1) // 2 + 1)
                if u >= 1:
                    act.wait_ge(free_wo, 4 + 2 * u)
                    residual_squares("n2", u - 1)
            act.wait_ge(free_wo, 4 + 2 * N_WO)
            residual_squares("n2", KC - 1)
            deviations("n2", HQ, 1.0 / D)
            highs("n2", TQ)
            act.wait_ge(ak_stored, 16)
            with act.Fori(0, N_PQ // 4) as it:
                for u in range(4):
                    n0 = B_PQ + u
                    hi_part(it * 4 + (n0 + 1), (u + 1) % 2, it * 2 + ((n0 + 1) // 2 + 1))
                    for h in range(2):
                        act.wait_ge(half_done, it * 8 + (2 * n0 + h + 5))
                        nc.scalar.copy(q_t[:, bass.ds(it * 4 + u, 1), h * HQ:(h + 1) * HQ],
                                       ps[:, 2 * (u % 2) + h:2 * (u % 2) + h + 1, 0:HQ]).then_inc(free_pq, 1)
            for i in range(RT_TILES * 4):
                t, b = i // 4, i % 4
                act.wait_ge(sc_done, i + 1)
                nc.scalar.copy(score[0:RT_TOK, t, 4 * b:4 * b + 4, :],
                               ps[0:RT_TOK, 4 + i % 4, :].rearrange("p (j n) -> p j n", j=4)).then_inc(sc_taken, 1)
            act.wait_ge(sc_taken, RT_TILES * 4)

            def v_high(g8, j, buf):
                act.wait_ge(v_prod, g8 + (j + 1))
                nc.scalar.copy((m1_hi, m0_hi)[buf][:, j, 0:TQ], gated[:, j % 2, :]).then_inc(v_hi, 1)

            def u_step(n, n0, u, it, per, between=None):
                hi_part(n + (B_U + 1), (u + 1) % 2, it * (per // 2) + ((B_U + n0 + 1) // 2 + 1))
                act.wait_ge(act_stored[u % 2], it * (8 * per) + (16 * (n0 // 2) + 16))
                for h in range(2):
                    if between is not None:
                        between(h)
                    act.wait_ge(half_done, n * 2 + (2 * B_U + h + 5))
                    nc.scalar.activation(act_st[:, u % 2, h * HQ:(h + 1) * HQ], ps[:, 2 * (u % 2) + h, 0:HQ],
                                         ACT.Gelu).then_inc(free_u, 1)

            with act.Fori(0, RT_TILES) as it:
                act.wait_ge(top_read, it + 1)
                nc.scalar.copy(cur[0:RT_TOK].unsqueeze(1),
                               score[0:RT_TOK, bass.ds(it, 1), :, :]).then_inc(cur_ready, 1)
                for u in range(U1_PER):
                    u_step(it * U1_PER + u, u, u, it, U1_PER)

            def gates_exp(h):
                if h == 0:
                    act.wait_ge(g_step, 1)
                    nc.scalar.activation(gexp[0:RT_TOK], gexp[0:RT_TOK], ACT.Exp).then_inc(g_exped, 1)

            for u in range(MID_TILES):
                u_step(U1_TILES + u, U1_TILES + u, u, 0, 0, gates_exp if u == 0 else None)
            for t in range(RT_TILES):
                act.wait_ge(rt_done, t + 1)
                nc.scalar.copy(rt_t[:, :, t * RT_TOK:(t + 1) * RT_TOK],
                               ps[:, 4 + t % 2, 0:4 * RT_TOK].rearrange("p (k t) -> p k t", k=4)).then_inc(rt_taken, 1)
            act.wait_ge(rt_taken, RT_TILES)
            act.sem_inc(gm_taken, GR)

            def rows_of(b, slot):
                act.wait_ge(hot_ready, b * 9 + 9)
                act.wait_ge(hot_j_ready, b * 9 + 9)
                nc.scalar.copy(rt_b[:, slot], rt_t[:, :, bass.ds(b * G_TOK, G_TOK)]).then_inc(rtb_ready, 1)

            def u2_iteration(it, last):

                def take_gates(q):
                    nb, qq = q // 9, q % 9
                    if qq == 1 and not (last and nb == BATCH_PER - 1):
                        rows_of(it * BATCH_PER + (nb + 1), (nb + 1) % 2)
                    act.wait_ge(hot_used, it * Q_PER + (q + 1 + HR))
                    if qq == 0:
                        act.wait_ge(g_stored[nb % 2], it * (8 * BATCH_PER) + (16 * (nb // 2) + 16))
                    nc.scalar.copy(g_st[:, nb % 2, :, 4 * qq:4 * qq + 4],
                                   ps[:, 4 + q % GR, :].rearrange("p (t j) -> p j t", t=4)).then_inc(gm_taken, 1)

                for u in range(U2_PER):
                    u_step(it * U2_PER + (B_U2 + u), B_U2 + u, u, it, U2_PER,
                           lambda h: [take_gates(q) for q in before_half(u, h)])
                for q in groups_at(U2_PER - 1, 47):
                    take_gates(q)

            rows_of(0, 0)
            with act.Fori(0, U2_ITERS - 1) as it:
                u2_iteration(it, False)
            u2_iteration(U2_ITERS - 1, True)
            for u in range(U3_TILES):
                n = B_U3 + u
                u_step(n, n, u, 0, 0, (lambda h: v_high(0, u - 6, 0) if h == 0 else None) if u >= 6 else None)

            def v_steps(g, gg, last):
                for c in range(KC):
                    n0 = B_V + gg * KC + c
                    if not (last and c == KC - 1):
                        hi_part(g * KC + (B_V + c + 1), (c + 1) % 2, g * 4 + ((B_V + c + 1) // 2 + 1))
                    if not last:
                        v_high(g * 8 + 8, c, (gg + 1) % 2)
                    elif c >= 1:
                        act.wait_ge(free_v, 4 + 2 * ((N_GROUP - 1) * KC + c))
                        residual_squares("nf", c - 1)

            with act.Fori(0, N_GROUP // 2 - 1) as it:
                for gg in range(2):
                    v_steps(it * 2 + gg, gg, False)
            v_steps(N_GROUP - 2, 0, False)
            v_steps(N_GROUP - 1, 1, True)
            act.wait_ge(free_v, 4 + 2 * N_GROUP * KC)
            residual_squares("nf", KC - 1)
            deviations("nf", HQ, 1.0 / D)

        @block.vector
        def _(dve):
            TT, TS = nc.vector.tensor_tensor, nc.vector.tensor_scalar

            def lo_part(n, slot):
                dve.wait_ge(hi_ready, n + 1)
                TT(w_lo[:, slot], raw[:, slot], w_hi[:, slot].bitcast(F32), SUB).then_inc(w_split, 1)

            def factors(name, w, rows=P):
                dve.wait_ge(norm_sems[name]["std"], 2)
                nc.vector.reciprocal(nrs[0:rows, 0:w], nrs[0:rows, 0:w]).then_inc(norm_sems[name]["rs"], 1)
                dve.wait_ge(norm_sems[name]["rs"], 1)

            def normed(name, src, gain, w, factor=None):
                s = norm_sems[name]

                def low(c):
                    dve.wait_ge(s["hi"], c + 1)
                    TT(m0_lo[:, c, 0:w], ntmp[:, c % 2, 0:w], m0_hi[:, c, 0:w].bitcast(F32), SUB).then_inc(s["lo"], 1)

                for c in range(KC):
                    if c >= 2:
                        dve.wait_ge(s["lo"], c - 1)
                    f = nrs[:, 0:w] if factor is None else factor(c)
                    nc.vector.scalar_tensor_tensor(ntmp[:, c % 2, 0:w], src(c), gain(c), f, MULT, MULT).then_inc(s["x"], 1)
                    if c >= 1:
                        low(c - 1)
                low(KC - 1)

            dve.wait_ge(consts_in, 32)
            for c in range(KC):
                dve.wait_ge(x_in[c], 16)
            lo_part(0, 0)
            factors("n1", T)
            normed("n1", lambda c: xh[:, c, :], lambda c: gn[:, G_ATTN + c:G_ATTN + c + 1], T)
            with dve.Fori(0, N_QKV // 4) as it:
                for u in range(4):
                    lo_part(it * 4 + (u + 1), (u + 1) % 2)

            dve.wait_ge(free_qkv, 4 + 2 * N_QKV)
            dve.wait_ge(tables_in, 16)
            for c in range(9):
                if c < 8:
                    b = 4 + 2 * (c % 2)
                    dve.wait_ge(rot_done, c + 1)
                    if c >= 2:
                        dve.wait_ge(rope_done, c - 1)
                    TT(rtmp[:, c % 2, :], psf[:, 512 * b:512 * b + T], tab[:, 1, :], MULT).then_inc(rope_step, 1)
                if c >= 1:
                    dve.wait_ge(rope_step, c)
                    dve.wait_ge(cos_done, c)
                    TT(qkv[:, c - 1, :], qkv[:, c - 1, :], rtmp[:, (c - 1) % 2, :], ADD).then_inc(rope_done, 1)
            dve.wait_ge(caches_in, 64)
            lp = lam_in[:].rearrange("p (a b d) -> p a b d", a=2, b=2)
            TT(lp[:, :, 0, :], lp[:, :, 0, :], lp[:, :, 1, :], MULT).then_inc(lam_step, 1)
            dve.wait_ge(lam_step, 1)
            nc.vector.tensor_reduce(lam[:, 0:2], lp[:, :, 0, :], AX_X, ADD).then_inc(lam_step, 1)
            dve.wait_ge(lam_exp, 1)
            TT(lam[:, 4:5], lam[:, 3:4], lam[:, 2:3], SUB).then_inc(lam_step, 1)
            dve.wait_ge(lam_step, 3)
            TS(lam[:, 5:6], lam[:, 4:5], -LAM_INIT, None, ADD).then_inc(lam_step, 1)
            TS(gn[:, G_A:G_A + 1], gn[:, G_A:G_A + 1], 1.0 - LAM_INIT, None, MULT).then_inc(lam_step, 1)
            dve.wait_ge(lam_step, 5)

            def b_first(idx):
                u = idx % 4
                dve.wait_ge(b_z, idx + 1)
                if idx >= 2:
                    dve.wait_ge(b_raw, idx - 1)
                for rows, o, n in UNITS[u][1]:
                    last = TS(t_pos[0:rows, idx % 2, o:o + n], ps[0:rows, idx % 6, o:o + n], 0.0, None, ALU.max)
                last.then_inc(b_pos, 1)
                dve.wait_ge(b_pos, idx + 1)
                if idx >= 3:
                    dve.wait_ge(b_lo, idx - 2)
                for rows, o, n in UNITS[u][1]:
                    last = nc.vector.scalar_tensor_tensor(t_abs[0:rows, idx % 3, o:o + n],
                                                          t_pos[0:rows, idx % 2, o:o + n], -2.0,
                                                          ps[0:rows, idx % 6, o:o + n], MULT, ADD)
                last.then_inc(b_abs, 1)

            def b_second(idx):
                u = idx % 4
                dve.wait_ge(b_ln, idx + 1)
                for rows, o, n in UNITS[u][1]:
                    t = t_abs[0:rows, idx % 3, o:o + n]
                    last = nc.vector.scalar_tensor_tensor(t, t, -1.0, t_pos[0:rows, idx % 2, o:o + n], MULT, SUB)
                last.then_inc(b_raw, 1)
                dve.wait_ge(b_raw, idx + 1)
                masks = {0: [(80, 256, 80, 0)], 1: [(128, 0, 128, 0), (128, 272, 128, 0)],
                         2: [(128, 0, 128, 0)], 3: [(128, 0, 112, 16)]}[u]
                for rows, o, n, m0 in masks:
                    t = t_abs[0:rows, idx % 3, o:o + n]
                    last = TT(t, t, mask[0:rows, m0:m0 + n], MULT)
                last.then_inc(b_log, 1)

            def b_third(idx):
                h, u = idx // 4, idx % 4
                dve.wait_ge(b_hi, idx + 1)
                for rows, o, n in UNITS[u][1]:
                    part = slice(UNITS[u][0] + o, UNITS[u][0] + o + n)
                    last = TT(log_lo[0:rows, h % 2, part], t_abs[0:rows, idx % 3, o:o + n],
                              log_hi[0:rows, h % 2, part].bitcast(F32), SUB)
                last.then_inc(b_lo, 1)

            b_first(0)
            for idx in range(4 * BH):
                if idx + 1 < 4 * BH:
                    b_first(idx + 1)
                if idx >= 1:
                    b_third(idx - 1)
                b_second(idx)
            b_third(4 * BH - 1)

            k_step = 0
            dve.wait_ge(b_out, BH)

            def a_step_done(ins):
                nonlocal k_step
                ins.then_inc(a_step, 1)
                k_step += 1
                dve.wait_ge(a_step, k_step)

            def a_greatest(idx):
                i = idx % 5
                rows, w = (P, 144 + P * i) if i < 4 else (64, T)
                for m in range(2):
                    dve.wait_ge(a_s, 2 * idx + m + 1)
                    if i < 4:
                        e0 = 1024 * m + w
                        if w > 512 and w - CHUNK < 512:
                            nc.vector.memset(psf[0:CHUNK, e0 - CHUNK:1024 * m + 512], NEG)
                            a_step_done(nc.vector.memset(psf[0:CHUNK, 1024 * m + 512:e0], NEG))
                        else:
                            a_step_done(nc.vector.memset(psf[0:CHUNK, e0 - CHUNK:e0], NEG))
                    nc.vector.tensor_reduce(stat[0:rows, m:m + 1], psf[0:rows, 1024 * m:1024 * m + w], AX_X,
                                            ALU.max).then_inc(a_max, 1)
                    dve.wait_ge(a_max, 2 * idx + m + 1)
                    TS(stat[0:rows, 2 + m:3 + m], stat[0:rows, m:m + 1], -SCALE, None, MULT).then_inc(a_neg, 1)

            a_greatest(0)
            for idx in range(NA):
                i = idx % 5
                rows, w = (P, 144 + P * i) if i < 4 else (64, T)
                p0 = 2 * (idx % 2)
                dve.wait_ge(a_prob, 2 * idx + 2)
                a_step_done(nc.vector.reciprocal(stat[0:rows, 6:8], stat[0:rows, 4:6]))
                TT(stat[0:rows, 8:9], stat[0:rows, 7:8], lam[0:rows, 5:6], MULT).then_inc(a_step, 1)
                k_step += 1
                if idx >= 2:
                    dve.wait_ge(a_t, idx - 1)
                a_step_done(TS(w_a[0:rows, idx % 2, 0:w], p_a[0:rows, p0, 0:w], stat[0:rows, 6:7], None, MULT))
                nc.vector.scalar_tensor_tensor(w_a[0:rows, idx % 2, 0:w], p_a[0:rows, p0 + 1, 0:w], stat[0:rows, 8:9],
                                               w_a[0:rows, idx % 2, 0:w], MULT, ADD).then_inc(a_w, 1)
                if idx + 1 < NA:
                    a_greatest(idx + 1)

            dve.wait_ge(a_t, 5 * AH)
            dve.wait_ge(a_o, 5 * AH)
            factors("nm", TQ, NH_ROWS)

            def head_factors(c):
                dve.wait_ge(nm_factored, c + 1)
                return ps[:, NM_BANK[c % 3]:NM_BANK[c % 3] + 2, 0:HQ]

            normed("nm", lambda c: merged(c), lambda c: gn[:, G_A:G_A + 1] if c < 4 else gn[:, G_B:G_B + 1], TQ,
                   head_factors)
            for u in range(N_WO):
                lo_part(B_WO + u + 1, (u + 1) % 2)
                for h in range(2):
                    dve.wait_ge(half_done, 2 * (B_WO + u) + h + 5)
                    dst = xh[:, u, N_META + h * HQ:N_META + (h + 1) * HQ]
                    TT(dst, ps[:, 2 * (u % 2) + h, 0:HQ], dst, ADD).then_inc(free_wo, 1)
            factors("n2", TQ)
            normed("n2", lambda c: xh[:, c, N_META:T], lambda c: gn[:, G_FFN + c:G_FFN + c + 1], TQ)
            with dve.Fori(0, N_PQ // 4) as it:
                for u in range(4):
                    lo_part(it * 4 + (B_PQ + u + 1), (u + 1) % 2)

            R = RT_TOK
            dve.sem_inc(top_read, 1)
            dve.wait_ge(sc_taken, RT_TILES * 4)
            n_links = [0]

            def route(it):
                k = 0

                def link(ins):
                    nonlocal k
                    k += 1
                    ins.then_inc(r_step, 1)
                    dve.wait_ge(r_step, it * R_LINKS + k)
                    dve.sem_inc(route_held, 1)

                dve.wait_ge(cur_ready, it + 1)
                dve.sem_inc(route_held, 1)
                for first in range(0, 16, 8):
                    for hp in range(first, first + 8):
                        last = nc.vector.max(s16[0:R, hp, 0:8], cur[0:R, hp, :])
                    yield
                link(last)
                for hp in range(16):
                    nc.vector.max_index(i16[0:R, hp, 0:8], s16[0:R, hp, 0:8], cur[0:R, hp, :])
                    last = nc.vector.match_replace(cur2[0:R, hp, :], s16[0:R, hp, 0:8], cur[0:R, hp, :], LOWEST)
                    if hp % 4 == 3 and hp < 15:
                        yield
                last.then_inc(top_read, 1)
                dve.wait_ge(top_read, it + 2)
                dve.sem_inc(route_held, 1)
                yield
                for hp in range(16):
                    last = nc.vector.max(s16[0:R, hp, 8:16], cur2[0:R, hp, :])
                    if hp == 7:
                        yield
                link(last)
                yield
                for hp in range(16):
                    nc.vector.max_index(i16[0:R, hp, 8:16], s16[0:R, hp, 8:16], cur2[0:R, hp, :])
                    if hp % 8 == 7:
                        yield
                s4 = s16[0:R].rearrange("p (h s) a -> p h s a", s=2)
                link(TT(cand[0:R], s4[:, :, 0, :].unsqueeze(3).broadcast_to((R, HEADS, TOPK, TOPK)),
                        s4[:, :, 1, :].unsqueeze(2).broadcast_to((R, HEADS, TOPK, TOPK)), ADD))
                link(nc.vector.tensor_copy(i16f[0:R], i16[0:R]))
                cf = cand[0:R].rearrange("p h a b -> p h (a b)")
                cf2 = cand2[0:R].rearrange("p h a b -> p h (a b)")
                for h in range(HEADS):
                    last = nc.vector.max(c16[0:R, h, 0:8], cf[:, h, :])
                link(last)
                yield
                for h in range(HEADS):
                    nc.vector.max_index(j16[0:R, h, 0:8], c16[0:R, h, 0:8], cf[:, h, :])
                    last = nc.vector.match_replace(cf2[:, h, :], c16[0:R, h, 0:8], cf[:, h, :], LOWEST)
                    if h == 3:
                        yield
                link(last)
                yield
                for h in range(HEADS):
                    last = nc.vector.max(c16[0:R, h, 8:16], cf2[:, h, :])
                link(last)
                yield
                for h in range(HEADS):
                    last = nc.vector.max_index(j16[0:R, h, 8:16], c16[0:R, h, 8:16], cf2[:, h, :])
                link(last)
                jj = j16[0:R].rearrange("p h k -> p (h k)")
                TS(jab[0:R, 0], jj, 4, None, ALU.logical_shift_right)
                link(TS(jab[0:R, 1], jj, TOPK - 1, None, ALU.bitwise_and))
                link(nc.vector.tensor_copy(jf[0:R], jab[0:R]))
                yield
                i4 = i16f[0:R].rearrange("p (h s) a -> p h s a", s=2)
                for s in range(2):
                    link(TT(eqs[0:R], jf[0:R, s].unsqueeze(2).broadcast_to((R, PAIRS, TOPK)),
                            iota16[0:R].unsqueeze(1).broadcast_to((R, PAIRS, TOPK)), ALU.is_equal))
                    yield
                    e4 = eqs[0:R].rearrange("p (h k) a -> p h k a", h=HEADS)
                    link(TT(e4, e4, i4[:, :, s, :].unsqueeze(2).broadcast_to((R, HEADS, TOPK, TOPK)), MULT))
                    yield
                    link(nc.vector.tensor_reduce(routed[0:R, bass.ds(it, 1), s, :].rearrange("p o k -> p (o k)"),
                                                 eqs[0:R], AX_X, ADD))
                    yield
                link(nc.vector.tensor_copy(routed[0:R, bass.ds(it, 1), 2, :].rearrange("p o k -> p (o k)"),
                                           c16[0:R].rearrange("p h k -> p (h k)")))
                n_links[0] = k
                yield "ended"

            with dve.Fori(0, RT_TILES) as it:
                steps = route(it)
                for u in range(U1_PER):
                    lo_part(it * U1_PER + (B_U + u + 1), (u + 1) % 2)
                    for _ in range(R_STEPS * u // U1_PER, R_STEPS * (u + 1) // U1_PER):
                        got = next(steps, "too many")
                assert got == "ended", got
                assert not list(steps)
                assert n_links[0] == R_LINKS, n_links

            G6 = (R, RT_TILES, HEADS, TOPK)
            sc = routed[0:R, :, 2, :].rearrange("p t (h k) -> p t h k", h=HEADS)
            ge = gexp[0:R].rearrange("p t (h k) -> p t h k", h=HEADS)
            gs = gsum[0:R, 0].rearrange("p (t h) -> p t h", h=HEADS)
            gr = gsum[0:R, 1].rearrange("p (t h) -> p t h", h=HEADS)

            def glink(ins, n):
                ins.then_inc(g_step, 1)
                dve.wait_ge(g_step, n)

            lo_part(B_U + U1_TILES + 1, 1)
            for t in range(RT_TILES):
                last = TT(ge[:, t], sc[:, t], sc[:, t, :, 0:1].broadcast_to((R, HEADS, TOPK)), SUB)
            glink(last, 1)
            dve.wait_ge(g_exped, 1)
            glink(nc.vector.tensor_reduce(gsum[0:R, 0], gexp[0:R].rearrange("p t (h k) -> p (t h) k", k=TOPK),
                                          AX_X, ADD), 2)
            glink(nc.vector.reciprocal(gsum[0:R, 1], gsum[0:R, 0]), 3)
            lo_part(B_U + U1_TILES + 2, 0)
            gk = gexp[0:R].rearrange("p t (h k) -> p (t h) k", k=TOPK)
            glink(TT(gk, gk, gsum[0:R, 1].unsqueeze(2).broadcast_to((R, RT_TILES * HEADS, TOPK)), MULT), 4)
            nc.vector.tensor_copy(g_hi[0:R], gexp[0:R]).then_inc(g_split, 1)
            dve.wait_ge(g_split, 1)
            TT(g_lo[0:R], gexp[0:R], g_hi[0:R].bitcast(F32), SUB).then_inc(g_split, 1)

            dve.sem_inc(hot_ready, 18)

            def one_hot(it, q):
                nb, qq = q // 9, q % 9
                if qq == 0:
                    dve.wait_ge(rtb_ready, it * BATCH_PER + (nb + 1))
                dve.wait_ge(hot_used, it * Q_PER + (q + 1))
                dve.wait_ge(hot_j_ready, it * Q_PER + (q + 16))

                def rows(k):
                    return rt_b[:, nb % 2, k, 4 * qq:4 * qq + 4].unsqueeze(2).broadcast_to((P, 4, P))

                TT(eq_j[:, q % 3], iota.unsqueeze(1).broadcast_to((P, 4, P)), rows(1), ALU.is_equal)
                TT(hot_i[:, q % HR], iota.unsqueeze(1).broadcast_to((P, 4, P)), rows(0),
                   ALU.is_equal).then_inc(hot_ready, 1)

            def u2_iteration(it, last):
                for u in range(U2_PER):
                    lo_part(it * U2_PER + (B_U + B_U2 + u + 1), (u + 1) % 2)
                    for q in groups_of(u):
                        if not (last and q + HOT_AHEAD >= Q_PER):
                            one_hot(it, q + HOT_AHEAD)

            for q in range(HOT_AHEAD):
                one_hot(0, q)
            with dve.Fori(0, U2_ITERS - 1) as it:
                u2_iteration(it, False)
            u2_iteration(U2_ITERS - 1, True)

            dve.sem_inc(v_lo, 16)

            def product(g8, gg, j, kg, ka):
                if j == 0:
                    dve.wait_ge(g_in_s[gg], kg)
                if j % 4 == 0:
                    dve.wait_ge(act_in_s[j // 4], ka)
                TT(gated[:, j % 2, :].rearrange("p (b t) -> p b t", b=G_BATCH),
                   act_in[:, j // 4, j % 4, :].rearrange("p (b t) -> p b t", b=G_BATCH),
                   g_in[:, gg, :, j, :], MULT).then_inc(v_prod, 1)
                dve.wait_ge(v_hi, g8 + (j + 1))
                TT((m1_lo, m0_lo)[gg][:, j, 0:TQ], gated[:, j % 2, :],
                   (m1_hi, m0_hi)[gg][:, j, 0:TQ].bitcast(F32), SUB).then_inc(v_lo, 1)

            for u in range(U3_TILES):
                lo_part(B_U + B_U3 + u + 1, (u + 1) % 2)
                if u == 6:
                    for s in g_stored:
                        dve.wait_ge(s, 16 * (G_BATCH // 2) + 16)
                if u >= 6:
                    product(0, 0, u - 6, 16, 16)

            def v_steps(g, gg, it, last):
                for c in range(KC):
                    if not (last and c == KC - 1):
                        lo_part(g * KC + (B_V + c + 1), (c + 1) % 2)
                    if not last:
                        nxt = (gg + 1) % 2
                        if c == 0:
                            dve.wait_ge(half_done, g * (2 * KC) + (2 * B_V + 4))
                        product(g * 8 + 8, nxt, c, it * 16 + (16 if nxt else 32), g * 16 + 32)
                    for h in range(2):
                        dve.wait_ge(half_done, g * (2 * KC) + (2 * (B_V + c) + h + 5))
                        dst = xh[:, c, N_META + h * HQ:N_META + (h + 1) * HQ]
                        TT(dst, ps[:, 2 * (c % 2) + h, 0:HQ], dst, ADD).then_inc(free_v, 1)

            with dve.Fori(0, N_GROUP // 2 - 1) as it:
                for gg in range(2):
                    v_steps(it * 2 + gg, gg, it, False)
            v_steps(N_GROUP - 2, 0, N_GROUP // 2 - 1, False)
            v_steps(N_GROUP - 1, 1, N_GROUP // 2 - 1, True)
            factors("nf", TQ)
            for c in range(KC):
                nc.vector.scalar_tensor_tensor(y_st[:, c], xh[:, c, N_META:T], gn[:, G_FINAL + c:G_FINAL + c + 1],
                                               nrs[:, 0:TQ], MULT, MULT).then_inc(norm_sems["nf"]["x"], 1)



R_LINKS = 17
R_STEPS = 22


def constants():
    k, m = np.arange(P)[:, None], np.arange(P)[None, :]
    c = np.zeros((P, C_W), np.float32)
    c[:, C_ID:C_ID + P] = k == m
    c[:, C_TRI:C_TRI + P] = k >= m
    c[:, C_ONE:C_ONE + P] = 1
    spread = np.zeros((NH_ROWS, KC, P), np.float32)
    for j in range(KC):
        for d in range(P):
            row = j if j < 4 else 4 + 2 * (j - 4) + d // HD
            c[d, C_SEL + NH_ROWS * j + row] = 1.0 / (P if j < 4 else HD)
            spread[row, j, d] = 1
    half = HD // 8
    d = np.arange(P)
    for j in range(P):
        if d[j] % HD < half:
            c[j + half, C_ROT + j] = -1
        elif d[j] % HD < 2 * half:
            c[j - half, C_ROT + j] = 1
    c[:, C_MASK:C_MASK + P] = k < m
    c[:, C_NEG:C_NEG + P] = np.where(k < m, 0, NEG)
    c[:, C_IOTA:C_IOTA + P] = m
    c[:, C_IOTA16:C_IOTA16 + TOPK] = np.arange(TOPK)
    c[:, C_EPS] = EPS
    inv = (np.float32(500000.0) ** (-np.arange(half, dtype=np.float32) * np.float32(2.0) / np.float32(2 * half)))
    ang = np.arange(T, dtype=np.float32)[None, :] * inv.astype(np.float32)[:, None]
    tab = np.zeros((P, 2, T), np.float32)
    tab[:, 0] = 1
    for j in range(P):
        if d[j] % HD < 2 * half:
            tab[j, 0] = np.cos(ang[d[j] % half])
            tab[j, 1] = np.sin(ang[d[j] % half])
    return c, tab, spread


def kernel(x_prompt, x_sample, cache_a_k, cache_a_v, cache_b_k, cache_b_v, meta_tokens, g_attn, w_qkv,
           diff_lambda, a_norm_g, b_norm_g, w_o, g_ffn, w_peer_q, peer_sub_keys, peer_u, peer_v, g_final):
    import concourse.bacc as bacc
    from concourse.bass_utils import run_bass_kernel_spmd

    consts, tab, spread = constants()
    x = np.concatenate([meta_tokens, x_prompt[0], x_sample[0]], axis=0)
    x_t = x.T.reshape(KC, P, T).transpose(1, 0, 2)
    col = lambda g: np.asarray(g).reshape(-1, P).T
    gains = np.concatenate([col(g_attn[0]), col(g_ffn[0]), col(g_final), col(a_norm_g[0]),
                            np.concatenate([b_norm_g[0], b_norm_g[0]]).reshape(P, 1)], axis=1)

    def k_t(c):
        return np.asarray(c).reshape(KP, 4, P).transpose(2, 1, 0)

    cache_k = np.concatenate([k_t(cache_a_k[0, 0]), k_t(cache_b_k[0, 0])], axis=1)
    va, vb = np.asarray(cache_a_v)[0, 0].reshape(KP, 512), np.asarray(cache_b_v)[0, 0].reshape(KP, 512)
    v = np.concatenate([va, vb], axis=1)
    cache_v = v[:512].reshape(4, P, 1024).transpose(1, 0, 2)
    cache_vt = v[512:].T.reshape(8, P, N_META).transpose(1, 0, 2)

    def w_t(w):
        w = np.asarray(w)
        return w.reshape(KC, P, w.shape[1] // P, P).transpose(2, 1, 0, 3).reshape(-1, KC * P)

    u_t = np.asarray(peer_u)[0].reshape(P, P, KC, P).transpose(1, 3, 2, 0).reshape(-1, KC * P)
    v_t = np.asarray(peer_v)[0].reshape(P, N_GROUP, 8, KC, P).transpose(1, 3, 0, 2, 4).reshape(-1, KC * P)
    w_tiles = np.concatenate([w_t(w_qkv[0]), w_t(w_o[0]), w_t(w_peer_q[0]), u_t, v_t], axis=0)
    sub_keys = np.asarray(peer_sub_keys)[0].transpose(2, 0, 1)

    nc = bacc.Bacc("TRN2", target_bir_lowering=False, num_devices=1)
    arrays, args = {}, []
    for name, a in (("x_t", x_t), ("consts", consts), ("tables", tab), ("spread", spread), ("gains", gains),
                    ("lam_p", np.asarray(diff_lambda)[0].reshape(256)), ("cache_k", cache_k), ("cache_v", cache_v),
                    ("cache_vt", cache_vt), ("w_tiles", w_tiles), ("sub_keys", sub_keys)):
        arrays[name] = np.ascontiguousarray(a)
        args.append(nc.dram_tensor(name, a.shape, F32, kind="ExternalInput").ap())
    args.append(nc.dram_tensor("y_t", (KC, P, TQ), F32, kind="ExternalOutput").ap())
    args.append(nc.dram_tensor("kv_t", (4, P, 4, T), F32, kind="ExternalOutput").ap())
    bass_hybrid_step(nc, *args)
    out = run_bass_kernel_spmd(nc, [arrays], core_ids=[0]).results[0]

    y = out["y_t"].reshape(D, TQ).T
    a_k, a_v, b_k, b_v = out["kv_t"].transpose(0, 3, 2, 1).reshape(4, T, 512)
    a_shape, b_shape = (1, 1, -1, AH, 2 * HD), (1, 1, -1, BH, HD)
    parts = [(a_k, a_shape), (a_v, a_shape), (b_k, b_shape), (b_v, b_shape)]
    return ((np.ascontiguousarray(y[None, :SEQ]), np.ascontiguousarray(y[None, SEQ:]))
            + tuple(np.ascontiguousarray(a[:KP].reshape(s)) for a, s in parts)
            + tuple(np.ascontiguousarray(a[KP:].reshape(s)) for a, s in parts))
```
